# Optimizing a Trainium2 kernel written in Bass

```python
import jax
import jax.numpy as jnp
from jax import lax
import numpy as np
import jax, jax.numpy as jnp

D_MODEL = 2048
BATCH = 1
SEQ = 256
DEPTH = 1

GRID_W = 64
CTX_LEN = 256
HEAD_DIM = 64
D_RWKV = D_MODEL // 2
N_RWKV_HEADS = D_RWKV // HEAD_DIM
D_CONV = D_MODEL // 4
D_FOURIER = D_MODEL // 4
N_FOURIER_GROUPS = D_FOURIER // HEAD_DIM
D_MIX = D_RWKV + D_CONV + D_FOURIER
DECAY_LORA = 96
ICLR_LORA = 96
GATE_LORA = 256
D_FF = ((8 * D_MODEL + 3 * 256 - 1) // (3 * 256)) * 256
N_MOD = 6
RMS_EPS = 1e-6
GN_EPS = 64e-5
KK_EPS = 1e-12

R0 = 0
K0 = R0 + D_RWKV
V0 = K0 + D_RWKV
WD0 = V0 + D_RWKV
AD0 = WD0 + DECAY_LORA
GD0 = AD0 + ICLR_LORA
RW_COLS = GD0 + GATE_LORA
CG0 = RW_COLS
CX0 = CG0 + D_CONV
CB0 = CX0 + D_CONV
FT0 = CB0 + D_CONV
D_IN = FT0 + D_FOURIER


def rms_norm(x, g):
    xf = x.astype(jnp.float32)
    y = xf * lax.rsqrt(jnp.mean(xf * xf, axis=-1, keepdims=True) + RMS_EPS)
    return (y * g.astype(jnp.float32)).astype(x.dtype)

def adaln(cvec, w, b):
    m = jax.nn.silu(cvec) @ w + b
    return jnp.split(m[:, None, :], N_MOD, axis=-1)

def modulate(h, shift, scale):
    return h * (1.0 + scale) + shift

def conv3(u, w):
    pad = [(0, 0)] * (u.ndim - 2) + [(1, 1), (0, 0)]
    up = jnp.pad(u, pad)
    return up[..., :-2, :] * w[0] + up[..., 1:-1, :] * w[1] + up[..., 2:, :] * w[2]

def grid_conv3(u, w):
    b, l, ch = u.shape
    rows = l // GRID_W
    return conv3(u.reshape(b, rows, GRID_W, ch), w).reshape(b, l, ch)

def rwkv_streams(rw, dec_w0, dec_up, iclr_a0, iclr_up, k_k, k_a):
    rw = rw.astype(jnp.float32)
    b, l = rw.shape[:2]

    def heads(t):
        return t.reshape(b, l, N_RWKV_HEADS, HEAD_DIM)

    r = rw[..., R0:K0]
    k = rw[..., K0:V0]
    v = rw[..., V0:WD0]
    wd = jnp.tanh(rw[..., WD0:AD0])
    ad = rw[..., AD0:GD0]
    gd = rw[..., GD0:RW_COLS]
    kk = heads(k * k_k)
    kk = kk / jnp.maximum(jnp.sqrt(jnp.sum(kk * kk, axis=-1, keepdims=True)), KK_EPS)
    per_dir = []
    for d in range(2):
        w_log = -jax.nn.softplus(-(dec_w0[d] + wd @ dec_up[d])) - 0.5
        a = jax.nn.sigmoid(iclr_a0[d] + ad @ iclr_up[d])
        kd = k * (1.0 + (a - 1.0) * k_a)
        per_dir.append((heads(jnp.exp(-jnp.exp(w_log))), heads(kd), heads(a)))
    return heads(r), heads(v), kk, per_dir, gd

def wkv_scan(r, w, k, v, kk, a, s0, reverse):
    def step(s, inp):
        r_t, w_t, k_t, v_t, kk_t, a_t = inp
        sa = jnp.einsum('bhij,bhj->bhi', s, -kk_t)
        s = (s * w_t[:, :, None, :] + sa[..., None] * (kk_t * a_t)[:, :, None, :]
             + v_t[..., None] * k_t[:, :, None, :])
        return s, jnp.einsum('bhij,bhj->bhi', s, r_t)

    xs = tuple(jnp.moveaxis(t, 1, 0) for t in (r, w, k, v, kk, a))
    s_fin, ys = lax.scan(step, s0, xs, reverse=reverse)
    return jnp.moveaxis(ys, 0, 1), s_fin

def rwkv_mix(streams, s0, ln_w, ln_b, r_k, g_up):
    r, v, kk, per_dir, gd = streams
    (wf, kf, af), (wb, kb, ab) = per_dir
    yf, sf = wkv_scan(r, wf, kf, v, kk, af, s0[0], False)
    yb, sb = wkv_scan(r, wb, kb, v, kk, ab, s0[1], True)
    y = yf + yb
    mu = jnp.mean(y, axis=-1, keepdims=True)
    var = jnp.mean(jnp.square(y - mu), axis=-1, keepdims=True)
    y = ((y - mu) * lax.rsqrt(var + GN_EPS) * ln_w.reshape(N_RWKV_HEADS, HEAD_DIM)
         + ln_b.reshape(N_RWKV_HEADS, HEAD_DIM))
    y = y + jnp.sum(r * (kf + kb) * r_k, axis=-1, keepdims=True) * v
    b, l = y.shape[:2]
    g = jax.nn.sigmoid(gd) @ g_up
    return y.reshape(b, l, D_RWKV) * g, (sf, sb)

def short_conv_mix(p, conv_w, conv_fn):
    return p[..., CB0:FT0] * conv_fn(p[..., CG0:CX0] * p[..., CX0:CB0], conv_w)

def fourier_mix(p):
    u = p[..., FT0:D_IN].astype(jnp.float32)
    b, l = u.shape[:2]
    u = u.reshape(b, l, N_FOURIER_GROUPS, HEAD_DIM)
    y = jnp.fft.fftn(u, axes=(1, 3), norm='ortho').real
    return y.reshape(b, l, D_FOURIER).astype(p.dtype)

def ffn(h, wg, wu, wd):
    return (jax.nn.silu(h @ wg) * (h @ wu)) @ wd

def first_inputs(seed: int = 0) -> dict:
    key = jax.random.key(seed)
    ks = jax.random.split(key, 32)
    f32 = jnp.float32

    def nrm(k, shape, s):
        return jax.random.normal(k, shape, f32) * s

    L = DEPTH
    left = jax.random.uniform(ks[8], (L, 1, RW_COLS), f32, 0.0, 0.4)
    right = jax.random.uniform(ks[9], (L, 1, RW_COLS), f32, 0.0, 0.4)
    rw_shift = jnp.concatenate([left, 1.0 - 0.5 * (left + right), right], axis=1)
    return {
        'x': nrm(ks[0], (BATCH, SEQ, D_MODEL), 1.0),
        'c': nrm(ks[1], (BATCH, D_MODEL), 1.0),
        'ctx': nrm(ks[2], (BATCH, CTX_LEN, D_MODEL), 1.0),
        'c_ctx': nrm(ks[3], (D_MODEL,), 1.0),
        'w_mod': nrm(ks[4], (L, D_MODEL, N_MOD * D_MODEL), 0.5 * D_MODEL ** -0.5),
        'b_mod': nrm(ks[5], (L, N_MOD * D_MODEL), 0.02),
        'norm_mix': 1.0 + nrm(ks[6], (L, D_MODEL), 0.05),
        'w_in': nrm(ks[7], (L, D_MODEL, D_IN), D_MODEL ** -0.5),
        'rw_shift': rw_shift,
        'dec_w0': jax.random.uniform(ks[10], (L, 2, D_RWKV), f32, -6.0, 1.0),
        'dec_up': nrm(ks[11], (L, 2, DECAY_LORA, D_RWKV), 0.5 * DECAY_LORA ** -0.5),
        'iclr_a0': nrm(ks[12], (L, 2, D_RWKV), 0.1),
        'iclr_up': nrm(ks[13], (L, 2, ICLR_LORA, D_RWKV), 0.5 * ICLR_LORA ** -0.5),
        'k_k': 0.85 + nrm(ks[14], (L, D_RWKV), 0.05),
        'k_a': 1.0 + nrm(ks[15], (L, D_RWKV), 0.05),
        'r_k': nrm(ks[16], (L, N_RWKV_HEADS, HEAD_DIM), 0.1),
        'ln_w': 1.0 + nrm(ks[17], (L, D_RWKV), 0.05),
        'ln_b': nrm(ks[18], (L, D_RWKV), 0.02),
        'g_up': nrm(ks[19], (L, GATE_LORA, D_RWKV), GATE_LORA ** -0.5),
        'conv_w': nrm(ks[20], (L, 3, D_CONV), 0.5),
        'w_out': nrm(ks[21], (L, D_MIX, D_MODEL), D_MIX ** -0.5),
        'norm_ffn': 1.0 + nrm(ks[22], (L, D_MODEL), 0.05),
        'w_gate': nrm(ks[23], (L, D_MODEL, D_FF), D_MODEL ** -0.5),
        'w_up': nrm(ks[24], (L, D_MODEL, D_FF), D_MODEL ** -0.5),
        'w_down': nrm(ks[25], (L, D_FF, D_MODEL), D_FF ** -0.5),
        'norm_final': 1.0 + nrm(ks[26], (D_MODEL,), 0.05),
    }

def first_block(x, c, ctx, c_ctx, w_mod, b_mod, norm_mix, w_in, rw_shift, dec_w0, dec_up,
              iclr_a0, iclr_up, k_k, k_a, r_k, ln_w, ln_b, g_up, conv_w, w_out,
              norm_ffn, w_gate, w_up, w_down, norm_final):
    xc = ctx
    s_zero = jnp.zeros((ctx.shape[0], N_RWKV_HEADS, HEAD_DIM, HEAD_DIM), jnp.float32)
    for i in range(DEPTH):
        sh1, sc1, ga1, sh2, sc2, ga2 = adaln(c, w_mod[i], b_mod[i])
        csh1, csc1, cga1, csh2, csc2, cga2 = adaln(c_ctx[None, :], w_mod[i], b_mod[i])
        px = modulate(rms_norm(x, norm_mix[i]), sh1, sc1) @ w_in[i]
        pc = modulate(rms_norm(xc, norm_mix[i]), csh1, csc1) @ w_in[i]
        rw_args = (dec_w0[i], dec_up[i], iclr_a0[i], iclr_up[i], k_k[i], k_a[i])
        out_args = (ln_w[i], ln_b[i], r_k[i], g_up[i])
        yc_rw, s_ctx = rwkv_mix(rwkv_streams(conv3(pc[..., :RW_COLS], rw_shift[i]), *rw_args),
                                (s_zero, s_zero), *out_args)
        yx_rw, _ = rwkv_mix(rwkv_streams(conv3(px[..., :RW_COLS], rw_shift[i]), *rw_args),
                            s_ctx, *out_args)
        yx = jnp.concatenate([yx_rw.astype(px.dtype),
                              short_conv_mix(px, conv_w[i], grid_conv3),
                              fourier_mix(px)], axis=-1) @ w_out[i]
        x = x + ga1 * yx
        x = x + ga2 * ffn(modulate(rms_norm(x, norm_ffn[i]), sh2, sc2),
                          w_gate[i], w_up[i], w_down[i])
        if i < DEPTH - 1:
            yc = jnp.concatenate([yc_rw.astype(pc.dtype),
                                  short_conv_mix(pc, conv_w[i], conv3),
                                  fourier_mix(pc)], axis=-1) @ w_out[i]
            xc = xc + cga1 * yc
            xc = xc + cga2 * ffn(modulate(rms_norm(xc, norm_ffn[i]), csh2, csc2),
                                 w_gate[i], w_up[i], w_down[i])
    return rms_norm(x, norm_final)


HG_HEADS = 8
HG_DK = 128
HG_DV = 128
HG_WIDTH = HG_HEADS * HG_DV
HG_CHUNK = 32
ATT_HEADS = 8
ATT_KV_HEADS = 2
HEAD_DIM_2 = 128
ATT_WIDTH = ATT_HEADS * HEAD_DIM_2
WINDOW = 128
ATT_BLOCK = 128
ROPE_THETA = 10000.0
D_MIX_2 = HG_WIDTH + ATT_WIDTH
HG_COLS = 3 * HG_HEADS * HG_DK + 2 * HG_HEADS * HG_DV
ATT_COLS = (ATT_HEADS + 2 * ATT_KV_HEADS) * HEAD_DIM_2
IN_COLS = HG_COLS + ATT_COLS
D_FF_2 = ((8 * D_MODEL + 3 * 256 - 1) // (3 * 256)) * 256
NEG_INF = -1e30
LB_SLACK = 1.0


def rms_norm_2(x, g):
    xf = x.astype(jnp.float32)
    y = xf * lax.rsqrt(jnp.mean(xf * xf, axis=-1, keepdims=True) + RMS_EPS)
    return (y * g.astype(jnp.float32)).astype(x.dtype)

def modulate_2(h, shift, scale):
    return h * (1 + scale) + shift

def axial_rope(x, row, col):
    half = HEAD_DIM_2 // 2
    nf = half // 2
    inv_freq = ROPE_THETA ** (-jnp.arange(nf, dtype=jnp.float32) / nf)
    extra = (1,) * (x.ndim - 3)

    def rotate(xa, pos):
        ang = pos.astype(jnp.float32)[:, None] * inv_freq
        cos = jnp.cos(ang).reshape((1, -1) + extra + (nf,))
        sin = jnp.sin(ang).reshape((1, -1) + extra + (nf,))
        x1 = xa[..., :nf].astype(jnp.float32)
        x2 = xa[..., nf:].astype(jnp.float32)
        return jnp.concatenate([x1 * cos - x2 * sin, x1 * sin + x2 * cos], axis=-1)

    out = jnp.concatenate([rotate(x[..., :half], row), rotate(x[..., half:], col)], axis=-1)
    return out.astype(x.dtype)

def chunked_gated_linear_scan(q, k, v, log_f, s0):
    B, H, T, DK = q.shape
    DV = v.shape[-1]
    N = T // HG_CHUNK
    q = q.reshape(B, H, N, HG_CHUNK, DK)
    k = k.reshape(B, H, N, HG_CHUNK, DK)
    v = v.reshape(B, H, N, HG_CHUNK, DV)
    b = jnp.cumsum(log_f.reshape(B, H, N, HG_CHUNK, DK), axis=3)
    b_last = b[:, :, :, -1:, :]
    q_dec = q * jnp.exp(b)
    k_inv = k * jnp.exp(-b)
    causal_in_chunk = jnp.tril(jnp.ones((HG_CHUNK, HG_CHUNK), dtype=bool))
    scores = jnp.einsum('bhnck,bhnsk->bhncs', q_dec, k_inv)
    scores = jnp.where(causal_in_chunk, scores, 0.0)
    o_intra = jnp.einsum('bhncs,bhnsv->bhncv', scores, v)
    kv_chunk = jnp.einsum('bhnsk,bhnsv->bhnkv', k * jnp.exp(b_last - b), v)
    decay = jnp.exp(b_last[:, :, :, 0, :])

    def step(s, inp):
        d, u = inp
        return d[..., None] * s + u, s

    s_final, s_starts = lax.scan(step, s0, (jnp.moveaxis(decay, 2, 0), jnp.moveaxis(kv_chunk, 2, 0)))
    s_starts = jnp.moveaxis(s_starts, 0, 2)
    o_inter = jnp.einsum('bhnck,bhnkv->bhncv', q_dec, s_starts)
    return (o_intra + o_inter).reshape(B, H, T, DV), s_final

def reverse_gated_linear_scan(q, k, v, log_f, s0):
    flip = lambda a: jnp.flip(a, axis=2)
    o, s = chunked_gated_linear_scan(flip(q), flip(k), flip(v), flip(log_f), s0)
    return flip(o), s

def hgrn2_mixer(p_lat, p_ctx, lb, norm_g, need_ctx_out):
    splits = [HG_HEADS * HG_DK, 2 * HG_HEADS * HG_DK, 3 * HG_HEADS * HG_DK,
              3 * HG_HEADS * HG_DK + HG_HEADS * HG_DV]

    def prep(p):
        B, T, _ = p.shape
        heads = lambda a: a.reshape(B, T, HG_HEADS, -1).transpose(0, 2, 1, 3).astype(jnp.float32)
        q, f_fwd, f_bwd, i, g = jnp.split(p, splits, axis=-1)
        q = jax.nn.silu(heads(q))
        gates = []
        for d, f_pre in enumerate((f_fwd, f_bwd)):
            lb_d = lb[d].reshape(HG_HEADS, 1, HG_DK)
            f = lb_d + (1.0 - lb_d) * jax.nn.sigmoid(heads(f_pre))
            gates.append((1.0 - f, jnp.log(f)))
        return q, heads(i), gates, g

    def readout(o, g):
        B, H, T, DV = o.shape
        o = rms_norm_2(o, norm_g).transpose(0, 2, 1, 3).reshape(B, T, H * DV)
        return (o * jax.nn.silu(g.astype(jnp.float32))).astype(g.dtype)

    qc, ic, (gc_f, gc_b), g_c = prep(p_ctx)
    ql, il, (gl_f, gl_b), g_l = prep(p_lat)
    B = p_lat.shape[0]
    zero = jnp.zeros((B, HG_HEADS, HG_DK, HG_DV), jnp.float32)
    oc_f, s_ctx_f = chunked_gated_linear_scan(qc, gc_f[0], ic, gc_f[1], zero)
    oc_b, s_ctx_b = reverse_gated_linear_scan(qc, gc_b[0], ic, gc_b[1], zero)
    ol_f, _ = chunked_gated_linear_scan(ql, gl_f[0], il, gl_f[1], s_ctx_f)
    ol_b, _ = reverse_gated_linear_scan(ql, gl_b[0], il, gl_b[1], s_ctx_b)
    lat_out = readout(ol_f + ol_b, g_l)
    ctx_out = readout(oc_f + oc_b, g_c) if need_ctx_out else None
    return lat_out, ctx_out

def window_attention(p_lat, p_ctx, q_g, k_g, sink, row, col, need_ctx_out):
    G = ATT_HEADS // ATT_KV_HEADS
    scale = HEAD_DIM_2 ** -0.5

    def split_heads(p):
        B, T, _ = p.shape
        q, k, v = jnp.split(p, [ATT_HEADS * HEAD_DIM_2, (ATT_HEADS + ATT_KV_HEADS) * HEAD_DIM_2], axis=-1)
        q = rms_norm_2(q.reshape(B, T, ATT_KV_HEADS, G, HEAD_DIM_2), q_g)
        k = rms_norm_2(k.reshape(B, T, ATT_KV_HEADS, HEAD_DIM_2), k_g)
        return q, k, v.reshape(B, T, ATT_KV_HEADS, HEAD_DIM_2)

    ql, kl, vl = split_heads(p_lat)
    qc, kc, vc = split_heads(p_ctx)
    ql = axial_rope(ql, row, col)
    kl = axial_rope(kl, row, col)
    B, T = p_lat.shape[:2]
    L = p_ctx.shape[1]
    NB = T // ATT_BLOCK
    sink_f = sink.astype(jnp.float32).reshape(ATT_KV_HEADS, G, 1, 1)

    qb = ql.reshape(B, NB, ATT_BLOCK, ATT_KV_HEADS, G, HEAD_DIM_2)
    pad = ((0, 0), (ATT_BLOCK, ATT_BLOCK), (0, 0), (0, 0))
    kp = jnp.pad(kl, pad).reshape(B, NB + 2, ATT_BLOCK, ATT_KV_HEADS, HEAD_DIM_2)
    vp = jnp.pad(vl, pad).reshape(B, NB + 2, ATT_BLOCK, ATT_KV_HEADS, HEAD_DIM_2)
    k_band = jnp.concatenate([kp[:, :-2], kp[:, 1:-1], kp[:, 2:]], axis=2)
    v_band = jnp.concatenate([vp[:, :-2], vp[:, 1:-1], vp[:, 2:]], axis=2)
    s_band = jnp.einsum('bnqhgd,bnkhd->bhgnqk', qb, k_band).astype(jnp.float32) * scale
    s_ctx = jnp.einsum('bnqhgd,bkhd->bhgnqk', qb, kc).astype(jnp.float32) * scale
    qi = jnp.arange(ATT_BLOCK)[:, None]
    kj = jnp.arange(3 * ATT_BLOCK)[None, :]
    within = jnp.abs(kj - ATT_BLOCK - qi) <= WINDOW
    k_pos = (jnp.arange(NB)[:, None] - 1) * ATT_BLOCK + kj
    in_range = (k_pos >= 0) & (k_pos < T)
    mask = within[None, :, :] & in_range[:, None, :]
    s_band = jnp.where(mask, s_band, NEG_INF)
    sink_col = jnp.broadcast_to(sink_f[None, :, :, :, :, None], s_band.shape[:-1] + (1,))
    probs = jax.nn.softmax(jnp.concatenate([s_band, s_ctx, sink_col], axis=-1), axis=-1)
    p_band = probs[..., :3 * ATT_BLOCK].astype(vl.dtype)
    p_ctxk = probs[..., 3 * ATT_BLOCK:3 * ATT_BLOCK + L].astype(vc.dtype)
    o_lat = (jnp.einsum('bhgnqk,bnkhd->bnqhgd', p_band, v_band)
             + jnp.einsum('bhgnqk,bkhd->bnqhgd', p_ctxk, vc))
    lat_out = o_lat.reshape(B, T, ATT_WIDTH)

    ctx_out = None
    if need_ctx_out:
        sc = jnp.einsum('bqhgd,bkhd->bhgqk', qc, kc).astype(jnp.float32) * scale
        sink_c = jnp.broadcast_to(sink_f[None, :, :, :, :], sc.shape[:-1] + (1,))
        pc = jax.nn.softmax(jnp.concatenate([sc, sink_c], axis=-1), axis=-1)[..., :L]
        o_c = jnp.einsum('bhgqk,bkhd->bqhgd', pc.astype(vc.dtype), vc)
        ctx_out = o_c.reshape(B, L, ATT_WIDTH)
    return lat_out, ctx_out

def swiglu(h, w_gate_up, w_down):
    gate, up = jnp.split(h @ w_gate_up, 2, axis=-1)
    return (jax.nn.silu(gate) * up) @ w_down

def second_inputs(seed: int = 0) -> dict:
    key = jax.random.key(seed)
    ks = jax.random.split(key, 17)
    nrm = lambda k, shape, s: s * jax.random.normal(k, shape, jnp.float32)
    hg_lb = nrm(ks[9], (DEPTH + 1, 2, HG_HEADS * HG_DK), 0.1).at[DEPTH].add(LB_SLACK)
    return {
        "x": nrm(ks[0], (BATCH, SEQ, D_MODEL), 1.0),
        "c": nrm(ks[1], (BATCH, D_MODEL), 1.0),
        "ctx": nrm(ks[2], (BATCH, CTX_LEN, D_MODEL), 1.0),
        "c_ctx": nrm(ks[3], (D_MODEL,), 1.0),
        "w_mod": nrm(ks[4], (DEPTH, D_MODEL, N_MOD * D_MODEL), 0.5 * D_MODEL ** -0.5),
        "b_mod": nrm(ks[5], (DEPTH, N_MOD * D_MODEL), 0.01),
        "norm_mix_g": 1.0 + nrm(ks[6], (DEPTH, D_MODEL), 0.05),
        "norm_ffn_g": 1.0 + nrm(ks[7], (DEPTH, D_MODEL), 0.05),
        "w_in": nrm(ks[8], (DEPTH, D_MODEL, IN_COLS), D_MODEL ** -0.5),
        "hg_lb": hg_lb,
        "hg_norm_g": 1.0 + nrm(ks[10], (DEPTH, HG_DV), 0.05),
        "q_norm_g": 1.0 + nrm(ks[11], (DEPTH, HEAD_DIM_2), 0.05),
        "k_norm_g": 1.0 + nrm(ks[12], (DEPTH, HEAD_DIM_2), 0.05),
        "attn_sink": nrm(ks[13], (DEPTH, ATT_HEADS), 1.0),
        "w_out": nrm(ks[14], (DEPTH, D_MIX_2, D_MODEL), D_MIX_2 ** -0.5),
        "w_gate_up": nrm(ks[15], (DEPTH, D_MODEL, 2 * D_FF_2), D_MODEL ** -0.5),
        "w_down": nrm(ks[16], (DEPTH, D_FF_2, D_MODEL), D_FF_2 ** -0.5),
    }

def second_block(x, c, ctx, c_ctx, w_mod, b_mod, norm_mix_g, norm_ffn_g, w_in, hg_lb,
              hg_norm_g, q_norm_g, k_norm_g, attn_sink, w_out, w_gate_up, w_down):
    T = x.shape[1]
    rows = T // GRID_W
    row = jnp.broadcast_to(jnp.arange(rows)[:, None], (rows, GRID_W)).reshape(-1)
    col = jnp.broadcast_to(jnp.arange(GRID_W)[None, :], (rows, GRID_W)).reshape(-1)
    lb_all = jnp.cumsum(jax.nn.softmax(hg_lb.astype(jnp.float32), axis=0), axis=0)
    y = ctx
    for l in range(DEPTH):
        need_ctx_out = l < DEPTH - 1
        sh_m, sc_m, gt_m, sh_f, sc_f, gt_f = [m[:, None, :] for m in
            jnp.split(jax.nn.silu(c) @ w_mod[l] + b_mod[l], N_MOD, axis=-1)]
        csh_m, csc_m, cgt_m, csh_f, csc_f, cgt_f = jnp.split(
            jax.nn.silu(c_ctx) @ w_mod[l] + b_mod[l], N_MOD, axis=-1)

        h_lat = modulate_2(rms_norm_2(x, norm_mix_g[l]), sh_m, sc_m)
        h_ctx = modulate_2(rms_norm_2(y, norm_mix_g[l]), csh_m, csc_m)
        p_lat = h_lat @ w_in[l]
        p_ctx = h_ctx @ w_in[l]
        hg_lat, hg_ctx = hgrn2_mixer(p_lat[..., :HG_COLS], p_ctx[..., :HG_COLS],
                                     lb_all[l], hg_norm_g[l], need_ctx_out)
        at_lat, at_ctx = window_attention(p_lat[..., HG_COLS:], p_ctx[..., HG_COLS:],
                                          q_norm_g[l], k_norm_g[l], attn_sink[l],
                                          row, col, need_ctx_out)
        x = x + gt_m * (jnp.concatenate([hg_lat, at_lat], axis=-1) @ w_out[l])

        x = x + gt_f * swiglu(modulate_2(rms_norm_2(x, norm_ffn_g[l]), sh_f, sc_f),
                              w_gate_up[l], w_down[l])

        if need_ctx_out:
            y = y + cgt_m * (jnp.concatenate([hg_ctx, at_ctx], axis=-1) @ w_out[l])
            y = y + cgt_f * swiglu(modulate_2(rms_norm_2(y, norm_ffn_g[l]), csh_f, csc_f),
                                   w_gate_up[l], w_down[l])
    return x


def setup_inputs(seed=0):
    out = dict(first_inputs(seed))
    for name, value in second_inputs(seed + 1).items():
        if name != "x":
            out[name + "_2"] = value
    return out


def reference(
    x, c, ctx, c_ctx, w_mod, b_mod, norm_mix, w_in, rw_shift, dec_w0, dec_up, iclr_a0, iclr_up,
    k_k, k_a, r_k, ln_w, ln_b, g_up, conv_w, w_out, norm_ffn, w_gate, w_up, w_down, norm_final,
    c_2, ctx_2, c_ctx_2, w_mod_2, b_mod_2, norm_mix_g_2, norm_ffn_g_2, w_in_2, hg_lb_2,
    hg_norm_g_2, q_norm_g_2, k_norm_g_2, attn_sink_2, w_out_2, w_gate_up_2, w_down_2,
):
    x = first_block(
        x, c, ctx, c_ctx, w_mod, b_mod, norm_mix, w_in, rw_shift, dec_w0, dec_up, iclr_a0,
        iclr_up, k_k, k_a, r_k, ln_w, ln_b, g_up, conv_w, w_out, norm_ffn, w_gate, w_up, w_down,
        norm_final,
    )
    return second_block(
        x, c_2, ctx_2, c_ctx_2, w_mod_2, b_mod_2, norm_mix_g_2, norm_ffn_g_2, w_in_2, hg_lb_2,
        hg_norm_g_2, q_norm_g_2, k_norm_g_2, attn_sink_2, w_out_2, w_gate_up_2, w_down_2,
    )


_drawn_inputs = setup_inputs


def setup_inputs(seed=0):
    import zlib

    import numpy as np

    out = dict(_drawn_inputs(seed))
    spreads = {}
    factors = {'norm_mix': 2.736,
     'dec_up': 8.0,
     'iclr_a0': 8.0,
     'k_k': 31.94,
     'k_a': 4.726,
     'ln_w': 8.0,
     'ln_b': 38.711,
     'norm_ffn': 3.662,
     'ctx_2': 4.233,
     'b_mod_2': 5.608,
     'norm_mix_g_2': 6.003,
     'norm_ffn_g_2': 3.973,
     'hg_norm_g_2': 7.871,
     'q_norm_g_2': 8.0,
     'k_norm_g_2': 8.0,
     'attn_sink_2': 8.0}
    for name, (base, spread) in spreads.items():
        noise = np.random.default_rng([zlib.crc32(name.encode()), seed]).standard_normal(out[name].shape)
        drawn = base * np.exp(spread * noise) if base else spread * noise
        out[name] = jnp.asarray(drawn.astype(out[name].dtype))
    for name, factor in factors.items():
        out[name] = (out[name] * factor).astype(out[name].dtype)
    return out
```

```python
import math

import numpy as np
import concourse.bass as bass
from concourse import mybir
from contextlib import ExitStack

F32 = mybir.dt.float32
ALU = mybir.AluOpType
ACT = mybir.ActivationFunctionType
AX = mybir.AxisListType

P = 128
DM = 2048
KT = DM // P
T = 256
L = 256
TA = T + L
TT = TA // P
CH = 32
NCH = TA // CH
CPT = P // CH
RMS_EPS = 1e-6
GN_EPS = 64e-5
KK_EPS = 1e-12
HD = 64
D_RW = DM // 2
NP1 = D_RW // P
LORA = 96
D_CV = DM // 4
NCV = D_CV // P
D_IN = 3 * D_RW + 2 * LORA + 256 + 4 * D_CV
D_FF = 5632
NFF = D_FF // P
GRID_W = 64
DECAY = math.exp(-0.5)
NH2 = 8
NKV = 2
WINDOW = 128
IN2 = 5 * NH2 * P + (NH2 + 2 * NKV) * P
NEG = -1e30

RING = 3
SLOT_COLS = 256
DOWN_K = NFF // 4


def constants():
    s = np.arange(P)[:, None]
    t = np.arange(P)[None, :]
    out = {}
    out["ident"] = (s == t)
    out["ones"] = np.ones((P, P))
    out["head_ones"] = (s // HD == t // HD)
    out["ident64"] = np.concatenate([np.eye(HD), np.eye(HD)], 0)
    same = s // CH == t // CH
    out["strict"] = np.stack([same & (s < t), same & (s > t)], 1)
    out["incl"] = np.stack([same & (s <= t), same & (s >= t)], 1)
    incl, strict = out.pop("incl"), out["strict"]
    out["mask3"] = np.stack([incl, strict, incl], 2)
    out["strict_ts"] = strict[:, ::-1]
    pair = [(s // (2 * b) == t // (2 * b)) & (s // b != t // b) for b in (1, 2, 4, 8, 16)]
    out["level1"] = np.stack([pair[0] & (s < t), pair[0] & (s > t)], 1)
    out["levels"] = np.stack(pair, 1)
    out["carry"] = np.broadcast_to((np.arange(TA) % CH != 0)[None, :], (P, TA))
    seq = np.arange(T)
    ang = 2 * np.pi * ((seq[:, None] * seq[None, :]) % T) / T
    norm = 1.0 / math.sqrt(T * HD)
    out["seq_dft"] = np.stack([np.cos(ang).reshape(2, P, T), np.sin(ang).reshape(2, P, T)], 1).transpose(2, 0, 1, 3)
    hh = 2 * np.pi * (((s % HD) * (t % HD)) % HD) / HD
    blk = (s // HD == t // HD)
    out["head_dft"] = np.stack([blk * np.cos(hh) * norm, -1.0 * blk * np.sin(hh) * norm], 1)
    half, nf = HD, HD // 2
    inv = 10000.0 ** (-np.arange(nf, dtype=np.float32) / nf)
    d = np.arange(P)
    pos = np.where((d < half)[:, None], (seq // GRID_W)[None, :], (seq % GRID_W)[None, :])
    a = (pos.astype(np.float32) * inv.astype(np.float32)[d % nf][:, None]).astype(np.float32).astype(np.float64)
    out["rope"] = np.stack([np.cos(a), np.sin(a)], 1)
    rot = np.zeros((P, P))
    for i in range(P):
        if i % half < nf:
            rot[i + nf, i] = -1.0
        else:
            rot[i - nf, i] = 1.0
    out["rope_rot"] = rot
    q = np.arange(T).reshape(2, P).T[:, :, None]
    k = np.arange(T)[None, None, :]
    out["window"] = np.where(np.abs(q - k) <= WINDOW, 0.0, NEG)
    parts, at, where = [], 0, {}
    for name, v in out.items():
        v = np.ascontiguousarray(v, dtype=np.float32)
        where[name] = (at, v.shape[1:])
        parts.append(v.reshape(P, -1))
        at += parts[-1].shape[1]
    return np.concatenate(parts, 1), where


def row_params():
    b = {}
    at = 0
    for name, n in (("c", 16), ("c_ctx", 16), ("c_2", 16), ("c_ctx_2", 16), ("norm_mix", 16), ("norm_ffn", 16),
                    ("norm_final", 16), ("k_k", 8), ("k_a", 8)):
        b[name] = (0, at, n)
        at += n
    at = 0
    for name, n in (("b_mod", 96), ("dec_w0", 16), ("iclr_a0", 16)):
        b[name] = (1, at, n)
        at += n
    at = 0
    for name, n in (("b_mod_2", 96), ("norm_mix_g_2", 16), ("norm_ffn_g_2", 16)):
        b[name] = (2, at, n)
        at += n
    at = 0
    for name, n in (("rw_shift", 84), ("conv_w", 12), ("r_k", 8), ("hg_norm_g_2", 1), ("q_norm_g_2", 1),
                    ("k_norm_g_2", 1)):
        b[name] = (3, at, n)
        at += n
    b["hg_lb_2"] = (4, 0, 32)
    return b


ROWS = row_params()
N_BATCH = 5
BATCH_ROWS = (128, 128, 128, 107, 32)
RW_TILES = 28


def col(name, i=0):
    batch, at, _ = ROWS[name]
    return batch * P + at + i


class State:
    pass


class Link:

    def __init__(self, sem):
        self.sem, self.n, self.eng = sem, 0, None

    def __call__(self, ins):
        self.n += 1
        ins.then_inc(self.sem, 1)
        self.eng.wait_ge(self.sem, self.n)

    def mark(self, ins):
        self.n += 1
        ins.then_inc(self.sem, 1)

    def wait(self):
        self.eng.wait_ge(self.sem, self.n)


class Stream:

    def __init__(self, st):
        self.st = st
        self.issued = 0
        self.done = 0

    def place(self, n):
        return n % RING

    def load_count(self, n, i=0, per=0):
        return 16 * (n // RING + 1) + i * (16 * (per // RING))


def ring_view(st, n, k, cols):
    base = (n % RING) * KT * SLOT_COLS
    return st.ring[:, base:base + k * cols].rearrange("p (k c) -> p k c", k=k)


def arrived(eng, st, n, i=0, per=0):
    eng.wait_ge(st.s_load[n % RING], st.stream.load_count(n, i, per))


MOD_SLOTS = 6 * DM // SLOT_COLS
MOD_FIRST = 2 * DM // SLOT_COLS
IN1_STEPS, OUT_STEPS, FFN_UNITS, IN2_STEPS = 22, DM // SLOT_COLS, D_FF // SLOT_COLS, IN2 // SLOT_COLS
IN1_MOD = [[] for _ in range(IN1_STEPS)]
_at = MOD_FIRST
for _s in range(IN1_STEPS):
    for _ in range(2 if _s in (5, 9) else 1):
        IN1_MOD[_s].append(_at)
        _at += 1
OUT1_MOD = [_at + s for s in range(OUT_STEPS)]
assert OUT1_MOD[-1] == MOD_SLOTS - 1
FFN1_MOD, IN2_MOD = 0, FFN_UNITS
assert IN2_MOD + IN2_STEPS == MOD_SLOTS


def weight_slots():
    out = []
    spans = {}

    def span(name, items):
        spans[name] = (len(out), len(items))
        out.extend(items)

    def cols(name, c):
        return (name, 0, KT, c * 256, 256)

    def down(name, c):
        return [(name, k * DOWN_K, DOWN_K, c * 256, 256) for k in range(4)]

    span("mod1", [cols("w_mod", c) for c in range(MOD_FIRST)])
    items = [cols("w_in", c) for c in range(12)] + [("w_in", 0, KT, 3072, 192), ("w_in", 0, KT, 3264, 256)]
    items += [("w_in", 0, KT, 3520 + c * 256, 256) for c in range(8)]
    span("in1", [w for s, x in enumerate(items) for w in [x] + [cols("w_mod", c) for c in IN1_MOD[s]]])
    span("out1", [w for s in range(OUT_STEPS) for w in (cols("w_out", s), cols("w_mod", OUT1_MOD[s]))])
    span("ffn1", [w for u in range(FFN_UNITS) for w in (cols("w_gate", u), cols("w_up", u), cols("w_mod_2", FFN1_MOD + u))])
    span("down1", [w for u in range(8) for w in down("w_down", u)])
    span("in2", [w for c in range(IN2_STEPS) for w in (cols("w_in_2", c), cols("w_mod_2", IN2_MOD + c))])
    span("out2", [cols("w_out_2", c) for c in range(8)])
    span("ffn2", [("w_gate_up_2", 0, KT, u * D_FF + c * 256, 256) for c in range(22) for u in range(2)])
    span("down2", [w for u in range(8) for w in down("w_down_2", u)])
    return out, spans


SLOTS, SPANS = weight_slots()
BY_DVE = [name.startswith("w_mod") and n >= MOD_FIRST for n, (name, *_) in enumerate(SLOTS)]


def use_count(n):
    return sum(x == BY_DVE[n] for x in BY_DVE[:n + 1])


def stream_weights(sp, st, upto):
    while st.stream.issued < upto:
        n = st.stream.issued
        period, reps = best_run(n, upto)
        if reps >= 2:
            with sp.Fori(0, reps) as i:
                for t in range(period):
                    issue(sp, st, n + t, i, period)
            st.stream.issued += reps * period
        else:
            issue(sp, st, n, 0, 0)
            st.stream.issued += 1


def best_run(n, upto):
    best = (1, 1)
    if n < RING:
        return best
    for period in (RING, 2 * RING, 4 * RING):
        reps = 1
        while True:
            lo = n + reps * period
            if lo + period > upto:
                break
            a, b = SLOTS[n:n + period], SLOTS[lo:lo + period]
            step = SLOTS[n + period][3] - SLOTS[n][3]
            if any(x[:3] != y[:3] or x[4] != y[4] or y[3] - x[3] != reps * step for x, y in zip(a, b)):
                break
            if BY_DVE[n - RING:n - RING + period] != BY_DVE[lo - RING:lo - RING + period]:
                break
            reps += 1
        if reps >= 2 and reps * period > best[0] * best[1]:
            best = (period, reps)
    return best


def issue(sp, st, n, i, per):
    name, k0, k, c0, cols = SLOTS[n]
    w = st.dram[name]
    step = SLOTS[n + per][3] - c0 if per else 0
    columns = bass.ds(i * step + c0, cols) if per else slice(c0, c0 + cols)
    if n >= RING:
        old = n - RING
        per_turn = use_count(old + per) - use_count(old) if per else 0
        sp.wait_ge(st.s_mod_used if BY_DVE[old] else st.s_slot_used, i * per_turn + use_count(old))
    sp.dma_start(ring_view(st, n, k, cols),
                 w[k0 * P:(k0 + k) * P, columns].rearrange("(t p) n -> p t n", p=P)).then_inc(st.s_load[n % RING], 16)


def load_inputs(nc, st):
    d = st.dram
    rows = st.work[:, 4096 * 2:4096 * 2 + N_BATCH * P].rearrange("p (b c) -> p b c", b=N_BATCH)
    xtok = st.work[:, 8192 + 1024:8192 + 1024 + 4096].rearrange("p (t c) -> p t c", t=2)
    ctok = st.work[:, 8192 + 1024 + 4096:8192 + 1024 + 8192].rearrange("p (t c) -> p t c", t=2)
    hT = st.hT
    s_rows, s_x, s_zero, s_const = st.sem("rows_in"), st.sem("x_in"), st.sem("rows_zeroed"), st.sem("const_in")
    s_rowT, s_par, s_xT, s_xev = st.sem("rows_transposed"), st.sem("params_ready"), st.sem("x_transposed"), st.sem("x_evac")
    n_rows = 0

    with nc.Block() as block:
        @block.sync
        def _(sp):
            sp.dma_start(st.const[:], d["const"]).then_inc(s_const, 16)
            sp.dma_start(xtok, d["x"].rearrange("(t p) c -> p t c", p=P)).then_inc(s_x, 16)
            sp.dma_start(ctok, d["ctx"].rearrange("(t p) c -> p t c", p=P)).then_inc(s_x, 16)
            stream_weights(sp, st, RING)

        @block.gpsimd
        def _(pool):
            nc.gpsimd.memset(rows, 0.0).then_inc(s_zero, 1)

        @block.scalar
        def _(act):
            nonlocal n_rows
            act.wait_ge(s_zero, 1)

            def put(name, src, at=0, width=P):
                nonlocal n_rows
                batch, r, _ = ROWS[name]
                n_rows += 1
                act.dma_start(rows[r + at:r + at + src.shape[0], batch, 0:width], src).then_inc(s_rows, 16)

            for name in ("c", "c_ctx", "c_2", "c_ctx_2", "norm_mix", "norm_ffn", "norm_final", "k_k", "k_a",
                         "b_mod", "dec_w0", "iclr_a0", "b_mod_2", "norm_mix_g_2", "norm_ffn_g_2", "conv_w",
                         "r_k", "hg_norm_g_2", "q_norm_g_2", "k_norm_g_2", "hg_lb_2"):
                put(name, d[name].rearrange("(a c) -> a c", c=P))
            for tap in range(3):
                w = d["rw_shift"][tap, :]
                put("rw_shift", w[0:3072].rearrange("(a c) -> a c", c=P), tap * RW_TILES)
                put("rw_shift", w[3072:3072 + 192].rearrange("(a c) -> a c", c=LORA), tap * RW_TILES + 24, LORA)
                put("rw_shift", w[3264:3520].rearrange("(a c) -> a c", c=P), tap * RW_TILES + 26)
            act.dma_start(st.sink[:], d["attn_sink_2"].rearrange("(a c) -> a c", a=1).partition_broadcast(P)
                          ).then_inc(s_rows, 16)
            n_rows += 1
            act.wait_ge(s_par, 1)
            nc.scalar.activation(st.silu_c[:], st.par[:, 0:64], ACT.Silu).then_inc(st.s_silu, 1)
            act.wait_ge(st.s_silu, 1)

        @block.tensor
        def _(pe):
            pe.wait_ge(s_const, 16)
            pe.wait_ge(s_rows, 16 * n_rows)
            for b in range(N_BATCH):
                n = BATCH_ROWS[b]
                last = nc.tensor.transpose(st.psum[b // 4][:, (b % 4) * P:(b % 4) * P + n], rows[0:n, b, :],
                                           st.c("ident")[0:n, 0:n])
            last.then_inc(s_rowT, 1)
            pe.wait_ge(s_x, 32)
            for m in range(2 * KT // 2):
                src = (xtok, ctok)[m // (KT // 2)]
                if m >= 4:
                    pe.wait_ge(s_xev, m - 3)
                for j in range(4):
                    k, t = (m % (KT // 2)) * 2 + j // 2, j % 2
                    last = nc.tensor.transpose(st.psum[2 + m % 4][:, j * P:(j + 1) * P], src[:, t, k * P:(k + 1) * P],
                                               st.c("ident"))
                last.then_inc(s_xT, 1)

        @block.vector
        def _(dve):
            st.vl.eng = dve
            dve.wait_ge(s_rowT, 1)
            st.vl.mark(nc.vector.tensor_copy(st.par[:, 0:384], st.psum[0][:, 0:384]))
            st.vl.mark(nc.vector.tensor_copy(st.par[:, 384:384 + 107], st.psum[0][:, 384:384 + 107]))
            nc.vector.tensor_copy(st.par[:, 512:544], st.psum[1][:, 0:32]).then_inc(s_par, 1)
            for m in range(KT):
                dve.wait_ge(s_xT, m + 1)
                k = (m % (KT // 2)) * 2
                dst = st.xT[:, k:k + 2, :] if m < KT // 2 else hT[:, k:k + 2, 0:L]
                nc.vector.tensor_copy(dst, st.psum[2 + m % 4][:].rearrange("p (a b) -> p a b", a=2)).then_inc(s_xev, 1)


def mod_macs(dve, st, n, which, vectors, acc, s_mac, mac, s_col, col_count, i=0, per=0):
    v_ = st.nc.vector
    partial, sums = acc
    arrived(dve, st, n, i, per)
    w = ring_view(st, n, KT, 256)
    before = use_count(n) - 1
    if before:
        dve.wait_ge(st.s_mod_used, i * (use_count(n + per) - use_count(n)) + before)
    step = 0
    for k in range(KT):
        for v in range(vectors):
            c = st.silu_c[:, (2 * which + v) * KT + k:(2 * which + v) * KT + k + 1]
            a = partial[:, 2 * v + k % 2, :]
            if k < 2:
                ins = v_.tensor_scalar(a, w[:, k, :], c, None, ALU.mult)
            else:
                dve.wait_ge(s_mac, mac + (step + 1 - 2 * vectors))
                ins = v_.scalar_tensor_tensor(a, w[:, k, :], c, a, ALU.mult, ALU.add)
            ins.then_inc(s_mac, 1)
            step += 1
    dve.wait_ge(s_mac, mac + step)
    if col_count is not None:
        dve.wait_ge(s_col, col_count)
    for v in range(vectors):
        ins = v_.tensor_tensor(sums[:, v, :], partial[:, 2 * v, :], partial[:, 2 * v + 1, :], ALU.add)
        ins.then_inc(s_mac if v + 1 < vectors else st.s_mod_used, 1)


def mac_steps(vectors):
    return KT * vectors + vectors - 1


def mod_sums(nc, st, sums, vectors, at, s_col):
    for half in range(2):
        for v in range(vectors):
            last = nc.tensor.matmul(st.psum[7][:, at + 2 * half + v:at + 2 * half + v + 1],
                                    sums[:, v, half * P:(half + 1) * P], st.c("ones")[:, 0:1], start=True, stop=True)
    last.then_inc(s_col, 1)


class SideMod:

    def __init__(self, nc, st, name, which, slots, area):
        self.nc, self.st, self.which, self.slots = nc, st, which, slots
        self.partial = area[:, 0:512].rearrange("p (a c) -> p a c", a=2)
        self.sums = area[:, 512:1024].rearrange("p (a c) -> p a c", a=2)
        self.s_mac, self.s_col = st.sem(f"{name}_mod_step"), st.sem(f"{name}_mod_columns")
        self.dve_at = self.pe_at = 0

    def accumulate(self, dve, upto):
        while self.dve_at < len(self.slots) and self.slots[self.dve_at][0] < upto:
            j = self.dve_at
            mod_macs(dve, self.st, self.slots[j][0], self.which, 1, (self.partial, self.sums[:, j % 2:j % 2 + 1, :]),
                     self.s_mac, j * mac_steps(1), self.s_col, j - 1 if j >= 2 else None)
            self.dve_at += 1

    def columns(self, pe, upto):
        if self.pe_at < len(self.slots) and self.slots[self.pe_at][0] < upto:
            j = self.pe_at
            pe.wait_ge(self.st.s_mod_used, use_count(self.slots[j][0]))
            mod_sums(self.nc, self.st, self.sums[:, j % 2:j % 2 + 1, :], 1, 4 * j, self.s_col)
            self.pe_at += 1

    def flush(self, pe):
        while self.pe_at < len(self.slots):
            self.columns(pe, len(SLOTS))

    def collect(self, dve):
        st, n = self.st, len(self.slots)
        dve.wait_ge(self.s_col, n)
        t0 = 2 * self.slots[0][1]
        st.vl(st.nc.vector.tensor_copy(
            st.modraw[self.which][:].rearrange("p (t v) -> p t v", v=2)[:, t0:t0 + 2 * n, 0],
            st.psum[7][:, 0:4 * n].rearrange("p (t v) -> p t v", v=2)[:, :, 0]))
        mod_columns(st.nc, st, self.which, slice(t0, t0 + 2 * n), 1)


def mod_columns(nc, st, which, tiles, vectors):
    b = st.par[:, col(("b_mod", "b_mod_2")[which]):]
    for v in range(vectors):
        st.vl.mark(nc.vector.tensor_tensor(
            st.mod[which][:, v, tiles], st.modraw[which][:].rearrange("p (t v) -> p v t", v=2)[:, v, tiles],
            b[:, tiles], ALU.add))
    st.vl.wait()


def gain_columns(nc, st, which, norm, at, v, slot):
    st.vl(nc.vector.scalar_tensor_tensor(st.gain[:, which, slot, :], st.mod[which][:, v, at:at + 16], 1.0,
                                         st.par[:, col(norm):col(norm) + 16], ALU.add, ALU.mult))


def first_modulation(nc, st):
    s_row, s_out, s_T = st.sem("mod_row"), st.sem("mod_row_out"), st.sem("mod_row_transposed")
    first, count = SPANS["mod1"]
    rows = st.carve(16384, count, SLOT_COLS)
    with nc.Block() as block:
        @block.sync
        def _(sp):
            stream_weights(sp, st, first + count + RING)

        @block.tensor
        def _(pe):
            silu = st.silu_c[:].rearrange("p (v k) -> p k v", v=4)
            for s in range(count):
                arrived(pe, st, first + s)
                w = ring_view(st, first + s, KT, SLOT_COLS)
                if s >= 8:
                    pe.wait_ge(s_out, s - 7)
                for k in range(KT):
                    last = nc.tensor.matmul(st.psum[s % 8][0:2, 0:SLOT_COLS], silu[:, k, 0:2],
                                            w[:, k, :], start=k == 0, stop=k == KT - 1)
                last.then_inc(st.s_slot_used, 1)
            pe.wait_ge(s_out, count)
            for s in range(count):
                for half in range(2):
                    t = 2 * s + half
                    last = nc.tensor.transpose(st.psum[0][:, 2 * t:2 * t + 2], rows[0:2, s, half * P:(half + 1) * P],
                                               st.c("ident")[0:2, 0:2])
            last.then_inc(s_T, 1)

        @block.vector
        def _(dve):
            for s in range(count):
                dve.wait_ge(st.s_slot_used, s + 1)
                nc.vector.tensor_copy(rows[0:2, s, :], st.psum[s % 8][0:2, 0:SLOT_COLS]
                                      ).then_inc(s_out, 1)
            st.vl.eng = dve
            dve.wait_ge(s_T, 1)
            st.vl(nc.vector.tensor_copy(st.modraw[0][:, 0:4 * count], st.psum[0][:, 0:4 * count]))
            mod_columns(nc, st, 0, slice(0, 2 * count), 2)
            gain_columns(nc, st, 0, "norm_mix", 16, 0, 0)
            gain_columns(nc, st, 0, "norm_mix", 16, 1, 1)


def normalise(nc, st, name, parts):
    s_sq, s_ms, s_rt, s_xn, s_h = (st.sem(f"{name}_{x}") for x in ("squared", "mean_sq", "root", "scaled", "shifted"))
    with nc.Block() as block:
        @block.scalar
        def _(act):
            for src, dst, gain, shift in parts:
                nc.scalar.activation(st.sq, src, ACT.Square).then_inc(s_sq, 1)
                j = [p[0] is src for p in parts].index(True)
                act.wait_ge(s_ms, j + 1)
                nc.scalar.activation(st.rstd[:, j, :], st.psum[j][:, 0:256], ACT.Sqrt, bias=st.eps[:, 0:1],
                                     scale=1.0 / DM).then_inc(s_rt, 1)
            for j, (src, dst, gain, shift) in enumerate(parts):
                act.wait_ge(s_xn, j + 1)
                for k in range(KT):
                    nc.scalar.activation(dst[:, k, :], dst[:, k, :], ACT.Identity, scale=gain[:, k:k + 1],
                                         bias=shift[:, k:k + 1] if shift is not None else 0.0).then_inc(s_h, 1)

        @block.tensor
        def _(pe):
            for j in range(len(parts)):
                pe.wait_ge(s_sq, j + 1)
                for k in range(KT):
                    last = nc.tensor.matmul(st.psum[j][:, 0:256], st.c("ones"), st.sq[:, k, :], start=k == 0,
                                            stop=k == KT - 1)
                last.then_inc(s_ms, 1)

        @block.vector
        def _(dve):
            st.vl.eng = dve
            for j, (src, dst, gain, shift) in enumerate(parts):
                dve.wait_ge(s_rt, j + 1)
                st.vl(nc.vector.reciprocal(st.rstd[:, j, :], st.rstd[:, j, :]))
                nc.vector.tensor_tensor(dst, src, st.rstd[:, j:j + 1, :].broadcast_to([P, KT, 256]),
                                        ALU.mult).then_inc(s_xn, 1)


def in_projection1(nc, st, lookahead):
    first, count = SPANS["in1"]
    tiles = []
    for s in range(12):
        for half in range(2):
            g = 2 * s + half
            tiles.append((s, half * P, P, "rkv"[g // 8], g % 8, g))
    tiles += [(12, 0, LORA, "wd", 0, 24), (12, LORA, LORA, "ad", 0, 25), (13, 0, P, "gd", 0, 26), (13, P, P, "gd", 1, 27)]
    for j, kind in enumerate(("cg", "cx", "cb")):
        tiles += [(14 + 2 * j + i // 2, (i % 2) * P, P, kind, i, 0) for i in range(4)]
    tiles += [(20 + s, 0, 256, "ft", (s, t), 0) for s in range(2) for t in range(2)]
    dst = {"r": st.r, "k": st.k, "v": st.v, "wd": st.wd, "ad": st.ad, "gd": st.gd}
    both = ("k", "v", "wd", "ad")
    s_acc, s_mid, s_free = st.sem("in1_acc"), st.sem("in1_centre_tap"), st.sem("in1_bank_free")
    slot_at = [first + s + sum(len(x) for x in IN1_MOD[:s]) for s in range(IN1_STEPS)]
    side = SideMod(nc, st, "in1", 0, [(slot_at[s] + 1 + j, c) for s in range(IN1_STEPS) for j, c in enumerate(IN1_MOD[s])],
                   st.carve(24064, 1024))

    def shapes(kind, i, width):
        segs = 2 if kind in both else 1
        out = dst[kind][0:width, i, :].rearrange("p (s t) -> p s t", s=segs)
        return segs, out

    with nc.Block() as block:
        @block.sync
        def _(sp):
            stream_weights(sp, st, first + count + lookahead)

        @block.tensor
        def _(pe):
            for m, (s, c0, width, kind, i, _) in enumerate(tiles):
                n = slot_at[s]
                arrived(pe, st, n)
                cols = SLOTS[n][4]
                w = ring_view(st, n, KT, cols)
                if m >= 4:
                    pe.wait_ge(s_free, m - 3)
                bank = st.psum[m % 4]
                for k in range(KT):
                    if kind == "ft":
                        t = i[1]
                        last = nc.tensor.matmul(bank[:, 0:256], st.hT[:, k, L + t * P:L + (t + 1) * P], w[:, k, :],
                                                start=k == 0, stop=k == KT - 1)
                    elif kind in both:
                        last = nc.tensor.matmul(bank[0:width, :], w[:, k, c0:c0 + width], st.hT[:, k, :],
                                                start=k == 0, stop=k == KT - 1)
                    else:
                        last = nc.tensor.matmul(bank[0:width, 0:T], w[:, k, c0:c0 + width], st.hT[:, k, L:TA],
                                                start=k == 0, stop=k == KT - 1)
                    if k == 0 and m and tiles[m - 1][0] != s and n - slot_at[s - 1] < RING:
                        last.then_inc(st.s_slot_used, 1)
                last.then_inc(s_acc, 1)
                if m + 1 < len(tiles) and tiles[m + 1][0] != s and slot_at[s + 1] - n == RING:
                    pe.wait_ge(s_acc, m + 1)
                    pe.sem_inc(st.s_slot_used, 1)
                side.columns(pe, n)
            pe.wait_ge(s_acc, len(tiles))
            pe.sem_inc(st.s_slot_used, 1)
            side.flush(pe)

        @block.scalar
        def _(act):
            for m, (s, c0, width, kind, i, row) in enumerate(tiles):
                if kind in dst:
                    act.wait_ge(s_acc, m + 1)
                    segs, out = shapes(kind, i, width)
                    src = st.psum[m % 4][0:width, 0:segs * 256].rearrange("p (s t) -> p s t", s=segs)
                    tap = col("rw_shift", RW_TILES + row)
                    nc.scalar.activation(out, src, ACT.Identity, scale=st.par[0:width, tap:tap + 1]).then_inc(s_mid, 1)

        @block.vector
        def _(dve):
            vl = st.vl
            vl.eng = dve
            mids = 0
            for m, (s, c0, width, kind, i, row) in enumerate(tiles):
                bank = st.psum[m % 4]
                if m == 0 or tiles[m - 1][0] != s:
                    side.accumulate(dve, slot_at[s] + 1 + len(IN1_MOD[s]))
                dve.wait_ge(s_acc, m + 1)
                if kind in dst:
                    mids += 1
                    dve.wait_ge(s_mid, mids)
                    segs, out = shapes(kind, i, width)
                    src = bank[0:width, 0:segs * 256].rearrange("p (s t) -> p s t", s=segs)
                    t0, t2 = col("rw_shift", row), col("rw_shift", 2 * RW_TILES + row)
                    vl(nc.vector.scalar_tensor_tensor(out[:, :, 1:], src[:, :, :-1], st.par[0:width, t0:t0 + 1],
                                                      out[:, :, 1:], ALU.mult, ALU.add))
                    nc.vector.scalar_tensor_tensor(out[:, :, :-1], src[:, :, 1:], st.par[0:width, t2:t2 + 1],
                                                   out[:, :, :-1], ALU.mult, ALU.add).then_inc(s_free, 1)
                elif kind == "cg":
                    nc.vector.tensor_copy(st.conv_u[:, i, :], bank[:, 0:T]).then_inc(s_free, 1)
                elif kind == "cx":
                    dve.wait_ge(s_free, m - 3)
                    nc.vector.tensor_tensor(st.conv_u[:, i, :], bank[:, 0:T], st.conv_u[:, i, :],
                                            ALU.mult).then_inc(s_free, 1)
                    dve.wait_ge(s_free, m + 1)
                    u = st.conv_u[:, i, :].rearrange("p (r t) -> p r t", t=GRID_W)
                    y = st.ycf[:, i, :].rearrange("p (r t) -> p r t", t=GRID_W)
                    tap = [st.par[:, col("conv_w", 4 * j + i):col("conv_w", 4 * j + i) + 1] for j in range(3)]
                    vl(nc.vector.tensor_scalar(y, u, tap[1], None, ALU.mult))
                    vl(nc.vector.scalar_tensor_tensor(y[:, :, 1:], u[:, :, :-1], tap[0], y[:, :, 1:], ALU.mult, ALU.add))
                    vl(nc.vector.scalar_tensor_tensor(y[:, :, :-1], u[:, :, 1:], tap[2], y[:, :, :-1], ALU.mult, ALU.add))
                elif kind == "cb":
                    nc.vector.tensor_tensor(st.ycf[:, i, :], bank[:, 0:T], st.ycf[:, i, :], ALU.mult).then_inc(s_free, 1)
                else:
                    s_, t = i
                    nc.vector.tensor_copy(st.ft[:, t, s_ * 256:(s_ + 1) * 256], bank[:, 0:256]).then_inc(s_free, 1)
            side.collect(dve)
            gain_columns(nc, st, 0, "norm_ffn", 64, 0, 2)


def fourier(nc, st):
    s_a, s_ev, s_b, s_done = (st.sem(f"ft_{x}") for x in ("seq", "seq_evac", "head", "head_evac"))
    with nc.Block() as block:
        @block.tensor
        def _(pe):
            dft = st.c("seq_dft").rearrange("p (k f t) -> p k (f t)", k=2, f=2)
            for j in range(4):
                for k in range(2):
                    last = nc.tensor.matmul(st.psum[j][:], st.ft[:, k, j * P:(j + 1) * P], dft[:, k, :],
                                            start=k == 0, stop=k == 1)
                last.then_inc(s_a, 1)
            hd = st.c("head_dft").rearrange("p (f c) -> p f c", f=2)
            for j in range(4):
                pe.wait_ge(s_ev, j + 1)
                for f in range(2):
                    last = nc.tensor.matmul(st.psum[4 + j][:, 0:T], hd[:, f, :], st.ftz[:, j, f, :], start=f == 0, stop=f == 1)
                last.then_inc(s_b, 1)

        @block.scalar
        def _(act):
            for j in range(4):
                act.wait_ge(s_a, j + 1)
                nc.scalar.copy(st.ftz[:, j, :, :], st.psum[j][:].rearrange("p (f t) -> p f t", f=2)).then_inc(s_ev, 1)

        @block.vector
        def _(dve):
            for j in range(4):
                dve.wait_ge(s_b, j + 1)
                nc.vector.tensor_copy(st.ycf[:, 4 + j, :], st.psum[4 + j][:, 0:T]).then_inc(s_done, 1)


def rwkv(nc, st):
    names = {}

    def S(name):
        if name not in names:
            names[name] = st.sem("rw_" + name)
        return names[name]

    c = st.c
    ring = st.ring
    use = {"ring": 0, "hT": 0, "mid": 0, "tail": 0}
    area = {"ring": (st.ring, 0, 12288), "hT": (st.work, 0, 8192), "mid": (st.work, 19968, 2048), "tail": (st.work, 24064, 5120)}

    def take(where, *shape):
        base, at, size = area[where]
        n = int(np.prod(shape))
        assert use[where] + n <= size, (where, use[where] + n, size)
        v = base[:, at + use[where]:at + use[where] + n]
        use[where] += n
        if len(shape) > 1:
            nm = "abcd"[:len(shape)]
            v = v.rearrange(f"p ({' '.join(nm)}) -> p {' '.join(nm)}", **dict(zip(nm, shape)))
        return v

    Bp, Kp = ([take("ring", TA) for _ in range(2)] for _ in range(2))
    BK = take("ring", 2, CPT, 4, CH)
    AR = [take("ring", NCH, 4, CH) for _ in range(2)]
    A = [take("ring", TA) for _ in range(2)]
    BKt = take("ring", 2, CPT, P)
    UV = take("ring", NCH, HD)
    Q = take("ring", 4, P)
    Pm, PT, Lm, WAX = (take("hT", 4, P) for _ in range(4))
    Loff = [take("hT", 4, P) for _ in range(2)]
    GM = take("hT", 4, 3, P)
    Vt = take("hT", TT, P)
    WXx = take("hT", 2, CPT, 2, CH)
    XA = take("hT", 4, 2, HD)
    SS, SD = take("hT", 2, HD), take("hT", 2, HD)
    ups = take("hT", 2, 2, P)
    lora_half = take("hT", 32)
    omka, DC = take("hT", NP1), take("hT", 2, NCH)
    bonus = take("hT", 2, 2)
    ytok, bv = take("mid", 2, D_RW), take("tail", 2, D_RW)
    t1, t2, t3, t4, t5, t6 = (take("tail", TA) for _ in range(6))
    if use["tail"] + 0 > 5120:
        raise ValueError
    st.ytok, st.bv = ytok, bv
    kk = take("hT", TA)
    am = t6
    lat = slice(L, TA)
    HS = [slice(h * HD, (h + 1) * HD) for h in range(2)]

    def tile_of(s, d):
        return s if d == 0 else s ^ 1

    def toks(tile):
        return slice(tile * P, (tile + 1) * P)

    with nc.Block() as block:
        @block.sync
        def _(sp):
            for hp in range(NP1):
                cs = slice(hp * P, (hp + 1) * P)
                if hp:
                    sp.wait_ge(S("lora_mm"), hp)
                for d in range(2):
                    sp.dma_start(ups[0:LORA, 0, d, :], st.dram["dec_up"][d, :, cs]).then_inc(S("ups_in"), 16)
                    sp.dma_start(ups[0:LORA, 1, d, :], st.dram["iclr_up"][d, :, cs]).then_inc(S("ups_in"), 16)
                sp.wait_ge(S("vtok"), hp + 1)
                if hp:
                    sp.wait_ge(S("mmB"), hp * 32)
                for h in range(2):
                    for q in range(CPT):
                        sp.dma_start(UV[64 + 32 * h:96 + 32 * h, :, :].rearrange("p (t c) i -> p t c i", c=CPT)[:, :, q, :],
                                     Vt[32 * q:32 * q + 32, :, HS[h]]).then_inc(S("vstack"), 16)

        @block.tensor
        def _(pe):
            W = lambda name, n: pe.wait_ge(S(name), n) if n > 0 else None
            mm, tr = nc.tensor.matmul, nc.tensor.transpose
            bank = st.psum
            I = c("ident")
            W("lora_act", 2)
            for hp in range(NP1):
                W("ups_in", 64 * (hp + 1))
                W("S_new", hp * 32)
                for j, x in enumerate((st.wd, st.ad)):
                    for d in range(2):
                        last = mm(bank[2 * j + d][:], ups[0:LORA, j, d, :], x[0:LORA, 0, :], start=True, stop=True)
                last.then_inc(S("lora_mm"), 1)
                W("k_squared", hp + 1)
                mm(bank[4][:], c("head_ones"), t1, start=True, stop=True).then_inc(S("k_sumsq"), 1)
                for t in range(TT):
                    last = tr(bank[5][:, toks(t)], st.v[:, hp, toks(t)], I)
                last.then_inc(S("vT"), 1)
                W("prod_ready", hp + 1)
                for t in range(2):
                    last = mm(bank[6][:, 2 * t:2 * t + 2], t5[:, toks(2 + t)], c("head_ones")[:, 0:P:HD], start=True, stop=True)
                last.then_inc(S("bonus_mm"), 1)
                W("operands", hp + 1)
                W("vtok", hp + 1)
                W("bonus_read", hp + 1)
                for s in range(4):
                    g = hp * 4 + s
                    tl = [tile_of(s, d) for d in range(2)]
                    is_lat = s >= 2
                    ch0 = [t * CPT for t in tl]
                    W("bk_placed", (g + 1) * 8)
                    for d in range(2):
                        for q in range(CPT):
                            last = tr(bank[d][:, q * P:(q + 1) * P], BK[:, d, q, :, :], I)
                        last.then_inc(S("bkT"), 1)
                    for d in range(2):
                        last = tr(bank[2][:, d * P:(d + 1) * P], A[d][:, toks(tl[d])], I)
                    last.then_inc(S("aT"), 1)
                    if s:
                        W("S_new", g * 8)
                        W("U_out", g * 8)
                        W("y_inter", (hp * 2 + max(0, s - 2)) * 8)
                    for d in range(2):
                        for h in range(2):
                            b = bank[4 + 2 * d + h]
                            for j, x in enumerate((Bp, Kp)):
                                lhs = x[d][HS[h], toks(tl[d])]
                                last = mm(b[:, 2 * j * P:(2 * j + 1) * P], lhs, A[d][HS[h], toks(tl[d])], start=True, stop=True)
                                if is_lat:
                                    last = mm(b[:, (2 * j + 1) * P:(2 * j + 2) * P], lhs,
                                              AR[d][HS[h], ch0[d]:ch0[d] + CPT, 2 + h, :], start=True, stop=True)
                            last.then_inc(S("gram"), 1)
                    W("aT_out", (g + 1) * 2)
                    for h in range(2):
                        for d in range(2):
                            last = mm(bank[3 - h][:, d * P:(d + 1) * P], A[d][HS[h], toks(tl[d])],
                                      Bp[d][HS[h], toks(tl[d])], start=True, stop=True)
                        last.then_inc(S("lgram"), 1)
                    W("gram_out", (g + 1) * 4)
                    W("bkT_out", (g + 1) * 2)
                    for d in range(2):
                        for h in range(2):
                            q = 2 * d + h
                            last = mm(bank[0][:, q * HD:(q + 1) * HD], GM[:, q, 1, :], Vt[:, tl[d], HS[h]], start=True, stop=True)
                    last.then_inc(S("x0"), 1)
                    for lv in range(4):
                        n = g * 4 + lv + 1
                        W("loff", n)
                        if lv == 0:
                            W("p_first", g + 1)
                            W("lgram_out", (g + 1) * 2)
                        else:
                            W("p_new", n - 1)
                        for q in range(4):
                            last = mm(bank[1][:, q * P:(q + 1) * P], Loff[lv % 2][:, q, :], Pm[:, q, :], start=True, stop=True)
                        last.then_inc(S("q_mm"), 1)
                        if lv == 0:
                            W("pt_first", g + 1)
                        else:
                            W("pt_new", g * 3 + lv)
                        W("q_out", n)
                        for q in range(4):
                            last = mm(bank[2][:, q * P:(q + 1) * P], PT[:, q, :], Q[:, q, :], start=True, stop=True)
                        last.then_inc(S("p_mm"), 1)
                        if lv < 3:
                            for q in range(4):
                                last = mm(bank[3][:, q * P:(q + 1) * P], Q[:, q, :], PT[:, q, :], start=True, stop=True)
                            last.then_inc(S("pt_mm"), 1)
                    W("p_new", (g + 1) * 4)
                    W("x0_out", (g + 1) * 2)
                    for q in range(4):
                        last = mm(bank[0][:, q * P:(q + 1) * P], Pm[:, q, :], XA[:, q, :, :], start=True, stop=True)
                    last.then_inc(S("wax"), 1)
                    W("wax_out", g + 1)
                    for q in range(4):
                        last = tr(bank[1][:, q * P:(q + 1) * P], WAX[:, q, :], I)
                    last.then_inc(S("waxT"), 1)
                    if is_lat:
                        for q in range(4):
                            d, h = q // 2, q % 2
                            last = mm(bank[2][HS[h], d * P:(d + 1) * P], WAX[:, q, HS[h]], GM[:, q, 0, :], start=True, stop=True)
                        last.then_inc(S("r_mm"), 1)
                        for q in range(4):
                            d, h = q // 2, q % 2
                            mm(bank[3][:, q * HD:(q + 1) * HD], GM[:, q, 0, :], WAX[:, q, HS[1 - h]], start=True, stop=False)
                            last = mm(bank[3][:, q * HD:(q + 1) * HD], GM[:, q, 2, :], Vt[:, tl[d], HS[h]], start=False, stop=True)
                        last.then_inc(S("yloc"), 1)
                    W("waxT_out", (g + 1) * 6)
                    if is_lat:
                        W("r_out", (hp * 2 + s - 1) * 4)
                        W("yloc_out", (hp * 2 + s - 1) * 2)
                    W("vstack", (hp + 1) * 128)
                    for q in range(CPT):
                        for d in range(2):
                            n = (g * CPT + q) * 2 + d + 1
                            cc = q if d == 0 else CPT - 1 - q
                            if n > 2:
                                W("S_new", n - 2)
                                W("U_out", n - 2)
                            if is_lat and (s > 2 or q > 0):
                                W("y_inter", (hp * 2 + s - 2) * 8 + q * 2 + d - 1)
                            ba = bank[4 + d]
                            if is_lat:
                                mm(ba[:, 0:HD], AR[d][:, ch0[d] + cc, :, :], SS[:, d, :], start=True, stop=True)
                            else:
                                mm(ba[0:64, 0:HD], AR[d][:, ch0[d] + cc, 0:2, :], SS[:, d, :], start=True, stop=True)
                            mm(ba[0:64, 0:HD], WXx[:, d, cc, :, :], c("ident64"), start=False, stop=True,
                               skip_group_check=True).then_inc(S("mmA"), 1)
                        for d in range(2):
                            n = (g * CPT + q) * 2 + d + 1
                            cc = q if d == 0 else CPT - 1 - q
                            W("U_out", n)
                            mm(bank[6 + d][:, 0:HD], BKt[:, d, cc, :], UV[:, ch0[d] + cc, :], start=True,
                               stop=True).then_inc(S("mmB"), 1)

        @block.scalar
        def _(act):
            W = lambda name, n: act.wait_ge(S(name), n) if n > 0 else None
            a_ = nc.scalar.activation
            bank = st.psum
            a_(st.wd[0:LORA], st.wd[0:LORA], ACT.Tanh).then_inc(S("lora_act"), 1)
            a_(st.gd, st.gd, ACT.Sigmoid).then_inc(S("lora_act"), 1)
            W("setup", 1)
            for hp in range(NP1):
                W("prep_free", hp)
                kk_col = st.par[:, col("k_k", hp):col("k_k", hp) + 1]
                a_(t1, st.k[:, hp, :], ACT.Square, scale=kk_col).then_inc(S("k_squared"), 1)
                W("k_sumsq", hp + 1)
                a_(t2, bank[4][:], ACT.Sqrt).then_inc(S("k_norm"), 1)
                W("vT", hp + 1)
                if hp:
                    W("vstack", hp * 128)
                nc.scalar.copy(Vt, bank[5][:].rearrange("p (t c) -> p t c", t=TT)).then_inc(S("vtok"), 1)
                W("lora_mm", hp + 1)
                W("kk_done", hp + 1)
                for d in range(2):
                    b = [lora_half[:, 16 * j + 8 * d + hp:16 * j + 8 * d + hp + 1] for j in range(2)]
                    if d:
                        W("dir_done", hp + 1)
                    a_(t1, bank[d][:], ACT.Tanh, scale=0.5, bias=b[0]).then_inc(S("decay_tanh"), 1)
                    a_(t6, bank[2 + d][:], ACT.Tanh, scale=0.5, bias=b[1]).then_inc(S("rate_tanh"), 1)
                    W("cums", 2 * hp + d + 1)
                    a_(t3, t3, ACT.Exp).then_inc(S("exps"), 1)
                    ends = t2.rearrange("p (n c) -> p n c", c=CH)[:, :, CH - 1]
                    a_(DC[:, d, :], ends, ACT.Exp).then_inc(S("exps"), 1)
                    a_(t1, t4, ACT.Exp, scale=-1.0).then_inc(S("exps"), 1)
                    W("exps", (2 * hp + d) * 4 + 3)
                    a_(t4, t4, ACT.Exp).then_inc(S("exps"), 1)
                W("bonus_mm", hp + 1)
                if hp:
                    W("bv_done", hp)
                nc.scalar.copy(bonus, bank[6][:, 0:4].rearrange("p (a b) -> p a b", a=2)).then_inc(S("bonus_read"), 1)
                for s in range(4):
                    g = hp * 4 + s
                    tl = [tile_of(s, d) for d in range(2)]
                    is_lat = s >= 2
                    ch0 = [t * CPT for t in tl]
                    for d in range(2):
                        W("bkT", g * 2 + d + 1)
                        nc.scalar.copy(BKt[:, d, :, :], bank[d][:].rearrange("p (a b) -> p a b", a=CPT)).then_inc(S("bkT_out"), 1)
                    W("aT", g + 1)
                    for h in range(2):
                        src = bank[2][:, 0:256].rearrange("p (d h j) -> p d h j", d=2, h=2)[:, :, h, :]
                        nc.scalar.copy(XA[:, h::2, h, :], src).then_inc(S("aT_out"), 1)
                    W("x0", g + 1)
                    for h in range(2):
                        src = bank[0][:, 0:256].rearrange("p (d h j) -> p d h j", d=2, h=2)[:, :, h, :]
                        nc.scalar.copy(XA[:, h::2, 1 - h, :], src).then_inc(S("x0_out"), 1)
                    for lv in range(4):
                        W("q_mm", g * 4 + lv + 1)
                        if lv:
                            W("pt_mm", g * 3 + lv)
                        nc.scalar.copy(Q, bank[1][:].rearrange("p (a b) -> p a b", a=4)).then_inc(S("q_out"), 1)
                    W("wax", g + 1)
                    nc.scalar.copy(WAX, bank[0][:].rearrange("p (a b) -> p a b", a=4)).then_inc(S("wax_out"), 1)
                    W("waxT", g + 1)
                    for h in range(2):
                        src = bank[1][HS[1 - h], :].rearrange("p (d h c t) -> p d h c t", d=2, h=2, c=CPT)[:, :, h, :, :]
                        nc.scalar.copy(WXx[HS[1 - h], :, :, h, :].rearrange("p d c t -> p (d c) t") if False else
                                       WXx[HS[1 - h], :, :, h, :], src).then_inc(S("waxT_out"), 1)
                    for d in range(2):
                        for h in range(2):
                            q = 2 * d + h
                            nc.scalar.copy(AR[d][HS[h], ch0[d]:ch0[d] + CPT, h, :],
                                           bank[1][HS[h], q * P:(q + 1) * P].rearrange("p (c t) -> p c t", c=CPT)
                                           ).then_inc(S("waxT_out"), 1)
                    for q in range(CPT):
                        for d in range(2):
                            n = (g * CPT + q) * 2 + d + 1
                            cc = q if d == 0 else CPT - 1 - q
                            W("mmA", n)
                            nc.scalar.copy(UV[0:64, ch0[d] + cc, :], bank[4 + d][0:64, 0:HD]).then_inc(S("U_out"), 1)
                        for d in range(2):
                            n = (g * CPT + q) * 2 + d + 1
                            cc = q if d == 0 else CPT - 1 - q
                            if n > 2:
                                W("S_new", n - 2)
                            gc = ch0[d] + cc
                            a_(SD[:, d, :], SS[:, d, :], ACT.Copy, scale=DC[:, d, gc:gc + 1]).then_inc(S("S_decayed"), 1)

        @block.gpsimd
        def _(pool):
            W = lambda name, n: pool.wait_ge(S(name), n) if n > 0 else None
            g_ = nc.gpsimd
            for x in [BK] + AR:
                g_.memset(x, 0.0).then_inc(S("zeroed"), 1)
            g_.memset(WXx, 0.0).then_inc(S("zeroed"), 1)
            lvl = c("levels").rearrange("p (l t) -> p l t", l=5)
            W("zeroed", 4)
            for hp in range(NP1):
                W("operands", hp + 1)
                for s in range(4):
                    g = hp * 4 + s
                    W("bkT", g * 2)
                    for h in range(2):
                        W("bk_placed", g * 8 + 4 * h) if h else W("loff", g * 4)
                        for d in range(2):
                            for j, x in enumerate((Bp, Kp)):
                                src = x[d][HS[h], toks(tile_of(s, d))].rearrange("p (c t) -> p c t", c=CPT)
                                g_.tensor_copy(BK[HS[h], d, :, 2 * j + h, :], src).then_inc(S("bk_placed"), 1)
                    W("bk_placed", (g + 1) * 8)
                    W("gram_out", (g + 1) * 4)
                    I4 = c("ident").unsqueeze(1).broadcast_to([P, 4, P])
                    g_.tensor_tensor(Pm, Pm, I4, ALU.add).then_inc(S("p_first"), 1)
                    W("lgram_out", (g + 1) * 2)
                    g_.tensor_tensor(PT, Lm, lvl[:, 0:1, :].broadcast_to([P, 4, P]), ALU.mult).then_inc(S("pt_mask"), 1)
                    W("pt_mask", g + 1)
                    g_.tensor_tensor(Loff[0], Lm, lvl[:, 1:2, :].broadcast_to([P, 4, P]), ALU.mult).then_inc(S("loff"), 1)
                    g_.tensor_tensor(PT, PT, I4, ALU.add).then_inc(S("pt_first"), 1)
                    for lv in range(1, 4):
                        if lv >= 2:
                            W("q_mm", g * 4 + lv - 1)
                        g_.tensor_tensor(Loff[lv % 2], Lm, lvl[:, lv + 1:lv + 2, :].broadcast_to([P, 4, P]),
                                         ALU.mult).then_inc(S("loff"), 1)

        @block.vector
        def _(dve):
            W = lambda name, n: dve.wait_ge(S(name), n) if n > 0 else None
            v_ = nc.vector
            vl = st.vl
            vl.eng = dve
            bank = st.psum
            for j, name in enumerate(("dec_w0", "iclr_a0")):
                vl.mark(v_.tensor_scalar(lora_half[:, 16 * j:16 * j + 16], st.par[:, col(name):col(name) + 16], 0.5, None, ALU.mult))
            vl.mark(v_.tensor_scalar(omka, st.par[:, col("k_a"):col("k_a") + 8], -1.0, 1.0, ALU.mult, ALU.add))
            vl.wait()
            v_.memset(SS, 0.0).then_inc(S("setup"), 1)
            W("setup", 1)
            W("zeroed", 4)
            carry = c("carry")
            for hp in range(NP1):
                k, r = st.k[:, hp, :], st.r[:, hp, :]
                pc = lambda name: st.par[:, col(name, hp):col(name, hp) + 1]
                W("k_norm", hp + 1)
                vl(v_.tensor_scalar(t2, t2, KK_EPS, None, ALU.max))
                vl(v_.reciprocal(t2, t2))
                v_.scalar_tensor_tensor(kk, k, pc("k_k"), t2, ALU.mult, ALU.mult).then_inc(S("kk_done"), 1)
                for d in range(2):
                    n = 2 * hp + d + 1
                    W("decay_tanh", n)
                    vl(v_.tensor_scalar(t1, t1, -DECAY / 2, -DECAY / 2, ALU.mult, ALU.add))
                    vl(v_.tensor_tensor_scan(t2, carry, t1, 0.0, ALU.mult, ALU.add))
                    v2 = lambda x: x.rearrange("p (n c) -> p n c", c=CH)
                    if d == 0:
                        vl(v_.tensor_copy(t4, t2))
                        v_.tensor_tensor(t3, t2, t1, ALU.subtract).then_inc(S("cums"), 1)
                    else:
                        tot = v2(t2)[:, :, CH - 1:CH].broadcast_to([P, NCH, CH])
                        vl(v_.tensor_tensor(v2(t3), tot, v2(t2), ALU.subtract))
                        v_.tensor_tensor(t4, t3, t1, ALU.add).then_inc(S("cums"), 1)
                    W("rate_tanh", n)
                    vl(v_.tensor_scalar(am, t6, 0.5, 0.5, ALU.mult, ALU.add))
                    W("exps", 4 * (n - 1) + 2)
                    vl(v_.tensor_scalar(t2, am, pc("k_a"), omka[:, hp:hp + 1], ALU.mult, ALU.add))
                    vl(v_.tensor_tensor(t2, t2, k, ALU.mult))
                    if d == 0:
                        vl(v_.tensor_copy(t5, t2))
                    else:
                        vl(v_.tensor_tensor(t5, t5, t2, ALU.add))
                    vl(v_.tensor_tensor(am, am, kk, ALU.mult))
                    vl(v_.scalar_tensor_tensor(A[d], kk, -1.0, t3, ALU.mult, ALU.mult))
                    W("exps", 4 * n - 1)
                    vl.mark(v_.tensor_tensor(Bp[d], am, t1, ALU.mult))
                    vl.mark(v_.tensor_tensor(Kp[d], t2, t1, ALU.mult))
                    W("exps", 4 * n)
                    for h in range(2):
                        vl.mark(v_.tensor_tensor(AR[d][HS[h], NCH // 2:, 2 + h, :], r.rearrange("p (n c) -> p n c", c=CH)[HS[h]],
                                                 v2(t4)[HS[h], NCH // 2:, :], ALU.mult))
                    vl.wait()
                    if d == 1:
                        v_.scalar_tensor_tensor(t5[:, lat], t5[:, lat], pc("r_k"), r, ALU.mult, ALU.mult).then_inc(S("prod_ready"), 1)
                        W("prod_ready", hp + 1)
                        v_.memset(SS, 0.0).then_inc(S("operands"), 1)
                        W("operands", hp + 1)
                    else:
                        vl(v_.tensor_scalar(st.eps[:, 0:1], st.eps[:, 0:1], 1.0, None, ALU.mult)) if False else None
                        dve.sem_inc(S("dir_done"), 1)
                W("bonus_read", hp + 1)
                for t in range(2):
                    for h in range(2):
                        at = hp * P + h * HD
                        ins = v_.tensor_scalar(bv[:, t, at:at + HD], Vt[:, 2 + t, HS[h]], bonus[:, t, h:h + 1], None, ALU.mult)
                        ins.then_inc(S("bv_done"), 1) if (t, h) == (1, 1) else vl.mark(ins)
                for s in range(4):
                    g = hp * 4 + s
                    tl = [tile_of(s, d) for d in range(2)]
                    is_lat = s >= 2
                    ch0 = [t * CPT for t in tl]
                    lvl1 = c("level1").rearrange("p (d t) -> p d t", d=2)
                    strict = c("strict").rearrange("p (d t) -> p d t", d=2)
                    m3 = c("mask3").rearrange("p (d m t) -> p d m t", d=2, m=3)
                    for d in range(2):
                        for h in range(2):
                            q = 2 * d + h
                            W("gram", g * 4 + q + 1)
                            b = bank[4 + q][:].rearrange("p (m t) -> p m t", m=4)
                            vl.mark(v_.tensor_tensor(Pm[:, q, :], b[:, 0, :], lvl1[:, d, :], ALU.mult))
                            if is_lat:
                                v_.tensor_tensor(GM[:, q, :, :], b[:, 1:4, :], m3[:, d, :, :], ALU.mult).then_inc(S("gram_out"), 1)
                            else:
                                v_.tensor_tensor(GM[:, q, 1, :], b[:, 2, :], m3[:, d, 1, :], ALU.mult).then_inc(S("gram_out"), 1)
                    for h in range(2):
                        W("lgram", g * 2 + h + 1)
                        b = bank[3 - h][:, 0:256].rearrange("p (d t) -> p d t", d=2)
                        v_.tensor_tensor(Lm[:, h::2, :], b, strict[:, ::-1, :] if False else c("strict_ts").rearrange(
                            "p (d t) -> p d t", d=2), ALU.mult).then_inc(S("lgram_out"), 1)
                    for lv in range(4):
                        W("p_mm", g * 4 + lv + 1)
                        W("p_first", g + 1)
                        v_.tensor_tensor(Pm, bank[2][:].rearrange("p (a b) -> p a b", a=4), Pm, ALU.add).then_inc(S("p_new"), 1)
                        if lv < 3:
                            W("pt_mm", g * 3 + lv + 1)
                            v_.tensor_tensor(PT, bank[3][:].rearrange("p (a b) -> p a b", a=4), PT, ALU.add).then_inc(S("pt_new"), 1)
                    if is_lat:
                        W("r_mm", hp * 2 + s - 1)
                        for d in range(2):
                            for h in range(2):
                                x = AR[d][HS[h], ch0[d]:ch0[d] + CPT, 2 + h, :]
                                v_.tensor_tensor(x, bank[2][HS[h], d * P:(d + 1) * P].rearrange("p (c t) -> p c t", c=CPT), x,
                                                 ALU.add).then_inc(S("r_out"), 1)
                        W("yloc", hp * 2 + s - 1)
                        for d in range(2):
                            y = ytok[:, tl[d] - 2, hp * P:(hp + 1) * P]
                            src = bank[3][:, d * P:(d + 1) * P]
                            if s == 2:
                                v_.tensor_copy(y, src).then_inc(S("yloc_out"), 1)
                            else:
                                W("y_inter", (hp * 2 + 1) * 8)
                                v_.tensor_tensor(y, src, y, ALU.add).then_inc(S("yloc_out"), 1)
                        W("yloc_out", (hp * 2 + s - 1) * 2)
                    for q in range(CPT):
                        if is_lat:
                            for d in range(2):
                                n = (g * CPT + q) * 2 + d + 1
                                cc = q if d == 0 else CPT - 1 - q
                                W("mmA", n)
                                for h in range(2):
                                    y = ytok[CH * cc:CH * cc + CH, tl[d] - 2, hp * P + h * HD:hp * P + (h + 1) * HD]
                                    ins = v_.tensor_tensor(y, bank[4 + d][64 + CH * h:96 + CH * h, 0:HD], y, ALU.add)
                                    ins.then_inc(S("y_inter"), 1) if h else vl.mark(ins)
                        for d in range(2):
                            n = (g * CPT + q) * 2 + d + 1
                            cc = q if d == 0 else CPT - 1 - q
                            W("mmB", n)
                            W("S_decayed", n)
                            gc = ch0[d] + cc
                            v_.scalar_tensor_tensor(SS[:, d, :], bank[6 + d][:, 0:HD], DC[:, d, gc:gc + 1], SD[:, d, :],
                                                    ALU.mult, ALU.add).then_inc(S("S_new"), 1)
                W("S_new", (hp + 1) * 32)
                v_.tensor_copy(SD, SS).then_inc(S("prep_free"), 1)


def rwkv_out(nc, st):
    gup, ln = st.carve(0, 2, D_RW), st.carve(2048, 2, D_RW)
    sq, stat = st.carve(4096, 2, D_RW), st.carve(8192, 3, 32)
    yr = st.yr
    s_in, s_g, s_st, s_y, s_T, s_ev, s_sq = (st.sem(f"rwo_{x}") for x in (
        "weights_in", "gate", "root", "y_ready", "transposed", "evac", "squared"))
    y, bv = st.ytok, st.bv
    heads = lambda x: x.rearrange("p t (h i) -> p (t h) i", i=HD)
    with nc.Block() as block:
        @block.sync
        def _(sp):
            sp.dma_start(gup, st.dram["g_up"].rearrange("(k p) n -> p k n", p=P)).then_inc(s_in, 16)
            for j, name in enumerate(("ln_w", "ln_b")):
                sp.dma_start(ln[:, j, :], st.dram[name].rearrange("(a c) -> a c", a=1).partition_broadcast(P)).then_inc(s_in, 16)
            first, _ = SPANS["out1"]
            stream_weights(sp, st, first + RING)

        @block.tensor
        def _(pe):
            pe.wait_ge(s_in, 48)
            for t in range(2):
                for n in range(2):
                    for k in range(2):
                        last = nc.tensor.matmul(st.psum[2 * t + n][:], st.gd[:, k, t * P:(t + 1) * P],
                                                gup[:, k, n * 512:(n + 1) * 512], start=k == 0, stop=k == 1)
                    last.then_inc(s_g, 1)
            pe.wait_ge(s_y, 4)
            for j in range(4):
                for i in range(2):
                    for t in range(2):
                        last = nc.tensor.transpose(st.psum[4 + j][:, (2 * i + t) * P:(2 * i + t + 1) * P],
                                                   y[:, t, (2 * j + i) * P:(2 * j + i + 1) * P], st.c("ident"))
                last.then_inc(s_T, 1)

        @block.scalar
        def _(act):
            act.wait_ge(s_st, 1)
            nc.scalar.activation(sq, y, ACT.Square).then_inc(s_sq, 1)
            act.wait_ge(s_st, 2)
            nc.scalar.activation(stat[:, 1, :], stat[:, 1, :], ACT.Sqrt, scale=1.0 / HD, bias=st.eps[:, 1:2]).then_inc(s_sq, 1)

        @block.vector
        def _(dve):
            vl = st.vl
            vl.eng = dve
            yh = heads(y)
            one = lambda j: stat[:, j, :].unsqueeze(2).broadcast_to([P, 32, HD])
            vl(nc.vector.tensor_reduce(stat[:, 0, :], yh, AX.X, ALU.add))
            vl(nc.vector.tensor_scalar(stat[:, 0, :], stat[:, 0, :], 1.0 / HD, None, ALU.mult))
            nc.vector.tensor_tensor(yh, yh, one(0), ALU.subtract).then_inc(s_st, 1)
            dve.wait_ge(s_sq, 1)
            nc.vector.tensor_reduce(stat[:, 1, :], heads(sq), AX.X, ALU.add).then_inc(s_st, 1)
            dve.wait_ge(s_sq, 2)
            vl(nc.vector.reciprocal(stat[:, 1, :], stat[:, 1, :]))
            vl(nc.vector.tensor_tensor(yh, yh, one(1), ALU.mult))
            dve.wait_ge(s_in, 48)
            vl(nc.vector.tensor_tensor(y, y, ln[:, 0:1, :].broadcast_to([P, 2, D_RW]), ALU.mult))
            vl(nc.vector.tensor_tensor(y, y, ln[:, 1:2, :].broadcast_to([P, 2, D_RW]), ALU.add))
            vl(nc.vector.tensor_tensor(y, y, bv, ALU.add))
            for t in range(2):
                for n in range(2):
                    dve.wait_ge(s_g, 2 * t + n + 1)
                    part = y[:, t, n * 512:(n + 1) * 512]
                    nc.vector.tensor_tensor(part, st.psum[2 * t + n][:], part, ALU.mult).then_inc(s_y, 1)
            for j in range(4):
                dve.wait_ge(s_T, j + 1)
                nc.vector.tensor_copy(yr[:, 2 * j:2 * j + 2, :], st.psum[4 + j][:].rearrange("p (a b) -> p a b", a=2)
                                      ).then_inc(s_ev, 1)


def units(eng, count, slots, body):
    per = RING // math.gcd(RING, slots)
    turns = count // per
    done = 0
    if turns > 1:
        with eng.Fori(0, turns) as i:
            for u in range(per):
                body(u, i, per)
        done = turns * per
    for u in range(done, count):
        body(u, 0, 0)


class Residual:

    def __init__(self, nc, st, name, gate):
        self.nc, self.st, self.gate = nc, st, gate
        self.s_even, self.s_free = st.sem(f"{name}_even_tile"), st.sem(f"{name}_bank_free")

    def credit(self, dve):
        dve.sem_inc(self.s_free, 2)

    def bank_free(self, pe, u, half, i=0, per=0):
        pe.wait_ge(self.s_free, i * (2 * per) + 2 * u + half + 1)

    def add(self, dve, u, half, slot, i=0, per=0, slots=1):
        nc, st = self.nc, self.st
        if half == 0:
            dve.wait_ge(self.s_even, i * per + u + 1)
        else:
            dve.wait_ge(st.s_slot_used, i * (per * slots) + use_count(slot))
        m = i * (2 * per) + (2 * u + half)
        x = st.xT[:, bass.ds(m, 1), :] if per else st.xT[:, m:m + 1, :]
        g = self.gate[:, bass.ds(m, 1)] if per else self.gate[:, m:m + 1]
        nc.vector.scalar_tensor_tensor(x, st.psum[half][:, 0:T].unsqueeze(1), g, x, ALU.mult, ALU.add).then_inc(self.s_free, 1)


def out_projection(nc, st, name, which, rhs, mods):
    first, count = SPANS[name]
    res = Residual(nc, st, name, st.mod[which][:, 0, 32:48])
    at = [first + s * (2 if mods else 1) for s in range(8)]
    side = SideMod(nc, st, name, which, [(at[s] + 1, c) for s, c in enumerate(mods)], st.carve(24064, 1024)) if mods else None
    with nc.Block() as block:
        @block.sync
        def _(sp):
            stream_weights(sp, st, first + count + RING)

        @block.tensor
        def _(pe):
            for s in range(8):
                arrived(pe, st, at[s])
                w = ring_view(st, at[s], KT, 256)
                for half in range(2):
                    res.bank_free(pe, s, half)
                    for k in range(KT):
                        last = nc.tensor.matmul(st.psum[half][:, 0:T], w[:, k, half * P:(half + 1) * P], rhs(k),
                                                start=k == 0, stop=k == KT - 1)
                    last.then_inc(st.s_slot_used if half else res.s_even, 1)
                    if mods and half == 0:
                        side.columns(pe, at[s])
            if mods:
                side.flush(pe)

        @block.vector
        def _(dve):
            res.credit(dve)
            for s in range(8):
                if mods:
                    side.accumulate(dve, at[s] + 2)
                for half in range(2):
                    res.add(dve, s, half, at[s])
            if mods:
                st.vl.eng = dve
                side.collect(dve)


def ffn_up(nc, st, name, mod_at):
    first, count = SPANS[name]
    slots = 2 + (mod_at is not None)
    n_units = count // slots
    s_even, s_silu, s_free, s_mac, s_col, s_rawfree = (st.sem(f"{name}_{x}") for x in (
        "even_tile", "silu", "bank_free", "mod_step", "mod_columns", "mod_bank_free"))
    h, G, tmp = st.h, st.G, st.gate_tmp
    partial, sums = st.carve(24064, 4, SLOT_COLS), st.carve(25088, 2, SLOT_COLS)

    def tile_done(eng, u, half, i, per):
        if half == 0:
            eng.wait_ge(s_even, i * per + u + 1)
        else:
            eng.wait_ge(st.s_slot_used, i * (2 * per) + use_count(first) + 2 * u + 1)

    with nc.Block() as block:
        @block.sync
        def _(sp):
            stream_weights(sp, st, first + count + RING)

        @block.tensor
        def _(pe):
            def unit(u, i, per):
                n = first + u * slots
                for half in range(2):
                    pe.wait_ge(s_free, i * (2 * per) + 2 * u + half + 1)
                    for j in range(2):
                        if half == 0:
                            arrived(pe, st, n + j, i, per * slots)
                        w = ring_view(st, n + j, KT, 256)
                        for k in range(KT):
                            last = nc.tensor.matmul(st.psum[half][:, j * T:(j + 1) * T], w[:, k, half * P:(half + 1) * P],
                                                    h[:, k, :], start=k == 0, stop=k == KT - 1)
                        if half:
                            last.then_inc(st.s_slot_used, 1)
                    if half == 0:
                        last.then_inc(s_even, 1)
                if mod_at is not None:
                    pe.wait_ge(s_rawfree, i * per + u + 1)
                    pe.wait_ge(st.s_mod_used, i * per + use_count(first + 2) + u)
                    mod_sums(nc, st, sums, 2, 0, s_col)
            units(pe, n_units, slots, unit)

        @block.scalar
        def _(act):
            def unit(u, i, per):
                for half in range(2):
                    tile_done(act, u, half, i, per)
                    act.wait_ge(s_free, i * (2 * per) + 2 * u + half + 1)
                    nc.scalar.activation(tmp[:, half, :], st.psum[half][:, 0:T], ACT.Silu).then_inc(s_silu, 1)
            units(act, n_units, slots, unit)

        @block.vector
        def _(dve):
            dve.sem_inc(s_free, 2)
            if mod_at is not None:
                dve.sem_inc(s_rawfree, 1)

            def unit(u, i, per):
                if mod_at is not None:
                    mod_macs(dve, st, first + slots * u + 2, 1, 2, (partial, sums), s_mac,
                             i * (per * mac_steps(2)) + u * mac_steps(2), s_col, None, i, per * slots)
                for half in range(2):
                    dve.wait_ge(s_silu, i * (2 * per) + 2 * u + half + 1)
                    m = i * (2 * per) + (2 * u + half)
                    out = G[:, bass.ds(m, 1), :] if per else G[:, m:m + 1, :]
                    nc.vector.tensor_tensor(out, tmp[:, half:half + 1, :], st.psum[half][:, T:2 * T].unsqueeze(1),
                                            ALU.mult).then_inc(s_free, 1)
                if mod_at is not None:
                    dve.wait_ge(s_col, i * per + u + 1)
                    at = i * (4 * per) + 4 * (mod_at + u)
                    dst = st.modraw[1][:, bass.ds(at, 4)] if per else st.modraw[1][:, at:at + 4]
                    nc.vector.tensor_copy(dst, st.psum[7][:, 0:4]).then_inc(s_rawfree, 1)
            units(dve, n_units, slots, unit)
            if mod_at is not None:
                st.vl.eng = dve
                dve.wait_ge(s_rawfree, n_units + 1)
                mod_columns(nc, st, 1, slice(0, 32), 2)
                mod_columns(nc, st, 1, slice(32, 2 * (mod_at + n_units)), 1)
                gain_columns(nc, st, 1, "norm_mix_g_2", 16, 0, 0)
                gain_columns(nc, st, 1, "norm_mix_g_2", 16, 1, 1)


def ffn_down(nc, st, name, which):
    first, count = SPANS[name]
    slots = 4
    n_units = count // slots
    res = Residual(nc, st, name, st.mod[which][:, 0, 80:96])
    with nc.Block() as block:
        @block.sync
        def _(sp):
            stream_weights(sp, st, min(first + count + RING, len(SLOTS)))

        @block.tensor
        def _(pe):
            def unit(u, i, per):
                n = first + u * slots
                for s in range(4):
                    arrived(pe, st, n + s, i, per * slots)
                    w = ring_view(st, n + s, DOWN_K, 256)
                    for half in range(2):
                        if s == 0:
                            res.bank_free(pe, u, half, i, per)
                        for k in range(DOWN_K):
                            last = nc.tensor.matmul(st.psum[half][:, 0:T], w[:, k, half * P:(half + 1) * P],
                                                    st.G[:, s * DOWN_K + k, :], start=s == 0 and k == 0,
                                                    stop=s == 3 and k == DOWN_K - 1)
                        if s == 3 and half == 0:
                            last.then_inc(res.s_even, 1)
                    last.then_inc(st.s_slot_used, 1)
            units(pe, n_units, slots, unit)

        @block.vector
        def _(dve):
            res.credit(dve)

            def unit(u, i, per):
                for half in range(2):
                    res.add(dve, u, half, first + u * slots + 3, i, per, slots)
            units(dve, n_units, slots, unit)


def load_context2(nc, st):
    tok = st.carve(8192, 2, DM)
    s_in, s_T, s_ev = st.sem("ctx2_in"), st.sem("ctx2_transposed"), st.sem("ctx2_evac")
    with nc.Block() as block:
        @block.scalar
        def _(act):
            act.dma_start(tok, st.dram["ctx_2"].rearrange("(t p) c -> p t c", p=P)).then_inc(s_in, 16)

        @block.tensor
        def _(pe):
            pe.wait_ge(s_in, 16)
            for m in range(KT // 2):
                if m >= 4:
                    pe.wait_ge(s_ev, m - 3)
                for j in range(4):
                    k, t = 2 * m + j // 2, j % 2
                    last = nc.tensor.transpose(st.psum[m % 4][:, j * P:(j + 1) * P], tok[:, t, k * P:(k + 1) * P], st.c("ident"))
                last.then_inc(s_T, 1)

        @block.vector
        def _(dve):
            for m in range(KT // 2):
                dve.wait_ge(s_T, m + 1)
                nc.vector.tensor_copy(st.hT[:, 2 * m:2 * m + 2, 0:L], st.psum[m % 4][:].rearrange("p (a b) -> p a b", a=2)
                                      ).then_inc(s_ev, 1)


def in_projection2(nc, st):
    first, count = SPANS["in2"]
    dst = (("q", st.q2, 0), ("f", st.f2[0], 1), ("f", st.f2[1], 1), ("i", st.i2, 2), ("g", st.g2, 0), ("aq", st.aq, 0))
    s_acc, s_free = st.sem("in2_acc"), st.sem("in2_bank_free")
    side = SideMod(nc, st, "in2", 1, [(first + 2 * s + 1, IN2_MOD + s) for s in range(IN2_STEPS)], st.c("seq_dft"))
    jobs = []
    for s in range(26):
        if s < 24:
            _, x, kind = dst[s // 4]
            j = 2 * (s % 4)
        else:
            x, kind, j = (st.ak, 1, 0) if s == 24 else (st.av, 2, 0)
        if kind == 2:
            jobs += [(s, "tok", t, x[:, t, j * P:j * P + 256]) for t in range(TT)]
        else:
            jobs += [(s, ("lat", "both")[kind], h, x[:, j + h, :]) for h in range(2)]
    with nc.Block() as block:
        @block.sync
        def _(sp):
            stream_weights(sp, st, first + count + RING)

        @block.tensor
        def _(pe):
            for m, (s, kind, j, _) in enumerate(jobs):
                n = first + 2 * s
                arrived(pe, st, n)
                w = ring_view(st, n, KT, 256)
                if m >= 4:
                    pe.wait_ge(s_free, m - 3)
                bank = st.psum[m % 4]
                for k in range(KT):
                    if kind == "tok":
                        last = nc.tensor.matmul(bank[:, 0:256], st.hT[:, k, j * P:(j + 1) * P], w[:, k, :],
                                                start=k == 0, stop=k == KT - 1)
                    elif kind == "both":
                        last = nc.tensor.matmul(bank[:], w[:, k, j * P:(j + 1) * P], st.hT[:, k, :], start=k == 0, stop=k == KT - 1)
                    else:
                        last = nc.tensor.matmul(bank[:, 0:T], w[:, k, j * P:(j + 1) * P], st.hT[:, k, L:TA],
                                                start=k == 0, stop=k == KT - 1)
                    if k == 0 and m and jobs[m - 1][0] != s:
                        last.then_inc(st.s_slot_used, 1)
                last.then_inc(s_acc, 1)
                side.columns(pe, n)
            pe.wait_ge(s_acc, len(jobs))
            pe.sem_inc(st.s_slot_used, 1)
            side.flush(pe)

        @block.vector
        def _(dve):
            for m, (s, kind, j, x) in enumerate(jobs):
                if m == 0 or jobs[m - 1][0] != s:
                    side.accumulate(dve, first + 2 * s + 2)
                dve.wait_ge(s_acc, m + 1)
                n = 512 if kind == "both" else 256
                nc.vector.tensor_copy(x, st.psum[m % 4][:, 0:n]).then_inc(s_free, 1)
            st.vl.eng = dve
            side.collect(dve)
            gain_columns(nc, st, 1, "norm_ffn_g_2", 64, 0, 2)


def hgrn(nc, st):
    names = {}

    def S(name):
        if name not in names:
            names[name] = st.sem("hg_" + name)
        return names[name]

    at = 4096
    def take(*shape):
        nonlocal at
        v = st.carve(at, *shape)
        at += int(np.prod(shape))
        assert at <= 8192
        return v

    cum, b, te, kk = take(TA), take(TA), take(TA), take(TA)
    eb, enb = take(T), take(T)
    keT = take(TT, P)
    scT = take(2, P)
    states = st.ctx_states = take(6, P)
    lbs = st.carve(28672, 4, 16)
    D = st.carve(28736, NCH)
    y = st.y2
    latt = slice(L, TA)
    v2 = lambda x: x.rearrange("p (n c) -> p n c", c=CH)
    base = col("hg_lb_2")

    def chunk(d, n):
        if d == 0:
            return n
        return 7 - n if n < 8 else 23 - n

    with nc.Block() as block:
        @block.scalar
        def _(act):
            W = lambda name, n: act.wait_ge(S(name), n) if n > 0 else None
            a_ = nc.scalar.activation
            W("lb_centred", 1)
            a_(lbs[:, 0:2, :], lbs[:, 0:2, :], ACT.Exp).then_inc(S("lb_exp"), 1)
            a_(st.q2, st.q2, ACT.Silu).then_inc(S("q_silu"), 1)
            for u in range(16):
                h, d = u // 2, u % 2
                f = st.f2[d][:, h, :]
                a_(f, f, ACT.Exp, scale=-1.0).then_inc(S("pre_exp"), 1)
                W("f_ready", u + 1)
                a_(te, f, ACT.Ln).then_inc(S("logf"), 1)
                W("sums", u + 1)
                a_(eb, b[:, latt], ACT.Exp).then_inc(S("exps"), 1)
                a_(enb, b[:, latt], ACT.Exp, scale=-1.0).then_inc(S("exps"), 1)
                a_(D, v2(cum)[:, :, CH - 1], ACT.Exp).then_inc(S("exps"), 1)
                a_(te, te, ACT.Exp).then_inc(S("exps"), 1)
                W("keT", u + 1)
                nc.scalar.copy(keT, st.psum[4][:].rearrange("p (a b) -> p a b", a=TT)).then_inc(S("keT_out"), 1)
                if d:
                    W("o_done", h + 1)
                    nc.scalar.copy(y[:, h, :], st.psum[6 + h % 2][:, 0:T]).then_inc(S("o_out"), 1)

        @block.tensor
        def _(pe):
            W = lambda name, n: pe.wait_ge(S(name), n) if n > 0 else None
            mm = nc.tensor.matmul
            for u in range(16):
                h, d = u // 2, u % 2
                W("kend", u + 1)
                W("keT_out", u)
                for t in range(TT):
                    last = nc.tensor.transpose(st.psum[4][:, t * P:(t + 1) * P], kk[:, t * P:(t + 1) * P], st.c("ident"))
                last.then_inc(S("keT"), 1)
                W("qk", u + 1)
                for t in range(2):
                    last = mm(st.psum[5][:, t * P:(t + 1) * P], enb[:, t * P:(t + 1) * P], eb[:, t * P:(t + 1) * P],
                              start=True, stop=True)
                last.then_inc(S("scores"), 1)
                W("keT_out", u + 1)
                W("state", 16 * u)
                for q in range(CPT):
                    rows = slice(CH * q, CH * q + CH)
                    for t in range(TT):
                        last = mm(st.psum[q][:, t * P:(t + 1) * P], keT[rows, t, :], st.i2[rows, t, h * P:(h + 1) * P],
                                  start=True, stop=True)
                last.then_inc(S("kv"), 1)
                W("scores_out", u + 1)
                if d == 0:
                    W("o_out", h - 1)
                o = st.psum[6 + h % 2]
                for t in range(2):
                    mm(o[:, t * P:(t + 1) * P], st.i2[:, 2 + t, h * P:(h + 1) * P], scT[:, t, :],
                       start=d == 0 and t == 0, stop=False, skip_group_check=True)
                for n in range(8, 16):
                    W("state", 16 * u + n)
                    cl = chunk(d, n) - 8
                    last = mm(o[:, cl * CH:(cl + 1) * CH], states[:, 2 + n % 4, :], eb[:, cl * CH:(cl + 1) * CH],
                              start=False, stop=d == 1 and n == 15, skip_group_check=True)
                    last.then_inc(S("inter"), 1)
                if d:
                    W("inter", 8 * (u + 1))
                    pe.sem_inc(S("o_done"), 1)

        @block.vector
        def _(dve):
            W = lambda name, n: dve.wait_ge(S(name), n) if n > 0 else None
            v_ = nc.vector
            vl = st.vl
            vl.eng = dve
            b0, b1 = st.par[:, base:base + 16], st.par[:, base + 16:base + 32]
            vl(v_.tensor_tensor(lbs[:, 2, :], b0, b1, ALU.max))
            vl.mark(v_.tensor_tensor(lbs[:, 0, :], b0, lbs[:, 2, :], ALU.subtract))
            v_.tensor_tensor(lbs[:, 1, :], b1, lbs[:, 2, :], ALU.subtract).then_inc(S("lb_centred"), 1)
            W("lb_exp", 1)
            vl(v_.tensor_tensor(lbs[:, 3, :], lbs[:, 0, :], lbs[:, 1, :], ALU.add))
            vl(v_.reciprocal(lbs[:, 3, :], lbs[:, 3, :]))
            vl(v_.tensor_tensor(lbs[:, 2, :], lbs[:, 0, :], lbs[:, 3, :], ALU.mult))
            vl(v_.tensor_scalar(lbs[:, 3, :], lbs[:, 2, :], -1.0, 1.0, ALU.mult, ALU.add))
            W("q_silu", 1)
            incl = c_incl = st.c("mask3").rearrange("p (d m t) -> p d m t", d=2, m=3)[:, :, 0, :]
            for u in range(16):
                h, d = u // 2, u % 2
                f = st.f2[d][:, h, :]
                lc = 8 * d + h
                W("pre_exp", u + 1)
                vl(v_.tensor_scalar(f, f, 1.0, None, ALU.add))
                vl(v_.reciprocal(f, f))
                v_.tensor_scalar(f, f, lbs[:, 3, lc:lc + 1], lbs[:, 2, lc:lc + 1], ALU.mult, ALU.add).then_inc(S("f_ready"), 1)
                W("f_ready", u + 1)
                W("logf", u + 1)
                vl(v_.tensor_tensor_scan(cum, st.c("carry"), te, 0.0, ALU.mult, ALU.add))
                tot = v2(cum)[:, :, CH - 1:CH].broadcast_to([P, NCH, CH])
                if d == 0:
                    vl.mark(v_.tensor_copy(b, cum))
                    v_.tensor_tensor(v2(te), tot, v2(cum), ALU.subtract).then_inc(S("sums"), 1)
                else:
                    vl(v_.tensor_tensor(v2(b), tot, v2(cum), ALU.subtract))
                    vl(v_.tensor_tensor(b, b, te, ALU.add))
                    v_.tensor_tensor(v2(te), tot, v2(b), ALU.subtract).then_inc(S("sums"), 1)
                W("keT", u)
                vl(v_.tensor_scalar(f, f, -1.0, 1.0, ALU.mult, ALU.add))
                W("exps", 4 * u + 2)
                vl.mark(v_.tensor_tensor(enb, enb, f[:, latt], ALU.mult))
                v_.tensor_tensor(eb, eb, st.q2[:, h, :], ALU.mult).then_inc(S("qk"), 1)
                W("exps", 4 * u + 4)
                v_.tensor_tensor(kk, f, te, ALU.mult).then_inc(S("kend"), 1)
                W("scores", u + 1)
                m = incl[:, d:d + 1, :].broadcast_to([P, 2, P])
                if u:
                    W("inter", 8 * u)
                v_.tensor_tensor(scT, st.psum[5][:, 0:256].rearrange("p (t c) -> p t c", t=2), m, ALU.mult).then_inc(S("scores_out"), 1)
                W("kv", u + 1)
                for n in range(16):
                    g = chunk(d, n)
                    kv = st.psum[g % CPT][:, (g // CPT) * P:(g // CPT + 1) * P]
                    where = lambda j: states[:, j % 2, :] if j < 8 else states[:, 2 + j % 4, :]
                    if n >= 11:
                        W("inter", 8 * u + n - 10)
                    if n == 15:
                        v_.tensor_copy(states[:, 0, :], kv).then_inc(S("state"), 1)
                        W("state", 16 * (u + 1))
                    elif n == 0:
                        v_.tensor_copy(where(1), kv).then_inc(S("state"), 1)
                        W("state", 16 * u + 1)
                    else:
                        v_.scalar_tensor_tensor(where(n + 1), where(n), D[:, g:g + 1], kv, ALU.mult, ALU.add).then_inc(S("state"), 1)
                        W("state", 16 * u + n + 1)
                W("inter", 8 * (u + 1))


def readout_and_rope(nc, st):
    s_sq, s_ms, s_rt, s_fin, s_rot, s_mid = (st.sem(f"ro_{x}") for x in ("squared", "mean", "root", "normed", "rotated", "parts"))
    tmp = st.carve(4096, 4, 512)
    rs = st.carve(6144, 4, 512)
    y = st.y2
    groups = [(y[:, 2 * j:2 * j + 2, :], "hg_norm_g_2") for j in range(4)]
    groups += [(st.aq[:, 2 * j:2 * j + 2, :], "q_norm_g_2") for j in range(4)]
    groups += [(st.ak[:, j:j + 1, :], "k_norm_g_2") for j in range(2)]
    flat = lambda v, x: v.rearrange("p (a b) -> p a b", a=x.shape[1])
    with nc.Block() as block:
        @block.scalar
        def _(act):
            for n, (x, _) in enumerate(groups):
                if n >= 4:
                    act.wait_ge(s_fin, n - 3)
                nc.scalar.activation(flat(tmp[:, n % 4, :], x), x, ACT.Square).then_inc(s_sq, 1)
                act.wait_ge(s_ms, n + 1)
                nc.scalar.activation(rs[:, n % 4, :], st.psum[n % 4][:], ACT.Sqrt, scale=1.0 / P, bias=st.eps[:, 0:1]
                                     ).then_inc(s_rt, 1)
            nc.scalar.activation(st.g2, st.g2, ACT.Silu).then_inc(s_rt, 1)

        @block.tensor
        def _(pe):
            for n, (x, _) in enumerate(groups):
                pe.wait_ge(s_sq, n + 1)
                nc.tensor.matmul(st.psum[n % 4][:], st.c("ones"), tmp[:, n % 4, :], start=True, stop=True).then_inc(s_ms, 1)
            for n in range(5):
                pe.wait_ge(s_fin, 4 + n + 1 if n < 4 else 10)
                x = st.aq[:, 2 * n:2 * n + 2, :] if n < 4 else st.ak[:, :, L:TA]
                if n >= 4:
                    pe.wait_ge(s_mid, 1)
                nc.tensor.matmul(st.psum[4 + n % 4][:], st.c("rope_rot"), x, start=True, stop=True).then_inc(s_rot, 1)

        @block.vector
        def _(dve):
            vl = st.vl
            vl.eng = dve
            for n, (x, g) in enumerate(groups):
                dve.wait_ge(s_rt, n + 1)
                r = rs[:, n % 4, :]
                vl(nc.vector.reciprocal(r, r))
                nc.vector.scalar_tensor_tensor(x, x, st.par[:, col(g):col(g) + 1], flat(r, x), ALU.mult, ALU.mult
                                               ).then_inc(s_fin, 1)
            dve.wait_ge(s_rt, len(groups) + 1)
            dve.wait_ge(s_fin, len(groups))
            vl(nc.vector.tensor_tensor(y[:, 0:8, :], y[:, 0:8, :], st.g2, ALU.mult))
            rope = st.c("rope").rearrange("p (f t) -> p f t", f=2)
            cos, sin = (rope[:, f:f + 1, :].broadcast_to([P, 2, T]) for f in range(2))
            for n in range(5):
                x = st.aq[:, 2 * n:2 * n + 2, :] if n < 4 else st.ak[:, :, L:TA]
                t_ = flat(tmp[:, n % 4, :], x)
                dve.wait_ge(s_rot, n + 1)
                ins = nc.vector.tensor_tensor(t_, st.psum[4 + n % 4][:].rearrange("p (a b) -> p a b", a=2), sin, ALU.mult)
                ins.then_inc(s_mid, 1)
                vl(nc.vector.tensor_tensor(x, x, cos, ALU.mult))
                dve.wait_ge(s_mid, n + 1)
                vl(nc.vector.tensor_tensor(x, x, t_, ALU.add))


def attention(nc, st):
    s_sc, s_m, s_e, s_pr, s_pT, s_pTo, s_o, s_oo, s_scf = (st.sem(f"at_{x}") for x in (
        "scores", "max", "exp", "probs", "probsT", "probsT_out", "out_acc", "out_evac", "scores_read"))
    sc = st.carve(4096, 2, 512)
    pT = st.carve(5120, 2, TT, T)
    small = st.carve(7168, 2, 8)
    scale = P ** -0.5
    rounds = [(h, t) for h in range(NH2) for t in range(2)]
    with nc.Block() as block:
        @block.tensor
        def _(pe):
            def scores(n):
                h, t = rounds[n]
                if n >= 2:
                    pe.wait_ge(s_scf, n - 1)
                nc.tensor.matmul(st.psum[n % 2][:], st.aq[:, h, t * P:(t + 1) * P], st.ak[:, h // (NH2 // NKV), :],
                                 start=True, stop=True).then_inc(s_sc, 1)
            scores(0)
            for n, (h, t) in enumerate(rounds):
                if n + 1 < len(rounds):
                    scores(n + 1)
                pe.wait_ge(s_pr, n + 1)
                if n >= 2:
                    pe.wait_ge(s_pTo, n - 1)
                for k in range(TT):
                    last = nc.tensor.transpose(st.psum[2 + n % 2][:, k * P:(k + 1) * P], sc[:, n % 2, k * P:(k + 1) * P], st.c("ident"))
                last.then_inc(s_pT, 1)
                if t == 1:
                    pe.wait_ge(s_pTo, n + 1)
                    if h >= 2:
                        pe.wait_ge(s_oo, h - 1)
                    for k in range(TT):
                        kv = h // (NH2 // NKV)
                        last = nc.tensor.matmul(st.psum[4 + h % 2][:, 0:T], st.av[:, k, kv * P:(kv + 1) * P], pT[:, h % 2, k, :],
                                                start=k == 0, stop=k == TT - 1)
                    last.then_inc(s_o, 1)

        @block.scalar
        def _(act):
            for n, (h, t) in enumerate(rounds):
                act.wait_ge(s_m, n + 1)
                w = small[:, n % 2, :]
                nc.scalar.activation(sc[:, n % 2, :], sc[:, n % 2, :], ACT.Exp, bias=w[:, 1:2], accum_out=w[:, 2:3]).then_inc(s_e, 1)
                nc.scalar.activation(w[:, 3:4], st.sink[:, h:h + 1], ACT.Exp, bias=w[:, 1:2]).then_inc(s_e, 1)
                act.wait_ge(s_pT, n + 1)
                if t == 0 and h >= 2:
                    act.wait_ge(s_o, h - 1)
                nc.scalar.copy(pT[:, h % 2, :, t * P:(t + 1) * P], st.psum[2 + n % 2][:].rearrange("p (k q) -> p k q", k=TT)
                               ).then_inc(s_pTo, 1)

        @block.vector
        def _(dve):
            vl = st.vl
            vl.eng = dve
            win = st.c("window").rearrange("p (t k) -> p t k", t=2)
            for n, (h, t) in enumerate(rounds):
                w = small[:, n % 2, :]
                dve.wait_ge(s_sc, n + 1)
                if n >= 2:
                    dve.wait_ge(s_pT, n - 1)
                x = st.psum[n % 2]
                vl(nc.vector.tensor_scalar(sc[:, n % 2, 0:L], x[:, 0:L], scale, None, ALU.mult))
                nc.vector.scalar_tensor_tensor(sc[:, n % 2, L:TA], x[:, L:TA], scale, win[:, t, :], ALU.mult, ALU.add
                                               ).then_inc(s_scf, 1)
                dve.wait_ge(s_scf, n + 1)
                vl(nc.vector.tensor_reduce(w[:, 0:1], sc[:, n % 2, :], AX.X, ALU.max))
                vl(nc.vector.tensor_tensor(w[:, 0:1], w[:, 0:1], st.sink[:, h:h + 1], ALU.max))
                nc.vector.tensor_scalar(w[:, 1:2], w[:, 0:1], -1.0, None, ALU.mult).then_inc(s_m, 1)
                dve.wait_ge(s_e, 2 * n + 2)
                vl(nc.vector.tensor_tensor(w[:, 2:3], w[:, 2:3], w[:, 3:4], ALU.add))
                vl(nc.vector.reciprocal(w[:, 2:3], w[:, 2:3]))
                nc.vector.tensor_scalar(sc[:, n % 2, :], sc[:, n % 2, :], w[:, 2:3], None, ALU.mult).then_inc(s_pr, 1)
                if t == 1:
                    dve.wait_ge(s_o, h + 1)
                    nc.vector.tensor_copy(st.y2[:, 8 + h, :], st.psum[4 + h % 2][:, 0:T]).then_inc(s_oo, 1)


def store_output(nc, st, out):
    s_T, s_ev, s_out = st.sem("out_transposed"), st.sem("out_evac"), st.sem("out_stored")
    tok = st.carve(0, 2, DM)
    with nc.Block() as block:
        @block.tensor
        def _(pe):
            for m in range(8):
                t, j = m // 4, m % 4
                if m >= 4:
                    pe.wait_ge(s_ev, m - 3)
                for i in range(4):
                    last = nc.tensor.transpose(st.psum[m % 4][:, i * P:(i + 1) * P], st.xT[:, 4 * j + i, t * P:(t + 1) * P], st.c("ident"))
                last.then_inc(s_T, 1)

        @block.vector
        def _(dve):
            for m in range(8):
                dve.wait_ge(s_T, m + 1)
                nc.vector.tensor_copy(tok[:, m // 4, (m % 4) * 512:(m % 4 + 1) * 512], st.psum[m % 4][:]).then_inc(s_ev, 1)

        @block.sync
        def _(sp):
            for t in range(2):
                sp.wait_ge(s_ev, 4 * (t + 1))
                sp.dma_start(out[t * P:(t + 1) * P, :], tok[:, t, :]).then_inc(s_out, 16)
            sp.wait_ge(s_out, 32)


def program(nc, dram, const_where, out, stop=None, dump=None):
    st = State()
    st.dram = dram
    st.nc = nc
    with ExitStack() as ctx:
        sb = lambda name, shape: ctx.enter_context(nc.sbuf_tensor(name, shape, F32))
        st.stage_sems = []
        st.sem = lambda name: ctx.enter_context(nc.semaphore(name))
        st.const = sb("const", [P, dram["const"].shape[1]])
        st.par = sb("params", [P, N_BATCH * P])
        st.silu_c = sb("silu_c", [P, 64])
        st.mod = [sb(f"mod{i}", [P, 2, 96]) for i in range(2)]
        st.modraw = [sb(f"modraw{i}", [P, 192]) for i in range(2)]
        st.gain = sb("gain", [P, 2, 3, 16])
        st.eps = sb("eps", [P, 2])
        st.sink = sb("sink", [P, NH2])
        st.xT = sb("x_channels", [P, KT, T])
        st.ring = sb("weight_ring", [P, RING * KT * SLOT_COLS])
        st.work = sb("work", [P, WORK])
        st.psum = [ctx.enter_context(nc.psum_tensor(f"bank{i}", [P, 512], F32)) for i in range(8)]
        st.s_load = [st.sem(f"weights_in{i}") for i in range(RING)]
        st.s_slot_used, st.s_mod_used = st.sem("slot_used"), st.sem("mod_slot_used")
        st.s_silu = st.sem("silu_c_ready")
        st.vl, st.al, st.pl, st.gl = Link(st.sem("dve_step")), Link(st.sem("act_step")), Link(st.sem("pe_step")), Link(st.sem("pool_step"))
        st.stream = Stream(st)

        def stage_sem(name):
            st.stage_sems.append(nc.alloc_semaphore(name=name))
            return st.stage_sems[-1]
        st.sem = stage_sem

        def c(name):
            at, shape = const_where[name]
            n = int(np.prod(shape))
            v = st.const[:, at:at + n]
            return v
        st.c = c

        def carve(at, *shape):
            n = int(np.prod(shape))
            v = st.work[:, at:at + n]
            if len(shape) > 1:
                names = "abc"[:len(shape)]
                v = v.rearrange(f"p ({' '.join(names)}) -> p {' '.join(names)}", **{x: y for x, y in zip(names, shape)})
            return v
        st.carve = carve
        st.hT = carve(0, KT, TA)
        st.k, st.v = carve(8192, NP1, TA), carve(12288, NP1, TA)
        st.r = carve(16384, NP1, T)
        st.wd, st.ad, st.gd = carve(18432, 1, TA), carve(18944, 1, TA), carve(19456, 2, T)
        st.conv_u, st.ft, st.ycf = carve(19968, 4, T), carve(20992, 2, 512), carve(22016, 8, T)
        st.yr = carve(6144, 8, T)
        st.h, st.G, st.gate_tmp = carve(0, KT, T), carve(4096, NFF, T), carve(15360, 2, T)
        st.q2, st.g2, st.aq, st.ak = carve(8192, NH2, T), carve(22528, NH2, T), carve(24576, NH2, T), carve(26624, NKV, TA)
        st.f2 = [carve(10240, NH2, TA), carve(14336, NH2, TA)]
        st.i2, st.av, st.y2 = carve(18432, TT, NH2 * P), carve(27648, TT, NKV * P), carve(0, KT, T)
        st.ftz = st.work[:, 0:2048].rearrange("p (j f t) -> p j f t", j=4, f=2)
        st.sq, st.rstd = carve(8192, KT, 256), carve(12288, 2, 256)

        def finish(src):
            s_out = st.sem("out_stored")
            with nc.Block() as block:
                @block.sync
                def _(sp):
                    sp.dma_start(out, src).then_inc(s_out, 16)
                    sp.wait_ge(s_out, 16)

        stages = [
            ("eps", lambda: set_eps(nc, st)),
            ("load", lambda: load_inputs(nc, st)),
            ("mod", lambda: first_modulation(nc, st)),
            ("norm1", lambda: normalise(nc, st, "norm1", (
                (st.hT[:, :, 0:L], st.hT[:, :, 0:L], st.gain[:, 0, 1, :], st.mod[0][:, 1, 0:16]),
                (st.xT[:], st.hT[:, :, L:TA], st.gain[:, 0, 0, :], st.mod[0][:, 0, 0:16])))),
            ("in1", lambda: in_projection1(nc, st, 0)),
            ("fourier", lambda: fourier(nc, st)),
            ("rwkv", lambda: rwkv(nc, st)),
            ("rwkv_out", lambda: rwkv_out(nc, st)),
            ("out1", lambda: out_projection(nc, st, "out1", 0, lambda k: st.yr[:, k, :] if k < 8 else st.ycf[:, k - 8, :], OUT1_MOD)),
            ("norm2", lambda: normalise(nc, st, "norm2", ((st.xT[:], st.h, st.gain[:, 0, 2, :], st.mod[0][:, 0, 48:64]),))),
            ("ffn1", lambda: ffn_up(nc, st, "ffn1", FFN1_MOD)),
            ("down1", lambda: ffn_down(nc, st, "down1", 0)),
            ("norm_final", lambda: normalise(nc, st, "norm3", (
                (st.xT[:], st.xT[:], st.par[:, col("norm_final"):col("norm_final") + 16], None),))),
            ("ctx2", lambda: load_context2(nc, st)),
            ("norm4", lambda: normalise(nc, st, "norm4", (
                (st.hT[:, :, 0:L], st.hT[:, :, 0:L], st.gain[:, 1, 1, :], st.mod[1][:, 1, 0:16]),
                (st.xT[:], st.hT[:, :, L:TA], st.gain[:, 1, 0, :], st.mod[1][:, 0, 0:16])))),
            ("in2", lambda: in_projection2(nc, st)),
            ("hgrn", lambda: hgrn(nc, st)),
            ("readout", lambda: readout_and_rope(nc, st)),
            ("attention", lambda: attention(nc, st)),
            ("out2", lambda: out_projection(nc, st, "out2", 1, lambda k: st.y2[:, k, :], None)),
            ("norm5", lambda: normalise(nc, st, "norm5", ((st.xT[:], st.h, st.gain[:, 1, 2, :], st.mod[1][:, 0, 48:64]),))),
            ("ffn2", lambda: ffn_up(nc, st, "ffn2", None)),
            ("down2", lambda: ffn_down(nc, st, "down2", 1)),
            ("store", lambda: store_output(nc, st, out)),
        ]
        for name, run in stages:
            run()
            if name in ("in1", "rwkv", "down1", "hgrn"):
                nc.clear_and_free_semaphores(st.stage_sems)
                st.stage_sems = []
                nc.all_engine_barrier()
            if name == stop:
                finish(dump(st))
                return


def set_eps(nc, st):
    s = st.sem("eps_set")
    with nc.Block() as block:
        @block.vector
        def _(dve):
            nc.vector.memset(st.eps[:, 0:1], RMS_EPS).then_inc(s, 1)
            nc.vector.memset(st.eps[:, 1:2], GN_EPS).then_inc(s, 1)


WORK = 29184


INPUTS = ("x", "c", "ctx", "c_ctx", "w_mod", "b_mod", "norm_mix", "w_in", "rw_shift", "dec_w0", "dec_up", "iclr_a0",
          "iclr_up", "k_k", "k_a", "r_k", "ln_w", "ln_b", "g_up", "conv_w", "w_out", "norm_ffn", "w_gate", "w_up",
          "w_down", "norm_final", "c_2", "ctx_2", "c_ctx_2", "w_mod_2", "b_mod_2", "norm_mix_g_2", "norm_ffn_g_2",
          "w_in_2", "hg_lb_2", "hg_norm_g_2", "q_norm_g_2", "k_norm_g_2", "attn_sink_2", "w_out_2", "w_gate_up_2",
          "w_down_2")
FLAT = ("c", "c_ctx", "b_mod", "norm_mix", "norm_ffn", "norm_final", "k_k", "k_a", "dec_w0", "iclr_a0", "c_2",
        "c_ctx_2", "b_mod_2", "norm_mix_g_2", "norm_ffn_g_2", "conv_w", "r_k", "hg_norm_g_2", "q_norm_g_2",
        "k_norm_g_2", "hg_lb_2", "attn_sink_2", "ln_w", "ln_b")
DEBUG = None


def kernel(**inputs):
    import concourse.bacc as bacc
    from concourse.bass_utils import run_bass_kernel_spmd

    nc = bacc.Bacc("TRN2", target_bir_lowering=False, num_devices=1)
    arrays, dram = {}, {}
    const, where = constants()
    for name in INPUTS:
        a = np.ascontiguousarray(inputs[name])
        if name in FLAT:
            a = a.reshape(-1)
        elif a.shape[0] == 1:
            a = a[0]
        arrays["in_" + name] = a
    arrays["in_const"] = const
    for key, a in arrays.items():
        dram[key[3:]] = nc.dram_tensor(key, a.shape, mybir.dt.from_np(a.dtype), kind="ExternalInput").ap()
    if DEBUG:
        out = nc.dram_tensor("out", (1, T, DM), F32, kind="ExternalOutput").ap()
        program(nc, dram, where, out[0, :, :].rearrange("(p a) b -> p (a b)", p=P), *DEBUG)
    else:
        out = nc.dram_tensor("out", (1, T, DM), F32, kind="ExternalOutput").ap()
        program(nc, dram, where, out[0, :, :])
    got = run_bass_kernel_spmd(nc, [arrays], core_ids=[0])
    return got.results[0]["out"]
```

```python
import math

import numpy as np
import concourse.bass as bass
from concourse import mybir
from contextlib import ExitStack

F32 = mybir.dt.float32
ALU = mybir.AluOpType
ACT = mybir.ActivationFunctionType
AX = mybir.AxisListType

P = 128
DM = 2048
KT = DM // P
T = 256
L = 256
TA = T + L
TT = TA // P
CH = 32
NCH = TA // CH
CPT = P // CH
RMS_EPS = 1e-6
GN_EPS = 64e-5
KK_EPS = 1e-12
HD = 64
D_RW = DM // 2
NP1 = D_RW // P
LORA = 96
D_CV = DM // 4
NCV = D_CV // P
D_IN = 3 * D_RW + 2 * LORA + 256 + 4 * D_CV
D_FF = 5632
NFF = D_FF // P
GRID_W = 64
DECAY = math.exp(-0.5)
NH2 = 8
NKV = 2
WINDOW = 128
IN2 = 5 * NH2 * P + (NH2 + 2 * NKV) * P
NEG = -1e30

RING = 3
SLOT_COLS = 256
DOWN_K = NFF // 4
WORK = 29184


def constants():
    s = np.arange(P)[:, None]
    t = np.arange(P)[None, :]
    out = {}
    out["ident"] = (s == t)
    out["ones"] = np.ones((P, P))
    out["head_ones"] = (s // HD == t // HD)
    out["ident64"] = np.concatenate([np.eye(HD), np.eye(HD)], 0)
    same = s // CH == t // CH
    out["strict"] = np.stack([same & (s < t), same & (s > t)], 1)
    out["incl"] = np.stack([same & (s <= t), same & (s >= t)], 1)
    incl, strict = out.pop("incl"), out.pop("strict")
    out["mask3"] = np.stack([incl, strict, incl], 2)
    out["strict_ts"] = strict[:, ::-1]
    pair = [(s // (2 * b) == t // (2 * b)) & (s // b != t // b) for b in (1, 2, 4, 8, 16)]
    out["level1"] = np.stack([pair[0] & (s < t), pair[0] & (s > t)], 1)
    out["levels"] = np.stack(pair, 1)
    out["carry"] = np.broadcast_to((np.arange(TA) % CH != 0)[None, :], (P, TA))
    seq = np.arange(T)
    ang = 2 * np.pi * ((seq[:, None] * seq[None, :]) % T) / T
    norm = 1.0 / math.sqrt(T * HD)
    out["seq_dft"] = np.stack([np.cos(ang).reshape(2, P, T), np.sin(ang).reshape(2, P, T)], 1).transpose(2, 0, 1, 3)
    hh = 2 * np.pi * (((s % HD) * (t % HD)) % HD) / HD
    blk = (s // HD == t // HD)
    out["head_dft"] = np.stack([blk * np.cos(hh) * norm, -1.0 * blk * np.sin(hh) * norm], 1)
    half, nf = HD, HD // 2
    inv = 10000.0 ** (-np.arange(nf, dtype=np.float32) / nf)
    d = np.arange(P)
    pos = np.where((d < half)[:, None], (seq // GRID_W)[None, :], (seq % GRID_W)[None, :])
    a = (pos.astype(np.float32) * inv.astype(np.float32)[d % nf][:, None]).astype(np.float32).astype(np.float64)
    out["rope"] = np.stack([np.cos(a), np.sin(a)], 1)
    rot = np.zeros((P, P))
    for i in range(P):
        if i % half < nf:
            rot[i + nf, i] = -1.0
        else:
            rot[i - nf, i] = 1.0
    out["rope_rot"] = rot
    q = np.arange(T).reshape(2, P).T[:, :, None]
    k = np.arange(T)[None, None, :]
    out["window"] = np.where(np.abs(q - k) <= WINDOW, 0.0, NEG)
    parts, at, where = [], 0, {}
    for name, v in out.items():
        v = np.ascontiguousarray(v, dtype=np.float32)
        where[name] = (at, v.shape[1:])
        parts.append(v.reshape(P, -1))
        at += parts[-1].shape[1]
    return np.concatenate(parts, 1), where


def row_params():
    b = {}
    at = 0
    for name, n in (("c", 16), ("c_ctx", 16), ("c_2", 16), ("c_ctx_2", 16), ("norm_mix", 16), ("norm_ffn", 16),
                    ("norm_final", 16), ("k_k", 8), ("k_a", 8)):
        b[name] = (0, at, n)
        at += n
    at = 0
    for name, n in (("b_mod", 96), ("dec_w0", 16), ("iclr_a0", 16)):
        b[name] = (1, at, n)
        at += n
    at = 0
    for name, n in (("b_mod_2", 96), ("norm_mix_g_2", 16), ("norm_ffn_g_2", 16)):
        b[name] = (2, at, n)
        at += n
    at = 0
    for name, n in (("rw_shift", 84), ("conv_w", 12), ("r_k", 8), ("hg_norm_g_2", 1), ("q_norm_g_2", 1),
                    ("k_norm_g_2", 1)):
        b[name] = (3, at, n)
        at += n
    b["hg_lb_2"] = (4, 0, 32)
    return b


ROWS = row_params()
N_BATCH = 5
BATCH_ROWS = (128, 128, 128, 107, 32)
RW_TILES = 28


def col(name, i=0):
    batch, at, _ = ROWS[name]
    return batch * P + at + i


class State:
    pass


class Link:

    def __init__(self, sem):
        self.sem, self.n, self.eng = sem, 0, None

    def __call__(self, ins):
        self.n += 1
        ins.then_inc(self.sem, 1)
        self.eng.wait_ge(self.sem, self.n)

    def mark(self, ins):
        self.n += 1
        ins.then_inc(self.sem, 1)

    def wait(self):
        self.eng.wait_ge(self.sem, self.n)


class Stream:

    def __init__(self, st):
        self.st = st
        self.issued = 0

    def load_count(self, n, i=0, per=0):
        return 16 * (n // RING + 1) + i * (16 * (per // RING))


def ring_view(st, n, k, cols):
    base = (n % RING) * KT * SLOT_COLS
    return st.ring[:, base:base + k * cols].rearrange("p (k c) -> p k c", k=k)


def arrived(eng, st, n, i=0, per=0):
    eng.wait_ge(st.s_load[n % RING], st.stream.load_count(n, i, per))


MOD_SLOTS = 6 * DM // SLOT_COLS
MOD_FIRST = 2 * DM // SLOT_COLS
IN1_STEPS, OUT_STEPS, FFN_UNITS, IN2_STEPS = 22, DM // SLOT_COLS, D_FF // SLOT_COLS, IN2 // SLOT_COLS
IN1_MOD = [[] for _ in range(IN1_STEPS)]
_at = MOD_FIRST
for _s in range(IN1_STEPS):
    for _ in range(2 if _s in (5, 9) else 1):
        IN1_MOD[_s].append(_at)
        _at += 1
OUT1_MOD = [_at + s for s in range(OUT_STEPS)]
assert OUT1_MOD[-1] == MOD_SLOTS - 1
FFN1_MOD, IN2_MOD = 0, FFN_UNITS
assert IN2_MOD + IN2_STEPS == MOD_SLOTS


def weight_slots():
    out = []
    spans = {}

    def span(name, items):
        spans[name] = (len(out), len(items))
        out.extend(items)

    def cols(name, c):
        return (name, 0, KT, c * 256, 256)

    def down(name, c):
        return [(name, k * DOWN_K, DOWN_K, c * 256, 256) for k in range(4)]

    span("mod1", [cols("w_mod", c) for c in range(MOD_FIRST)])
    items = [cols("w_in", c) for c in range(12)] + [("w_in", 0, KT, 3072, 192), ("w_in", 0, KT, 3264, 256)]
    items += [("w_in", 0, KT, 3520 + c * 256, 256) for c in range(8)]
    span("in1", [w for s, x in enumerate(items) for w in [x] + [cols("w_mod", c) for c in IN1_MOD[s]]])
    span("out1", [w for s in range(OUT_STEPS) for w in (cols("w_out", s), cols("w_mod", OUT1_MOD[s]))])
    span("ffn1", [w for u in range(FFN_UNITS) for w in (cols("w_gate", u), cols("w_up", u), cols("w_mod_2", FFN1_MOD + u))])
    span("down1", [w for u in range(8) for w in down("w_down", u)])
    span("in2", [w for c in range(IN2_STEPS) for w in (cols("w_in_2", c), cols("w_mod_2", IN2_MOD + c))])
    span("out2", [cols("w_out_2", c) for c in range(8)])
    span("ffn2", [("w_gate_up_2", 0, KT, u * D_FF + c * 256, 256) for c in range(22) for u in range(2)])
    span("down2", [w for u in range(8) for w in down("w_down_2", u)])
    return out, spans


SLOTS, SPANS = weight_slots()
BY_DVE = [name.startswith("w_mod") and n >= MOD_FIRST for n, (name, *_) in enumerate(SLOTS)]


def use_count(n):
    return sum(x == BY_DVE[n] for x in BY_DVE[:n + 1])


def stream_weights(sp, st, upto):
    while st.stream.issued < upto:
        n = st.stream.issued
        period, reps = best_run(n, upto)
        if reps >= 2:
            with sp.Fori(0, reps) as i:
                for t in range(period):
                    issue(sp, st, n + t, i, period)
            st.stream.issued += reps * period
        else:
            issue(sp, st, n, 0, 0)
            st.stream.issued += 1


def best_run(n, upto):
    best = (1, 1)
    if n < RING:
        return best
    for period in (RING, 2 * RING, 4 * RING):
        reps = 1
        while True:
            lo = n + reps * period
            if lo + period > upto:
                break
            a, b = SLOTS[n:n + period], SLOTS[lo:lo + period]
            step = SLOTS[n + period][3] - SLOTS[n][3]
            if any(x[:3] != y[:3] or x[4] != y[4] or y[3] - x[3] != reps * step for x, y in zip(a, b)):
                break
            if BY_DVE[n - RING:n - RING + period] != BY_DVE[lo - RING:lo - RING + period]:
                break
            reps += 1
        if reps >= 2 and reps * period > best[0] * best[1]:
            best = (period, reps)
    return best


def issue(sp, st, n, i, per):
    name, k0, k, c0, cols = SLOTS[n]
    w = st.dram[name]
    step = SLOTS[n + per][3] - c0 if per else 0
    columns = bass.ds(i * step + c0, cols) if per else slice(c0, c0 + cols)
    if n >= RING:
        old = n - RING
        per_turn = use_count(old + per) - use_count(old) if per else 0
        sp.wait_ge(st.s_mod_used if BY_DVE[old] else st.s_slot_used, i * per_turn + use_count(old))
    sp.dma_start(ring_view(st, n, k, cols),
                 w[k0 * P:(k0 + k) * P, columns].rearrange("(t p) n -> p t n", p=P)).then_inc(st.s_load[n % RING], 16)


def load_inputs(nc, st):
    d = st.dram
    rows = st.work[:, 4096 * 2:4096 * 2 + N_BATCH * P].rearrange("p (b c) -> p b c", b=N_BATCH)
    xtok = st.work[:, 8192 + 1024:8192 + 1024 + 4096].rearrange("p (t c) -> p t c", t=2)
    ctok = st.work[:, 8192 + 1024 + 4096:8192 + 1024 + 8192].rearrange("p (t c) -> p t c", t=2)
    hT = st.hT
    s_rows, s_x, s_zero, s_const = st.sem("rows_in"), st.sem("x_in"), st.sem("rows_zeroed"), st.sem("const_in")
    s_rowT, s_par, s_xT, s_xev = st.sem("rows_transposed"), st.sem("params_ready"), st.sem("x_transposed"), st.sem("x_evac")
    n_rows = 0

    with nc.Block() as block:
        @block.sync
        def _(sp):
            sp.dma_start(st.const[:], d["const"]).then_inc(s_const, 16)
            sp.dma_start(xtok, d["x"].rearrange("(t p) c -> p t c", p=P)).then_inc(s_x, 16)
            sp.dma_start(ctok, d["ctx"].rearrange("(t p) c -> p t c", p=P)).then_inc(s_x, 16)
            stream_weights(sp, st, RING)

        @block.gpsimd
        def _(pool):
            nc.gpsimd.memset(rows, 0.0).then_inc(s_zero, 1)

        @block.scalar
        def _(act):
            nonlocal n_rows
            act.wait_ge(s_zero, 1)

            def put(name, src, at=0, width=P):
                nonlocal n_rows
                batch, r, _ = ROWS[name]
                n_rows += 1
                act.dma_start(rows[r + at:r + at + src.shape[0], batch, 0:width], src).then_inc(s_rows, 16)

            for name in ("c", "c_ctx", "c_2", "c_ctx_2", "norm_mix", "norm_ffn", "norm_final", "k_k", "k_a",
                         "b_mod", "dec_w0", "iclr_a0", "b_mod_2", "norm_mix_g_2", "norm_ffn_g_2", "conv_w",
                         "r_k", "hg_norm_g_2", "q_norm_g_2", "k_norm_g_2", "hg_lb_2"):
                put(name, d[name].rearrange("(a c) -> a c", c=P))
            for tap in range(3):
                w = d["rw_shift"][tap, :]
                put("rw_shift", w[0:3072].rearrange("(a c) -> a c", c=P), tap * RW_TILES)
                put("rw_shift", w[3072:3072 + 192].rearrange("(a c) -> a c", c=LORA), tap * RW_TILES + 24, LORA)
                put("rw_shift", w[3264:3520].rearrange("(a c) -> a c", c=P), tap * RW_TILES + 26)
            act.dma_start(st.sink[:], d["attn_sink_2"].rearrange("(a c) -> a c", a=1).partition_broadcast(P)
                          ).then_inc(s_rows, 16)
            n_rows += 1
            act.wait_ge(s_par, 1)
            nc.scalar.activation(st.silu_c[:], st.par[:, 0:64], ACT.Silu).then_inc(st.s_silu, 1)
            act.wait_ge(st.s_silu, 1)

        @block.tensor
        def _(pe):
            pe.wait_ge(s_const, 16)
            pe.wait_ge(s_rows, 16 * n_rows)
            for b in range(N_BATCH):
                n = BATCH_ROWS[b]
                last = nc.tensor.transpose(st.psum[b // 4][:, (b % 4) * P:(b % 4) * P + n], rows[0:n, b, :],
                                           st.c("ident")[0:n, 0:n])
            last.then_inc(s_rowT, 1)
            pe.wait_ge(s_x, 32)
            for m in range(2 * KT // 2):
                src = (xtok, ctok)[m // (KT // 2)]
                if m >= 4:
                    pe.wait_ge(s_xev, m - 3)
                for j in range(4):
                    k, t = (m % (KT // 2)) * 2 + j // 2, j % 2
                    last = nc.tensor.transpose(st.psum[2 + m % 4][:, j * P:(j + 1) * P], src[:, t, k * P:(k + 1) * P],
                                               st.c("ident"))
                last.then_inc(s_xT, 1)

        @block.vector
        def _(dve):
            st.vl.eng = dve
            dve.wait_ge(s_rowT, 1)
            st.vl.mark(nc.vector.tensor_copy(st.par[:, 0:384], st.psum[0][:, 0:384]))
            st.vl.mark(nc.vector.tensor_copy(st.par[:, 384:384 + 107], st.psum[0][:, 384:384 + 107]))
            nc.vector.tensor_copy(st.par[:, 512:544], st.psum[1][:, 0:32]).then_inc(s_par, 1)
            for m in range(KT):
                dve.wait_ge(s_xT, m + 1)
                k = (m % (KT // 2)) * 2
                dst = st.xT[:, k:k + 2, :] if m < KT // 2 else hT[:, k:k + 2, 0:L]
                nc.vector.tensor_copy(dst, st.psum[2 + m % 4][:].rearrange("p (a b) -> p a b", a=2)).then_inc(s_xev, 1)


def mod_macs(dve, st, n, which, vectors, acc, s_mac, mac, s_col, col_count, i=0, per=0):
    v_ = st.nc.vector
    partial, sums = acc
    arrived(dve, st, n, i, per)
    w = ring_view(st, n, KT, 256)
    before = use_count(n) - 1
    if before:
        dve.wait_ge(st.s_mod_used, i * (use_count(n + per) - use_count(n)) + before)
    step = 0
    for k in range(KT):
        for v in range(vectors):
            c = st.silu_c[:, (2 * which + v) * KT + k:(2 * which + v) * KT + k + 1]
            a = partial[:, 2 * v + k % 2, :]
            if k < 2:
                ins = v_.tensor_scalar(a, w[:, k, :], c, None, ALU.mult)
            else:
                dve.wait_ge(s_mac, mac + (step + 1 - 2 * vectors))
                ins = v_.scalar_tensor_tensor(a, w[:, k, :], c, a, ALU.mult, ALU.add)
            ins.then_inc(s_mac, 1)
            step += 1
    dve.wait_ge(s_mac, mac + step)
    if col_count is not None:
        dve.wait_ge(s_col, col_count)
    for v in range(vectors):
        ins = v_.tensor_tensor(sums[:, v, :], partial[:, 2 * v, :], partial[:, 2 * v + 1, :], ALU.add)
        ins.then_inc(s_mac if v + 1 < vectors else st.s_mod_used, 1)


def mac_steps(vectors):
    return KT * vectors + vectors - 1


def mod_sums(nc, st, sums, vectors, at, s_col):
    for half in range(2):
        for v in range(vectors):
            last = nc.tensor.matmul(st.psum[7][:, at + 2 * half + v:at + 2 * half + v + 1],
                                    sums[:, v, half * P:(half + 1) * P], st.c("ones")[:, 0:1], start=True, stop=True)
    last.then_inc(s_col, 1)


class SideMod:

    def __init__(self, nc, st, name, which, slots, area):
        self.nc, self.st, self.which, self.slots = nc, st, which, slots
        self.partial = area[:, 0:512].rearrange("p (a c) -> p a c", a=2)
        self.sums = area[:, 512:1024].rearrange("p (a c) -> p a c", a=2)
        self.s_mac, self.s_col = st.sem(f"{name}_mod_step"), st.sem(f"{name}_mod_columns")
        self.dve_at = self.pe_at = 0

    def accumulate(self, dve, upto):
        while self.dve_at < len(self.slots) and self.slots[self.dve_at][0] < upto:
            j = self.dve_at
            mod_macs(dve, self.st, self.slots[j][0], self.which, 1, (self.partial, self.sums[:, j % 2:j % 2 + 1, :]),
                     self.s_mac, j * mac_steps(1), self.s_col, j - 1 if j >= 2 else None)
            self.dve_at += 1

    def columns(self, pe, upto):
        if self.pe_at < len(self.slots) and self.slots[self.pe_at][0] < upto:
            j = self.pe_at
            pe.wait_ge(self.st.s_mod_used, use_count(self.slots[j][0]))
            mod_sums(self.nc, self.st, self.sums[:, j % 2:j % 2 + 1, :], 1, 4 * j, self.s_col)
            self.pe_at += 1

    def flush(self, pe):
        while self.pe_at < len(self.slots):
            self.columns(pe, len(SLOTS))

    def collect(self, dve):
        st, n = self.st, len(self.slots)
        dve.wait_ge(self.s_col, n)
        t0 = 2 * self.slots[0][1]
        st.vl(st.nc.vector.tensor_copy(
            st.modraw[self.which][:].rearrange("p (t v) -> p t v", v=2)[:, t0:t0 + 2 * n, 0],
            st.psum[7][:, 0:4 * n].rearrange("p (t v) -> p t v", v=2)[:, :, 0]))
        mod_columns(st.nc, st, self.which, slice(t0, t0 + 2 * n), 1)


def mod_columns(nc, st, which, tiles, vectors):
    b = st.par[:, col(("b_mod", "b_mod_2")[which]):]
    for v in range(vectors):
        st.vl.mark(nc.vector.tensor_tensor(
            st.mod[which][:, v, tiles], st.modraw[which][:].rearrange("p (t v) -> p v t", v=2)[:, v, tiles],
            b[:, tiles], ALU.add))
    st.vl.wait()


def gain_columns(nc, st, which, norm, at, v, slot):
    st.vl(nc.vector.scalar_tensor_tensor(st.gain[:, which, slot, :], st.mod[which][:, v, at:at + 16], 1.0,
                                         st.par[:, col(norm):col(norm) + 16], ALU.add, ALU.mult))


def first_modulation(nc, st):
    s_row, s_out, s_T = st.sem("mod_row"), st.sem("mod_row_out"), st.sem("mod_row_transposed")
    first, count = SPANS["mod1"]
    rows = st.carve(16384, count, SLOT_COLS)
    with nc.Block() as block:
        @block.sync
        def _(sp):
            stream_weights(sp, st, first + count + RING)

        @block.tensor
        def _(pe):
            silu = st.silu_c[:].rearrange("p (v k) -> p k v", v=4)
            for s in range(count):
                arrived(pe, st, first + s)
                w = ring_view(st, first + s, KT, SLOT_COLS)
                if s >= 8:
                    pe.wait_ge(s_out, s - 7)
                for k in range(KT):
                    last = nc.tensor.matmul(st.psum[s % 8][0:2, 0:SLOT_COLS], silu[:, k, 0:2],
                                            w[:, k, :], start=k == 0, stop=k == KT - 1)
                last.then_inc(st.s_slot_used, 1)
            pe.wait_ge(s_out, count)
            for s in range(count):
                for half in range(2):
                    t = 2 * s + half
                    last = nc.tensor.transpose(st.psum[0][:, 2 * t:2 * t + 2], rows[0:2, s, half * P:(half + 1) * P],
                                               st.c("ident")[0:2, 0:2])
            last.then_inc(s_T, 1)

        @block.vector
        def _(dve):
            for s in range(count):
                dve.wait_ge(st.s_slot_used, s + 1)
                nc.vector.tensor_copy(rows[0:2, s, :], st.psum[s % 8][0:2, 0:SLOT_COLS]
                                      ).then_inc(s_out, 1)
            st.vl.eng = dve
            dve.wait_ge(s_T, 1)
            st.vl(nc.vector.tensor_copy(st.modraw[0][:, 0:4 * count], st.psum[0][:, 0:4 * count]))
            mod_columns(nc, st, 0, slice(0, 2 * count), 2)
            gain_columns(nc, st, 0, "norm_mix", 16, 0, 0)
            gain_columns(nc, st, 0, "norm_mix", 16, 1, 1)


def normalise(nc, st, name, parts):
    s_sq, s_ms, s_rt, s_xn, s_h = (st.sem(f"{name}_{x}") for x in ("squared", "mean_sq", "root", "scaled", "shifted"))
    with nc.Block() as block:
        @block.scalar
        def _(act):
            for src, dst, gain, shift in parts:
                nc.scalar.activation(st.sq, src, ACT.Square).then_inc(s_sq, 1)
                j = [p[0] is src for p in parts].index(True)
                act.wait_ge(s_ms, j + 1)
                nc.scalar.activation(st.rstd[:, j, :], st.psum[j][:, 0:256], ACT.Sqrt, bias=st.eps[:, 0:1],
                                     scale=1.0 / DM).then_inc(s_rt, 1)
            for j, (src, dst, gain, shift) in enumerate(parts):
                act.wait_ge(s_xn, j + 1)
                for k in range(KT):
                    nc.scalar.activation(dst[:, k, :], dst[:, k, :], ACT.Identity, scale=gain[:, k:k + 1],
                                         bias=shift[:, k:k + 1] if shift is not None else 0.0).then_inc(s_h, 1)

        @block.tensor
        def _(pe):
            for j in range(len(parts)):
                pe.wait_ge(s_sq, j + 1)
                for k in range(KT):
                    last = nc.tensor.matmul(st.psum[j][:, 0:256], st.c("ones"), st.sq[:, k, :], start=k == 0,
                                            stop=k == KT - 1)
                last.then_inc(s_ms, 1)

        @block.vector
        def _(dve):
            st.vl.eng = dve
            for j, (src, dst, gain, shift) in enumerate(parts):
                dve.wait_ge(s_rt, j + 1)
                st.vl(nc.vector.reciprocal(st.rstd[:, j, :], st.rstd[:, j, :]))
                nc.vector.tensor_tensor(dst, src, st.rstd[:, j:j + 1, :].broadcast_to([P, KT, 256]),
                                        ALU.mult).then_inc(s_xn, 1)


def in_projection1(nc, st, lookahead):
    first, count = SPANS["in1"]
    tiles = []
    for s in range(12):
        for half in range(2):
            g = 2 * s + half
            tiles.append((s, half * P, P, "rkv"[g // 8], g % 8, g))
    tiles += [(12, 0, LORA, "wd", 0, 24), (12, LORA, LORA, "ad", 0, 25), (13, 0, P, "gd", 0, 26), (13, P, P, "gd", 1, 27)]
    for j, kind in enumerate(("cg", "cx", "cb")):
        tiles += [(14 + 2 * j + i // 2, (i % 2) * P, P, kind, i, 0) for i in range(4)]
    tiles += [(20 + s, 0, 256, "ft", (s, t), 0) for s in range(2) for t in range(2)]
    dst = {"r": st.r, "k": st.k, "v": st.v, "wd": st.wd, "ad": st.ad, "gd": st.gd}
    both = ("k", "v", "wd", "ad")
    s_acc, s_mid, s_free = st.sem("in1_acc"), st.sem("in1_centre_tap"), st.sem("in1_bank_free")
    slot_at = [first + s + sum(len(x) for x in IN1_MOD[:s]) for s in range(IN1_STEPS)]
    side = SideMod(nc, st, "in1", 0, [(slot_at[s] + 1 + j, c) for s in range(IN1_STEPS) for j, c in enumerate(IN1_MOD[s])],
                   st.carve(24064, 1024))

    def shapes(kind, i, width):
        segs = 2 if kind in both else 1
        out = dst[kind][0:width, i, :].rearrange("p (s t) -> p s t", s=segs)
        return segs, out

    with nc.Block() as block:
        @block.sync
        def _(sp):
            stream_weights(sp, st, first + count + lookahead)

        @block.tensor
        def _(pe):
            for m, (s, c0, width, kind, i, _) in enumerate(tiles):
                n = slot_at[s]
                arrived(pe, st, n)
                cols = SLOTS[n][4]
                w = ring_view(st, n, KT, cols)
                if m >= 4:
                    pe.wait_ge(s_free, m - 3)
                bank = st.psum[m % 4]
                for k in range(KT):
                    if kind == "ft":
                        t = i[1]
                        last = nc.tensor.matmul(bank[:, 0:256], st.hT[:, k, L + t * P:L + (t + 1) * P], w[:, k, :],
                                                start=k == 0, stop=k == KT - 1)
                    elif kind in both:
                        last = nc.tensor.matmul(bank[0:width, :], w[:, k, c0:c0 + width], st.hT[:, k, :],
                                                start=k == 0, stop=k == KT - 1)
                    else:
                        last = nc.tensor.matmul(bank[0:width, 0:T], w[:, k, c0:c0 + width], st.hT[:, k, L:TA],
                                                start=k == 0, stop=k == KT - 1)
                    if k == 0 and m and tiles[m - 1][0] != s and n - slot_at[s - 1] < RING:
                        last.then_inc(st.s_slot_used, 1)
                last.then_inc(s_acc, 1)
                if m + 1 < len(tiles) and tiles[m + 1][0] != s and slot_at[s + 1] - n == RING:
                    pe.wait_ge(s_acc, m + 1)
                    pe.sem_inc(st.s_slot_used, 1)
                side.columns(pe, n)
            pe.wait_ge(s_acc, len(tiles))
            pe.sem_inc(st.s_slot_used, 1)
            side.flush(pe)

        @block.scalar
        def _(act):
            for m, (s, c0, width, kind, i, row) in enumerate(tiles):
                if kind in dst:
                    act.wait_ge(s_acc, m + 1)
                    segs, out = shapes(kind, i, width)
                    src = st.psum[m % 4][0:width, 0:segs * 256].rearrange("p (s t) -> p s t", s=segs)
                    tap = col("rw_shift", RW_TILES + row)
                    nc.scalar.activation(out, src, ACT.Identity, scale=st.par[0:width, tap:tap + 1]).then_inc(s_mid, 1)

        @block.vector
        def _(dve):
            vl = st.vl
            vl.eng = dve
            mids = 0
            for m, (s, c0, width, kind, i, row) in enumerate(tiles):
                bank = st.psum[m % 4]
                if m == 0 or tiles[m - 1][0] != s:
                    side.accumulate(dve, slot_at[s] + 1 + len(IN1_MOD[s]))
                dve.wait_ge(s_acc, m + 1)
                if kind in dst:
                    mids += 1
                    dve.wait_ge(s_mid, mids)
                    segs, out = shapes(kind, i, width)
                    src = bank[0:width, 0:segs * 256].rearrange("p (s t) -> p s t", s=segs)
                    t0, t2 = col("rw_shift", row), col("rw_shift", 2 * RW_TILES + row)
                    vl(nc.vector.scalar_tensor_tensor(out[:, :, 1:], src[:, :, :-1], st.par[0:width, t0:t0 + 1],
                                                      out[:, :, 1:], ALU.mult, ALU.add))
                    nc.vector.scalar_tensor_tensor(out[:, :, :-1], src[:, :, 1:], st.par[0:width, t2:t2 + 1],
                                                   out[:, :, :-1], ALU.mult, ALU.add).then_inc(s_free, 1)
                elif kind == "cg":
                    nc.vector.tensor_copy(st.conv_u[:, i, :], bank[:, 0:T]).then_inc(s_free, 1)
                elif kind == "cx":
                    dve.wait_ge(s_free, m - 3)
                    nc.vector.tensor_tensor(st.conv_u[:, i, :], bank[:, 0:T], st.conv_u[:, i, :],
                                            ALU.mult).then_inc(s_free, 1)
                    dve.wait_ge(s_free, m + 1)
                    u = st.conv_u[:, i, :].rearrange("p (r t) -> p r t", t=GRID_W)
                    y = st.ycf[:, i, :].rearrange("p (r t) -> p r t", t=GRID_W)
                    tap = [st.par[:, col("conv_w", 4 * j + i):col("conv_w", 4 * j + i) + 1] for j in range(3)]
                    vl(nc.vector.tensor_scalar(y, u, tap[1], None, ALU.mult))
                    vl(nc.vector.scalar_tensor_tensor(y[:, :, 1:], u[:, :, :-1], tap[0], y[:, :, 1:], ALU.mult, ALU.add))
                    vl(nc.vector.scalar_tensor_tensor(y[:, :, :-1], u[:, :, 1:], tap[2], y[:, :, :-1], ALU.mult, ALU.add))
                elif kind == "cb":
                    nc.vector.tensor_tensor(st.ycf[:, i, :], bank[:, 0:T], st.ycf[:, i, :], ALU.mult).then_inc(s_free, 1)
                else:
                    s_, t = i
                    nc.vector.tensor_copy(st.ft[:, t, s_ * 256:(s_ + 1) * 256], bank[:, 0:256]).then_inc(s_free, 1)
            side.collect(dve)
            gain_columns(nc, st, 0, "norm_ffn", 64, 0, 2)


def fourier(nc, st):
    s_a, s_ev, s_b, s_done = (st.sem(f"ft_{x}") for x in ("seq", "seq_evac", "head", "head_evac"))
    with nc.Block() as block:
        @block.tensor
        def _(pe):
            dft = st.c("seq_dft").rearrange("p (k f t) -> p k (f t)", k=2, f=2)
            for j in range(4):
                for k in range(2):
                    last = nc.tensor.matmul(st.psum[j][:], st.ft[:, k, j * P:(j + 1) * P], dft[:, k, :],
                                            start=k == 0, stop=k == 1)
                last.then_inc(s_a, 1)
            hd = st.c("head_dft").rearrange("p (f c) -> p f c", f=2)
            for j in range(4):
                pe.wait_ge(s_ev, j + 1)
                for f in range(2):
                    last = nc.tensor.matmul(st.psum[4 + j][:, 0:T], hd[:, f, :], st.ftz[:, j, f, :], start=f == 0, stop=f == 1)
                last.then_inc(s_b, 1)

        @block.scalar
        def _(act):
            for j in range(4):
                act.wait_ge(s_a, j + 1)
                nc.scalar.copy(st.ftz[:, j, :, :], st.psum[j][:].rearrange("p (f t) -> p f t", f=2)).then_inc(s_ev, 1)

        @block.vector
        def _(dve):
            for j in range(4):
                dve.wait_ge(s_b, j + 1)
                nc.vector.tensor_copy(st.ycf[:, 4 + j, :], st.psum[4 + j][:, 0:T]).then_inc(s_done, 1)


def rwkv(nc, st):
    names = {}

    def S(name):
        if name not in names:
            names[name] = st.sem("rw_" + name)
        return names[name]

    c = st.c
    ring = st.ring
    use = {"ring": 0, "hT": 0, "mid": 0, "tail": 0}
    area = {"ring": (st.ring, 0, 12288), "hT": (st.work, 0, 8192), "mid": (st.work, 19968, 2048), "tail": (st.work, 24064, 5120)}

    def take(where, *shape):
        base, at, size = area[where]
        n = int(np.prod(shape))
        assert use[where] + n <= size, (where, use[where] + n, size)
        v = base[:, at + use[where]:at + use[where] + n]
        use[where] += n
        if len(shape) > 1:
            nm = "abcd"[:len(shape)]
            v = v.rearrange(f"p ({' '.join(nm)}) -> p {' '.join(nm)}", **dict(zip(nm, shape)))
        return v

    Bp, Kp = ([take("ring", TA) for _ in range(2)] for _ in range(2))
    BK = take("ring", 2, CPT, 4, CH)
    AR = [take("ring", NCH, 4, CH) for _ in range(2)]
    A = [take("ring", TA) for _ in range(2)]
    BKt2 = [take("ring", 2, CPT, P) for _ in range(2)]
    UV = take("ring", NCH, HD)
    Q = take("ring", 4, P)
    Pm, PT, Lm, WAX = (take("hT", 4, P) for _ in range(4))
    Loff = [take("hT", 4, P) for _ in range(2)]
    GM = take("hT", 4, 3, P)
    Vt = take("hT", TT, P)
    WXx2 = [take("hT", 2, CPT, 2, CH), take("ring", 2, CPT, 2, CH)]
    XA = take("hT", 4, 2, HD)
    SS, SD = take("hT", 2, HD), take("hT", 2, HD)
    ups = take("hT", 2, 2, P)
    lora_half = take("hT", 32)
    omka, DC = take("hT", NP1), take("hT", 2, NCH)
    bonus = take("hT", 2, 2)
    ytok, bv = take("mid", 2, D_RW), take("tail", 2, D_RW)
    t1, t2, t3, t4, t5, t6 = (take("tail", TA) for _ in range(6))
    st.ytok, st.bv = ytok, bv
    kk = take("hT", TA)
    am = t6
    lat = slice(L, TA)
    HS = [slice(h * HD, (h + 1) * HD) for h in range(2)]

    def tile_of(s, d):
        return s if d == 0 else s ^ 1

    def toks(tile):
        return slice(tile * P, (tile + 1) * P)

    with nc.Block() as block:
        @block.sync
        def _(sp):
            for hp in range(NP1):
                cs = slice(hp * P, (hp + 1) * P)
                if hp:
                    sp.wait_ge(S("lora_mm"), hp)
                for d in range(2):
                    sp.dma_start(ups[0:LORA, 0, d, :], st.dram["dec_up"][d, :, cs]).then_inc(S("ups_in"), 16)
                    sp.dma_start(ups[0:LORA, 1, d, :], st.dram["iclr_up"][d, :, cs]).then_inc(S("ups_in"), 16)
                sp.wait_ge(S("vtok"), hp + 1)
                if hp:
                    sp.wait_ge(S("mmB"), hp * 32)
                for h in range(2):
                    for q in range(CPT):
                        sp.dma_start(UV[64 + 32 * h:96 + 32 * h, :, :].rearrange("p (t c) i -> p t c i", c=CPT)[:, :, q, :],
                                     Vt[32 * q:32 * q + 32, :, HS[h]]).then_inc(S("vstack"), 16)

        @block.tensor
        def _(pe):
            W = lambda name, n: pe.wait_ge(S(name), n) if n > 0 else None
            mm, tr = nc.tensor.matmul, nc.tensor.transpose
            bank = st.psum
            I = c("ident")

            def half_step(g, c_):
                q, s = c_ // 2, g % 4
                is_lat = s >= 2
                for d in range(2):
                    tile = tile_of(s, d)
                    n = (g * CPT + q) * 2 + d + 1
                    cc = q if d == 0 else CPT - 1 - q
                    ba = bank[4 + d]
                    if c_ % 2 == 0:
                        if n > 2:
                            W("S_new", n - 2)
                        if is_lat:
                            mm(ba[:, 0:HD], AR[d][:, tile * CPT + cc, :, :], SS[:, d, :], start=True, stop=True)
                        else:
                            mm(ba[0:64, 0:HD], AR[d][:, tile * CPT + cc, 0:2, :], SS[:, d, :], start=True, stop=True)
                        mm(ba[0:64, 0:HD], WXx2[g % 2][:, d, cc, :, :], c("ident64"), start=False, stop=True,
                           skip_group_check=True).then_inc(S("mmA"), 1)
                    else:
                        W("U_out", n)
                        if is_lat:
                            W("y_inter", (g // 4 * 2 + s - 2) * 8 + q * 2 + d + 1)
                        mm(ba[:, HD:2 * HD], BKt2[g % 2][:, d, cc, :], UV[:, tile * CPT + cc, :], start=True,
                           stop=True).then_inc(S("mmB"), 1)

            def key_norms(hp):
                W("k_squared", hp + 1)
                mm(bank[6][:], c("head_ones"), t1, start=True, stop=True).then_inc(S("k_sumsq"), 1)
                for t in range(TT):
                    last = tr(bank[7][:, toks(t)], st.v[:, hp, toks(t)], I)
                last.then_inc(S("vT"), 1)

            def low_rank(hp, j):
                W("ups_in", 64 * (hp + 1))
                for d in range(2):
                    last = mm(bank[2 * j + d][:], ups[0:LORA, j, d, :], (st.wd, st.ad)[j][0:LORA, 0, :], start=True, stop=True)
                if j:
                    last.then_inc(S("lora_mm"), 1)

            def keys_to_rows(g):
                W("bk_placed", (g + 1) * 8)
                for d in range(2):
                    for q in range(CPT):
                        last = tr(bank[d][:, q * P:(q + 1) * P], BK[:, d, q, :, :], I)
                    last.then_inc(S("bkT"), 1)

            W("lora_act", 2)
            for hp in range(NP1):
                if hp == 0:
                    key_norms(0)
                    low_rank(0, 0)
                    low_rank(0, 1)
                W("prod_ready", hp + 1)
                for t in range(2):
                    last = mm(bank[6][:, 2 * t:2 * t + 2], t5[:, toks(2 + t)], c("head_ones")[:, 0:P:HD], start=True, stop=True)
                last.then_inc(S("bonus_mm"), 1)
                W("operands", hp + 1)
                W("vtok", hp + 1)
                W("bonus_read", hp + 1)
                for s in range(4):
                    g = hp * 4 + s
                    tl = [tile_of(s, d) for d in range(2)]
                    is_lat = s >= 2
                    ch0 = [t * CPT for t in tl]

                    def chain(c):
                        if s:
                            half_step(g - 1, c)

                    if s:
                        keys_to_rows(g)
                    chain(0)
                    for d in range(2):
                        last = tr(bank[2][:, d * P:(d + 1) * P], A[d][:, toks(tl[d])], I)
                    last.then_inc(S("aT"), 1)
                    for d in range(2):
                        for h in range(2):
                            W("gram_out", g * 4 + 2 * d + h - 1)
                            b = bank[6 + h]
                            for j, x in enumerate((Bp, Kp)):
                                lhs = x[d][HS[h], toks(tl[d])]
                                last = mm(b[:, 2 * j * P:(2 * j + 1) * P], lhs, A[d][HS[h], toks(tl[d])], start=True, stop=True)
                                if is_lat:
                                    last = mm(b[:, (2 * j + 1) * P:(2 * j + 2) * P], lhs,
                                              AR[d][HS[h], ch0[d]:ch0[d] + CPT, 2 + h, :], start=True, stop=True)
                            last.then_inc(S("gram"), 1)
                        chain(1 + d)
                    W("aT_out", (g + 1) * 2)
                    for h in range(2):
                        for d in range(2):
                            last = mm(bank[3 - h][:, d * P:(d + 1) * P], A[d][HS[h], toks(tl[d])],
                                      Bp[d][HS[h], toks(tl[d])], start=True, stop=True)
                        last.then_inc(S("lgram"), 1)
                    chain(3)
                    if s == 0:
                        keys_to_rows(g)
                    W("gram_out", (g + 1) * 4)
                    W("bkT_out", (g + 1) * 2)
                    for d in range(2):
                        for h in range(2):
                            q = 2 * d + h
                            last = mm(bank[0][:, q * HD:(q + 1) * HD], GM[:, q, 1, :], Vt[:, tl[d], HS[h]], start=True, stop=True)
                    last.then_inc(S("x0"), 1)
                    chain(4)
                    for lv in range(4):
                        n = 2 * (g * 4 + lv)
                        W("loff", g * 4 + lv + 1)
                        if lv == 0:
                            W("p_first", g + 1)
                            W("lgram_out", (g + 1) * 2)
                            W("x0_out", (g + 1) * 2)
                        for d in range(2):
                            if lv:
                                W("p_new", n - 1 + d)
                            for h in range(2):
                                q = 2 * d + h
                                last = mm(bank[1 - d][:, h * P:(h + 1) * P], Loff[lv % 2][:, q, :], Pm[:, q, :], start=True, stop=True)
                            last.then_inc(S("q_mm"), 1)
                        if lv < 2:
                            chain(5 + 2 * lv)
                        if lv == 0:
                            W("pt_first", g + 1)
                        for d in range(2):
                            if lv:
                                W("pt_new", 2 * (g * 3 + lv) - 1 + d)
                            W("q_out", n + d + 1)
                            for h in range(2):
                                q = 2 * d + h
                                last = mm(bank[(2, 6)[d]][:, h * P:(h + 1) * P], PT[:, q, :], Q[:, q, :], start=True, stop=True)
                            last.then_inc(S("p_mm"), 1)
                            if lv < 3:
                                for h in range(2):
                                    q = 2 * d + h
                                    last = mm(bank[(3, 7)[d]][:, h * P:(h + 1) * P], Q[:, q, :], PT[:, q, :], start=True, stop=True)
                                last.then_inc(S("pt_mm"), 1)
                        if lv == 0:
                            chain(6)
                    W("p_new", (g + 1) * 8)
                    W("x0_out", (g + 1) * 2)
                    for q in range(4):
                        last = mm(bank[0][:, q * P:(q + 1) * P], Pm[:, q, :], XA[:, q, :, :], start=True, stop=True)
                    last.then_inc(S("wax"), 1)
                    W("wax_out", g + 1)
                    for q in range(4):
                        last = tr(bank[1][:, q * P:(q + 1) * P], WAX[:, q, :], I)
                    last.then_inc(S("waxT"), 1)
                    if is_lat:
                        for q in range(4):
                            d, h = q // 2, q % 2
                            last = mm(bank[2][HS[h], d * P:(d + 1) * P], WAX[:, q, HS[h]], GM[:, q, 0, :], start=True, stop=True)
                        last.then_inc(S("r_mm"), 1)
                        for q in range(4):
                            d, h = q // 2, q % 2
                            mm(bank[3][:, q * HD:(q + 1) * HD], GM[:, q, 0, :], WAX[:, q, HS[1 - h]], start=True, stop=False)
                            last = mm(bank[3][:, q * HD:(q + 1) * HD], GM[:, q, 2, :], Vt[:, tl[d], HS[h]], start=False, stop=True)
                        last.then_inc(S("yloc"), 1)
                    W("waxT_out", (g + 1) * 6)
                    if is_lat:
                        W("r_out", (hp * 2 + s - 1) * 4)
                        W("yloc_out", (hp * 2 + s - 1) * 2)
                    W("vstack", (hp + 1) * 128)
                    if s == 3:
                        for c_ in range(8):
                            half_step(g, c_)
                            if hp + 1 < NP1 and c_ == 0:
                                key_norms(hp + 1)
                            elif hp + 1 < NP1 and c_ in (2, 4):
                                low_rank(hp + 1, c_ // 2 - 1)

        @block.scalar
        def _(act):
            W = lambda name, n: act.wait_ge(S(name), n) if n > 0 else None
            a_ = nc.scalar.activation
            bank = st.psum
            a_(st.wd[0:LORA], st.wd[0:LORA], ACT.Tanh).then_inc(S("lora_act"), 1)
            a_(st.gd, st.gd, ACT.Sigmoid).then_inc(S("lora_act"), 1)

            def key_rows_out(g):
                W("mmB", (g - 1) * 8)
                for d in range(2):
                    W("bkT", g * 2 + d + 1)
                    nc.scalar.copy(BKt2[g % 2][:, d, :, :], bank[d][:].rearrange("p (a b) -> p a b", a=CPT)).then_inc(S("bkT_out"), 1)

            def key_squares(hp):
                W("operands", hp)
                kk_col = st.par[:, col("k_k", hp):col("k_k", hp) + 1]
                a_(t1, st.k[:, hp, :], ACT.Square, scale=kk_col).then_inc(S("k_squared"), 1)

            def key_norms(hp):
                W("k_sumsq", hp + 1)
                a_(t2, bank[6][:], ACT.Sqrt).then_inc(S("k_norm"), 1)
                W("vT", hp + 1)
                W("vstack", hp * 128)
                W("bv_done", hp)
                nc.scalar.copy(Vt, bank[7][:].rearrange("p (t c) -> p t c", t=TT)).then_inc(S("vtok"), 1)

            def chain_step(g, q):
                for d in range(2):
                    n = (g * CPT + q) * 2 + d + 1
                    gc = tile_of(g % 4, d) * CPT + (q if d == 0 else CPT - 1 - q)
                    W("mmA", n)
                    nc.scalar.copy(UV[0:64, gc, :], bank[4 + d][0:64, 0:HD]).then_inc(S("U_out"), 1)
                for d in range(2):
                    n = (g * CPT + q) * 2 + d + 1
                    gc = tile_of(g % 4, d) * CPT + (q if d == 0 else CPT - 1 - q)
                    if n > 2:
                        W("S_new", n - 2)
                    a_(SD[:, d, :], SS[:, d, :], ACT.Copy, scale=DC[:, d, gc:gc + 1]).then_inc(S("S_decayed"), 1)

            W("setup", 1)
            for hp in range(NP1):
                if hp == 0:
                    key_squares(0)
                    key_norms(0)
                W("prep_free", hp)
                W("lora_mm", hp + 1)
                W("kk_done", hp + 1)
                for d in range(2):
                    b = [lora_half[:, 16 * j + 8 * d + hp:16 * j + 8 * d + hp + 1] for j in range(2)]
                    if d:
                        W("dir_done", hp + 1)
                    a_(t1, bank[d][:], ACT.Tanh, scale=0.5, bias=b[0]).then_inc(S("decay_tanh"), 1)
                    a_(t6, bank[2 + d][:], ACT.Tanh, scale=0.5, bias=b[1]).then_inc(S("rate_tanh"), 1)
                    W("cums", 2 * hp + d + 1)
                    a_(t3, t3, ACT.Exp).then_inc(S("exps"), 1)
                    ends = t2.rearrange("p (n c) -> p n c", c=CH)[:, :, CH - 1]
                    a_(DC[:, d, :], ends, ACT.Exp).then_inc(S("exps"), 1)
                    a_(t1, t4, ACT.Exp, scale=-1.0).then_inc(S("exps"), 1)
                    W("exps", (2 * hp + d) * 4 + 3)
                    a_(t4, t4, ACT.Exp).then_inc(S("exps"), 1)
                W("bonus_mm", hp + 1)
                if hp:
                    W("bv_done", hp)
                nc.scalar.copy(bonus, bank[6][:, 0:4].rearrange("p (a b) -> p a b", a=2)).then_inc(S("bonus_read"), 1)
                for s in range(4):
                    g = hp * 4 + s
                    tl = [tile_of(s, d) for d in range(2)]
                    is_lat = s >= 2
                    ch0 = [t * CPT for t in tl]

                    def chain(q):
                        if s:
                            chain_step(g - 1, q)

                    if s:
                        key_rows_out(g)
                    chain(0)
                    W("aT", g + 1)
                    for h in range(2):
                        src = bank[2][:, 0:256].rearrange("p (d h j) -> p d h j", d=2, h=2)[:, :, h, :]
                        nc.scalar.copy(XA[:, h::2, h, :], src).then_inc(S("aT_out"), 1)
                    chain(1)
                    if s == 0:
                        key_rows_out(g)
                    W("x0", g + 1)
                    for h in range(2):
                        src = bank[0][:, 0:256].rearrange("p (d h j) -> p d h j", d=2, h=2)[:, :, h, :]
                        nc.scalar.copy(XA[:, h::2, 1 - h, :], src).then_inc(S("x0_out"), 1)
                    chain(2)
                    for lv in range(4):
                        for d in range(2):
                            W("q_mm", 2 * (g * 4 + lv) + d + 1)
                            if lv:
                                W("pt_mm", 2 * (g * 3 + lv) - 1 + d)
                            nc.scalar.copy(Q[:, 2 * d:2 * d + 2, :], bank[1 - d][:, 0:256].rearrange("p (a b) -> p a b", a=2)
                                           ).then_inc(S("q_out"), 1)
                        if lv == 0:
                            chain(3)
                    W("wax", g + 1)
                    nc.scalar.copy(WAX, bank[0][:].rearrange("p (a b) -> p a b", a=4)).then_inc(S("wax_out"), 1)
                    W("waxT", g + 1)
                    for h in range(2):
                        src = bank[1][HS[1 - h], :].rearrange("p (d h c t) -> p d h c t", d=2, h=2, c=CPT)[:, :, h, :, :]
                        nc.scalar.copy(WXx2[g % 2][HS[1 - h], :, :, h, :], src).then_inc(S("waxT_out"), 1)
                    for d in range(2):
                        for h in range(2):
                            q = 2 * d + h
                            nc.scalar.copy(AR[d][HS[h], ch0[d]:ch0[d] + CPT, h, :],
                                           bank[1][HS[h], q * P:(q + 1) * P].rearrange("p (c t) -> p c t", c=CPT)
                                           ).then_inc(S("waxT_out"), 1)
                    if s == 3:
                        if hp + 1 < NP1:
                            key_squares(hp + 1)
                        for q in range(CPT):
                            chain_step(g, q)
                            if q == 0 and hp + 1 < NP1:
                                key_norms(hp + 1)

        @block.gpsimd
        def _(pool):
            W = lambda name, n: pool.wait_ge(S(name), n) if n > 0 else None
            g_ = nc.gpsimd
            for x in [BK] + AR:
                g_.memset(x, 0.0).then_inc(S("zeroed"), 1)
            for x in WXx2:
                g_.memset(x, 0.0).then_inc(S("zeroed"), 1)
            lvl = c("levels").rearrange("p (l t) -> p l t", l=5)
            W("zeroed", 5)
            for hp in range(NP1):
                W("operands", hp + 1)
                for s in range(4):
                    g = hp * 4 + s
                    W("bkT", g * 2)
                    for h in range(2):
                        W("bk_placed", g * 8 + 4 * h) if h else W("loff", g * 4)
                        for d in range(2):
                            for j, x in enumerate((Bp, Kp)):
                                src = x[d][HS[h], toks(tile_of(s, d))].rearrange("p (c t) -> p c t", c=CPT)
                                g_.tensor_copy(BK[HS[h], d, :, 2 * j + h, :], src).then_inc(S("bk_placed"), 1)
                    W("bk_placed", (g + 1) * 8)
                    W("lgram_out", (g + 1) * 2)
                    for lv in range(4):
                        if lv >= 2:
                            W("q_mm", 2 * (g * 4 + lv - 1))
                        g_.tensor_tensor(Loff[lv % 2], Lm, lvl[:, lv + 1:lv + 2, :].broadcast_to([P, 4, P]),
                                         ALU.mult).then_inc(S("loff"), 1)

        @block.vector
        def _(dve):
            W = lambda name, n: dve.wait_ge(S(name), n) if n > 0 else None
            v_ = nc.vector
            vl = st.vl
            vl.eng = dve
            bank = st.psum
            for j, name in enumerate(("dec_w0", "iclr_a0")):
                vl.mark(v_.tensor_scalar(lora_half[:, 16 * j:16 * j + 16], st.par[:, col(name):col(name) + 16], 0.5, None, ALU.mult))
            vl.mark(v_.tensor_scalar(omka, st.par[:, col("k_a"):col("k_a") + 8], -1.0, 1.0, ALU.mult, ALU.add))
            vl.wait()
            v_.memset(SS, 0.0).then_inc(S("setup"), 1)
            W("setup", 1)
            W("zeroed", 5)
            carry = c("carry")
            lvl = c("levels").rearrange("p (l t) -> p l t", l=5)
            I4 = c("ident").unsqueeze(1).broadcast_to([P, 4, P])

            def unit_keys(hp):
                W("k_norm", hp + 1)
                vl(v_.tensor_scalar(t2, t2, KK_EPS, None, ALU.max))
                vl(v_.reciprocal(t2, t2))
                v_.scalar_tensor_tensor(kk, st.k[:, hp, :], st.par[:, col("k_k", hp):col("k_k", hp) + 1], t2, ALU.mult,
                                        ALU.mult).then_inc(S("kk_done"), 1)

            def half_step(g, c_):
                q, s = c_ // 2, g % 4
                for d in range(2):
                    n = (g * CPT + q) * 2 + d + 1
                    cc = q if d == 0 else CPT - 1 - q
                    tile = tile_of(s, d)
                    if c_ % 2 == 0 and s >= 2:
                        W("mmA", n)
                        for h in range(2):
                            at = g // 4 * P + h * HD
                            y = ytok[CH * cc:CH * cc + CH, tile - 2, at:at + HD]
                            ins = v_.tensor_tensor(y, bank[4 + d][64 + CH * h:96 + CH * h, 0:HD], y, ALU.add)
                            ins.then_inc(S("y_inter"), 1) if h else vl.mark(ins)
                    elif c_ % 2:
                        gc = tile * CPT + cc
                        W("mmB", n)
                        W("S_decayed", n)
                        v_.scalar_tensor_tensor(SS[:, d, :], bank[4 + d][:, HD:2 * HD], DC[:, d, gc:gc + 1], SD[:, d, :],
                                                ALU.mult, ALU.add).then_inc(S("S_new"), 1)

            for hp in range(NP1):
                k, r = st.k[:, hp, :], st.r[:, hp, :]
                pc = lambda name: st.par[:, col(name, hp):col(name, hp) + 1]
                if hp == 0:
                    unit_keys(0)
                for d in range(2):
                    n = 2 * hp + d + 1
                    W("decay_tanh", n)
                    vl(v_.tensor_scalar(t1, t1, -DECAY / 2, -DECAY / 2, ALU.mult, ALU.add))
                    vl(v_.tensor_tensor_scan(t2, carry, t1, 0.0, ALU.mult, ALU.add))
                    v2 = lambda x: x.rearrange("p (n c) -> p n c", c=CH)
                    if d == 0:
                        vl(v_.tensor_copy(t4, t2))
                        v_.tensor_tensor(t3, t2, t1, ALU.subtract).then_inc(S("cums"), 1)
                    else:
                        tot = v2(t2)[:, :, CH - 1:CH].broadcast_to([P, NCH, CH])
                        vl(v_.tensor_tensor(v2(t3), tot, v2(t2), ALU.subtract))
                        v_.tensor_tensor(t4, t3, t1, ALU.add).then_inc(S("cums"), 1)
                    W("rate_tanh", n)
                    vl(v_.tensor_scalar(am, t6, 0.5, 0.5, ALU.mult, ALU.add))
                    W("exps", 4 * (n - 1) + 2)
                    vl(v_.tensor_scalar(t2, am, pc("k_a"), omka[:, hp:hp + 1], ALU.mult, ALU.add))
                    vl(v_.tensor_tensor(t2, t2, k, ALU.mult))
                    if d == 0:
                        vl(v_.tensor_copy(t5, t2))
                    else:
                        vl(v_.tensor_tensor(t5, t5, t2, ALU.add))
                    vl(v_.tensor_tensor(am, am, kk, ALU.mult))
                    vl(v_.scalar_tensor_tensor(A[d], kk, -1.0, t3, ALU.mult, ALU.mult))
                    W("exps", 4 * n - 1)
                    vl.mark(v_.tensor_tensor(Bp[d], am, t1, ALU.mult))
                    vl.mark(v_.tensor_tensor(Kp[d], t2, t1, ALU.mult))
                    W("exps", 4 * n)
                    for h in range(2):
                        vl.mark(v_.tensor_tensor(AR[d][HS[h], NCH // 2:, 2 + h, :], r.rearrange("p (n c) -> p n c", c=CH)[HS[h]],
                                                 v2(t4)[HS[h], NCH // 2:, :], ALU.mult))
                    vl.wait()
                    if d == 1:
                        v_.scalar_tensor_tensor(t5[:, lat], t5[:, lat], pc("r_k"), r, ALU.mult, ALU.mult).then_inc(S("prod_ready"), 1)
                        W("prod_ready", hp + 1)
                        v_.memset(SS, 0.0).then_inc(S("operands"), 1)
                        W("operands", hp + 1)
                    else:
                        dve.sem_inc(S("dir_done"), 1)
                W("bonus_read", hp + 1)
                for t in range(2):
                    for h in range(2):
                        at = hp * P + h * HD
                        ins = v_.tensor_scalar(bv[:, t, at:at + HD], Vt[:, 2 + t, HS[h]], bonus[:, t, h:h + 1], None, ALU.mult)
                        ins.then_inc(S("bv_done"), 1) if (t, h) == (1, 1) else vl.mark(ins)
                for s in range(4):
                    g = hp * 4 + s
                    tl = [tile_of(s, d) for d in range(2)]
                    is_lat = s >= 2
                    ch0 = [t * CPT for t in tl]
                    lvl1 = c("level1").rearrange("p (d t) -> p d t", d=2)
                    m3 = c("mask3").rearrange("p (d m t) -> p d m t", d=2, m=3)

                    def chain(c_):
                        if s:
                            half_step(g - 1, c_)

                    chain(0)
                    for d in range(2):
                        for h in range(2):
                            q = 2 * d + h
                            W("gram", g * 4 + q + 1)
                            b = bank[6 + h][:].rearrange("p (m t) -> p m t", m=4)
                            vl.mark(v_.tensor_tensor(Pm[:, q, :], b[:, 0, :], lvl1[:, d, :], ALU.mult))
                            if is_lat:
                                v_.tensor_tensor(GM[:, q, :, :], b[:, 1:4, :], m3[:, d, :, :], ALU.mult).then_inc(S("gram_out"), 1)
                            else:
                                v_.tensor_tensor(GM[:, q, 1, :], b[:, 2, :], m3[:, d, 1, :], ALU.mult).then_inc(S("gram_out"), 1)
                        chain(1 + d)
                    W("gram_out", (g + 1) * 4)
                    v_.tensor_tensor(Pm, Pm, I4, ALU.add).then_inc(S("p_first"), 1)
                    for h in range(2):
                        W("lgram", g * 2 + h + 1)
                        b = bank[3 - h][:, 0:256].rearrange("p (d t) -> p d t", d=2)
                        v_.tensor_tensor(Lm[:, h::2, :], b, c("strict_ts").rearrange(
                            "p (d t) -> p d t", d=2), ALU.mult).then_inc(S("lgram_out"), 1)
                    chain(3)
                    W("lgram_out", (g + 1) * 2)
                    v_.tensor_tensor(PT, Lm, lvl[:, 0:1, :].broadcast_to([P, 4, P]), ALU.mult).then_inc(S("pt_mask"), 1)
                    W("pt_mask", g + 1)
                    v_.tensor_tensor(PT, PT, I4, ALU.add).then_inc(S("pt_first"), 1)
                    chain(4)
                    chain(5)
                    for lv in range(4):
                        W("p_first", g + 1)
                        W("pt_first", g + 1)
                        for d in range(2):
                            own = slice(2 * d, 2 * d + 2)
                            W("p_mm", 2 * (g * 4 + lv) + d + 1)
                            v_.tensor_tensor(Pm[:, own, :], bank[(2, 6)[d]][:, 0:256].rearrange("p (a b) -> p a b", a=2),
                                             Pm[:, own, :], ALU.add).then_inc(S("p_new"), 1)
                            if lv < 3:
                                W("pt_mm", 2 * (g * 3 + lv) + d + 1)
                                v_.tensor_tensor(PT[:, own, :], bank[(3, 7)[d]][:, 0:256].rearrange("p (a b) -> p a b", a=2),
                                                 PT[:, own, :], ALU.add).then_inc(S("pt_new"), 1)
                        if lv == 0:
                            chain(6)
                            chain(7)
                    if is_lat:
                        W("r_mm", hp * 2 + s - 1)
                        for d in range(2):
                            for h in range(2):
                                x = AR[d][HS[h], ch0[d]:ch0[d] + CPT, 2 + h, :]
                                v_.tensor_tensor(x, bank[2][HS[h], d * P:(d + 1) * P].rearrange("p (c t) -> p c t", c=CPT), x,
                                                 ALU.add).then_inc(S("r_out"), 1)
                        W("yloc", hp * 2 + s - 1)
                        for d in range(2):
                            y = ytok[:, tl[d] - 2, hp * P:(hp + 1) * P]
                            src = bank[3][:, d * P:(d + 1) * P]
                            if s == 2:
                                v_.tensor_copy(y, src).then_inc(S("yloc_out"), 1)
                            else:
                                W("y_inter", (hp * 2 + 1) * 8)
                                v_.tensor_tensor(y, src, y, ALU.add).then_inc(S("yloc_out"), 1)
                        W("yloc_out", (hp * 2 + s - 1) * 2)
                    if s == 3:
                        for c_ in range(8):
                            half_step(g, c_)
                            if c_ == 3 and hp + 1 < NP1:
                                unit_keys(hp + 1)
                W("S_new", (hp + 1) * 32)
                v_.tensor_copy(SD, SS).then_inc(S("prep_free"), 1)


def rwkv_out(nc, st):
    gup, ln = st.carve(0, 2, D_RW), st.carve(2048, 2, D_RW)
    sq, stat = st.carve(4096, 2, D_RW), st.carve(8192, 3, 32)
    yr = st.yr
    s_in, s_g, s_st, s_y, s_T, s_ev, s_sq = (st.sem(f"rwo_{x}") for x in (
        "weights_in", "gate", "root", "y_ready", "transposed", "evac", "squared"))
    y, bv = st.ytok, st.bv
    heads = lambda x: x.rearrange("p t (h i) -> p (t h) i", i=HD)
    with nc.Block() as block:
        @block.sync
        def _(sp):
            sp.dma_start(gup, st.dram["g_up"].rearrange("(k p) n -> p k n", p=P)).then_inc(s_in, 16)
            for j, name in enumerate(("ln_w", "ln_b")):
                sp.dma_start(ln[:, j, :], st.dram[name].rearrange("(a c) -> a c", a=1).partition_broadcast(P)).then_inc(s_in, 16)
            first, _ = SPANS["out1"]
            stream_weights(sp, st, first + RING)

        @block.tensor
        def _(pe):
            pe.wait_ge(s_in, 48)
            for t in range(2):
                for n in range(2):
                    for k in range(2):
                        last = nc.tensor.matmul(st.psum[2 * t + n][:], st.gd[:, k, t * P:(t + 1) * P],
                                                gup[:, k, n * 512:(n + 1) * 512], start=k == 0, stop=k == 1)
                    last.then_inc(s_g, 1)
            pe.wait_ge(s_y, 4)
            for j in range(4):
                for i in range(2):
                    for t in range(2):
                        last = nc.tensor.transpose(st.psum[4 + j][:, (2 * i + t) * P:(2 * i + t + 1) * P],
                                                   y[:, t, (2 * j + i) * P:(2 * j + i + 1) * P], st.c("ident"))
                last.then_inc(s_T, 1)

        @block.scalar
        def _(act):
            act.wait_ge(s_st, 1)
            nc.scalar.activation(sq, y, ACT.Square).then_inc(s_sq, 1)
            act.wait_ge(s_st, 2)
            nc.scalar.activation(stat[:, 1, :], stat[:, 1, :], ACT.Sqrt, scale=1.0 / HD, bias=st.eps[:, 1:2]).then_inc(s_sq, 1)

        @block.vector
        def _(dve):
            vl = st.vl
            vl.eng = dve
            yh = heads(y)
            one = lambda j: stat[:, j, :].unsqueeze(2).broadcast_to([P, 32, HD])
            vl(nc.vector.tensor_reduce(stat[:, 0, :], yh, AX.X, ALU.add))
            vl(nc.vector.tensor_scalar(stat[:, 0, :], stat[:, 0, :], 1.0 / HD, None, ALU.mult))
            nc.vector.tensor_tensor(yh, yh, one(0), ALU.subtract).then_inc(s_st, 1)
            dve.wait_ge(s_sq, 1)
            nc.vector.tensor_reduce(stat[:, 1, :], heads(sq), AX.X, ALU.add).then_inc(s_st, 1)
            dve.wait_ge(s_sq, 2)
            vl(nc.vector.reciprocal(stat[:, 1, :], stat[:, 1, :]))
            vl(nc.vector.tensor_tensor(yh, yh, one(1), ALU.mult))
            dve.wait_ge(s_in, 48)
            vl(nc.vector.tensor_tensor(y, y, ln[:, 0:1, :].broadcast_to([P, 2, D_RW]), ALU.mult))
            vl(nc.vector.tensor_tensor(y, y, ln[:, 1:2, :].broadcast_to([P, 2, D_RW]), ALU.add))
            vl(nc.vector.tensor_tensor(y, y, bv, ALU.add))
            for t in range(2):
                for n in range(2):
                    dve.wait_ge(s_g, 2 * t + n + 1)
                    part = y[:, t, n * 512:(n + 1) * 512]
                    nc.vector.tensor_tensor(part, st.psum[2 * t + n][:], part, ALU.mult).then_inc(s_y, 1)
            for j in range(4):
                dve.wait_ge(s_T, j + 1)
                nc.vector.tensor_copy(yr[:, 2 * j:2 * j + 2, :], st.psum[4 + j][:].rearrange("p (a b) -> p a b", a=2)
                                      ).then_inc(s_ev, 1)


def units(eng, count, slots, body):
    per = RING // math.gcd(RING, slots)
    turns = count // per
    done = 0
    if turns > 1:
        with eng.Fori(0, turns) as i:
            for u in range(per):
                body(u, i, per)
        done = turns * per
    for u in range(done, count):
        body(u, 0, 0)


class Residual:

    def __init__(self, nc, st, name, gate):
        self.nc, self.st, self.gate = nc, st, gate
        self.s_even, self.s_free = st.sem(f"{name}_even_tile"), st.sem(f"{name}_bank_free")

    def credit(self, dve):
        dve.sem_inc(self.s_free, 2)

    def bank_free(self, pe, u, half, i=0, per=0):
        pe.wait_ge(self.s_free, i * (2 * per) + 2 * u + half + 1)

    def add(self, dve, u, half, slot, i=0, per=0, slots=1):
        nc, st = self.nc, self.st
        if half == 0:
            dve.wait_ge(self.s_even, i * per + u + 1)
        else:
            dve.wait_ge(st.s_slot_used, i * (per * slots) + use_count(slot))
        m = i * (2 * per) + (2 * u + half)
        x = st.xT[:, bass.ds(m, 1), :] if per else st.xT[:, m:m + 1, :]
        g = self.gate[:, bass.ds(m, 1)] if per else self.gate[:, m:m + 1]
        nc.vector.scalar_tensor_tensor(x, st.psum[half][:, 0:T].unsqueeze(1), g, x, ALU.mult, ALU.add).then_inc(self.s_free, 1)


def out_projection(nc, st, name, which, rhs, mods):
    first, count = SPANS[name]
    res = Residual(nc, st, name, st.mod[which][:, 0, 32:48])
    at = [first + s * (2 if mods else 1) for s in range(8)]
    side = SideMod(nc, st, name, which, [(at[s] + 1, c) for s, c in enumerate(mods)], st.carve(24064, 1024)) if mods else None
    with nc.Block() as block:
        @block.sync
        def _(sp):
            stream_weights(sp, st, first + count + RING)

        @block.tensor
        def _(pe):
            for s in range(8):
                arrived(pe, st, at[s])
                w = ring_view(st, at[s], KT, 256)
                for half in range(2):
                    res.bank_free(pe, s, half)
                    for k in range(KT):
                        last = nc.tensor.matmul(st.psum[half][:, 0:T], w[:, k, half * P:(half + 1) * P], rhs(k),
                                                start=k == 0, stop=k == KT - 1)
                    last.then_inc(st.s_slot_used if half else res.s_even, 1)
                    if mods and half == 0:
                        side.columns(pe, at[s])
            if mods:
                side.flush(pe)

        @block.vector
        def _(dve):
            res.credit(dve)
            for s in range(8):
                if mods:
                    side.accumulate(dve, at[s] + 2)
                for half in range(2):
                    res.add(dve, s, half, at[s])
            if mods:
                st.vl.eng = dve
                side.collect(dve)


def ffn_up(nc, st, name, mod_at):
    first, count = SPANS[name]
    slots = 2 + (mod_at is not None)
    n_units = count // slots
    s_even, s_silu, s_free, s_mac, s_col, s_rawfree = (st.sem(f"{name}_{x}") for x in (
        "even_tile", "silu", "bank_free", "mod_step", "mod_columns", "mod_bank_free"))
    h, G, tmp = st.h, st.G, st.gate_tmp
    partial, sums = st.carve(24064, 4, SLOT_COLS), st.carve(25088, 2, SLOT_COLS)

    def tile_done(eng, u, half, i, per):
        if half == 0:
            eng.wait_ge(s_even, i * per + u + 1)
        else:
            eng.wait_ge(st.s_slot_used, i * (2 * per) + use_count(first) + 2 * u + 1)

    with nc.Block() as block:
        @block.sync
        def _(sp):
            stream_weights(sp, st, first + count + RING)

        @block.tensor
        def _(pe):
            def unit(u, i, per):
                n = first + u * slots
                for half in range(2):
                    pe.wait_ge(s_free, i * (2 * per) + 2 * u + half + 1)
                    for j in range(2):
                        if half == 0:
                            arrived(pe, st, n + j, i, per * slots)
                        w = ring_view(st, n + j, KT, 256)
                        for k in range(KT):
                            last = nc.tensor.matmul(st.psum[half][:, j * T:(j + 1) * T], w[:, k, half * P:(half + 1) * P],
                                                    h[:, k, :], start=k == 0, stop=k == KT - 1)
                        if half:
                            last.then_inc(st.s_slot_used, 1)
                    if half == 0:
                        last.then_inc(s_even, 1)
                if mod_at is not None:
                    pe.wait_ge(s_rawfree, i * per + u + 1)
                    pe.wait_ge(st.s_mod_used, i * per + use_count(first + 2) + u)
                    mod_sums(nc, st, sums, 2, 0, s_col)
            units(pe, n_units, slots, unit)

        @block.scalar
        def _(act):
            def unit(u, i, per):
                for half in range(2):
                    tile_done(act, u, half, i, per)
                    act.wait_ge(s_free, i * (2 * per) + 2 * u + half + 1)
                    nc.scalar.activation(tmp[:, half, :], st.psum[half][:, 0:T], ACT.Silu).then_inc(s_silu, 1)
            units(act, n_units, slots, unit)

        @block.vector
        def _(dve):
            dve.sem_inc(s_free, 2)
            if mod_at is not None:
                dve.sem_inc(s_rawfree, 1)

            def unit(u, i, per):
                if mod_at is not None:
                    mod_macs(dve, st, first + slots * u + 2, 1, 2, (partial, sums), s_mac,
                             i * (per * mac_steps(2)) + u * mac_steps(2), s_col, None, i, per * slots)
                for half in range(2):
                    dve.wait_ge(s_silu, i * (2 * per) + 2 * u + half + 1)
                    m = i * (2 * per) + (2 * u + half)
                    out = G[:, bass.ds(m, 1), :] if per else G[:, m:m + 1, :]
                    nc.vector.tensor_tensor(out, tmp[:, half:half + 1, :], st.psum[half][:, T:2 * T].unsqueeze(1),
                                            ALU.mult).then_inc(s_free, 1)
                if mod_at is not None:
                    dve.wait_ge(s_col, i * per + u + 1)
                    at = i * (4 * per) + 4 * (mod_at + u)
                    dst = st.modraw[1][:, bass.ds(at, 4)] if per else st.modraw[1][:, at:at + 4]
                    nc.vector.tensor_copy(dst, st.psum[7][:, 0:4]).then_inc(s_rawfree, 1)
            units(dve, n_units, slots, unit)
            if mod_at is not None:
                st.vl.eng = dve
                dve.wait_ge(s_rawfree, n_units + 1)
                mod_columns(nc, st, 1, slice(0, 32), 2)
                mod_columns(nc, st, 1, slice(32, 2 * (mod_at + n_units)), 1)
                gain_columns(nc, st, 1, "norm_mix_g_2", 16, 0, 0)
                gain_columns(nc, st, 1, "norm_mix_g_2", 16, 1, 1)


def ffn_down(nc, st, name, which):
    first, count = SPANS[name]
    slots = 4
    n_units = count // slots
    res = Residual(nc, st, name, st.mod[which][:, 0, 80:96])
    with nc.Block() as block:
        @block.sync
        def _(sp):
            stream_weights(sp, st, min(first + count + RING, len(SLOTS)))

        @block.tensor
        def _(pe):
            def unit(u, i, per):
                n = first + u * slots
                for s in range(4):
                    arrived(pe, st, n + s, i, per * slots)
                    w = ring_view(st, n + s, DOWN_K, 256)
                    for half in range(2):
                        if s == 0:
                            res.bank_free(pe, u, half, i, per)
                        for k in range(DOWN_K):
                            last = nc.tensor.matmul(st.psum[half][:, 0:T], w[:, k, half * P:(half + 1) * P],
                                                    st.G[:, s * DOWN_K + k, :], start=s == 0 and k == 0,
                                                    stop=s == 3 and k == DOWN_K - 1)
                        if s == 3 and half == 0:
                            last.then_inc(res.s_even, 1)
                    last.then_inc(st.s_slot_used, 1)
            units(pe, n_units, slots, unit)

        @block.vector
        def _(dve):
            res.credit(dve)

            def unit(u, i, per):
                for half in range(2):
                    res.add(dve, u, half, first + u * slots + 3, i, per, slots)
            units(dve, n_units, slots, unit)


def load_context2(nc, st):
    tok = st.carve(8192, 2, DM)
    s_in, s_T, s_ev = st.sem("ctx2_in"), st.sem("ctx2_transposed"), st.sem("ctx2_evac")
    with nc.Block() as block:
        @block.scalar
        def _(act):
            act.dma_start(tok, st.dram["ctx_2"].rearrange("(t p) c -> p t c", p=P)).then_inc(s_in, 16)

        @block.tensor
        def _(pe):
            pe.wait_ge(s_in, 16)
            for m in range(KT // 2):
                if m >= 4:
                    pe.wait_ge(s_ev, m - 3)
                for j in range(4):
                    k, t = 2 * m + j // 2, j % 2
                    last = nc.tensor.transpose(st.psum[m % 4][:, j * P:(j + 1) * P], tok[:, t, k * P:(k + 1) * P], st.c("ident"))
                last.then_inc(s_T, 1)

        @block.vector
        def _(dve):
            for m in range(KT // 2):
                dve.wait_ge(s_T, m + 1)
                nc.vector.tensor_copy(st.hT[:, 2 * m:2 * m + 2, 0:L], st.psum[m % 4][:].rearrange("p (a b) -> p a b", a=2)
                                      ).then_inc(s_ev, 1)


def in_projection2(nc, st):
    first, count = SPANS["in2"]
    dst = (("q", st.q2, 0), ("f", st.f2[0], 1), ("f", st.f2[1], 1), ("i", st.i2, 2), ("g", st.g2, 0), ("aq", st.aq, 0))
    s_acc, s_free = st.sem("in2_acc"), st.sem("in2_bank_free")
    side = SideMod(nc, st, "in2", 1, [(first + 2 * s + 1, IN2_MOD + s) for s in range(IN2_STEPS)], st.c("seq_dft"))
    jobs = []
    for s in range(26):
        if s < 24:
            _, x, kind = dst[s // 4]
            j = 2 * (s % 4)
        else:
            x, kind, j = (st.ak, 1, 0) if s == 24 else (st.av, 2, 0)
        if kind == 2:
            jobs += [(s, "tok", t, x[:, t, j * P:j * P + 256]) for t in range(TT)]
        else:
            jobs += [(s, ("lat", "both")[kind], h, x[:, j + h, :]) for h in range(2)]
    with nc.Block() as block:
        @block.sync
        def _(sp):
            stream_weights(sp, st, first + count)

        @block.tensor
        def _(pe):
            for m, (s, kind, j, _) in enumerate(jobs):
                n = first + 2 * s
                arrived(pe, st, n)
                w = ring_view(st, n, KT, 256)
                if m >= 4:
                    pe.wait_ge(s_free, m - 3)
                bank = st.psum[m % 4]
                for k in range(KT):
                    if kind == "tok":
                        last = nc.tensor.matmul(bank[:, 0:256], st.hT[:, k, j * P:(j + 1) * P], w[:, k, :],
                                                start=k == 0, stop=k == KT - 1)
                    elif kind == "both":
                        last = nc.tensor.matmul(bank[:], w[:, k, j * P:(j + 1) * P], st.hT[:, k, :], start=k == 0, stop=k == KT - 1)
                    else:
                        last = nc.tensor.matmul(bank[:, 0:T], w[:, k, j * P:(j + 1) * P], st.hT[:, k, L:TA],
                                                start=k == 0, stop=k == KT - 1)
                    if k == 0 and m and jobs[m - 1][0] != s:
                        last.then_inc(st.s_slot_used, 1)
                last.then_inc(s_acc, 1)
                side.columns(pe, n)
            pe.wait_ge(s_acc, len(jobs))
            pe.sem_inc(st.s_slot_used, 1)
            side.flush(pe)

        @block.vector
        def _(dve):
            for m, (s, kind, j, x) in enumerate(jobs):
                if m == 0 or jobs[m - 1][0] != s:
                    side.accumulate(dve, first + 2 * s + 2)
                dve.wait_ge(s_acc, m + 1)
                n = 512 if kind == "both" else 256
                nc.vector.tensor_copy(x, st.psum[m % 4][:, 0:n]).then_inc(s_free, 1)
            st.vl.eng = dve
            side.collect(dve)
            gain_columns(nc, st, 1, "norm_ffn_g_2", 64, 0, 2)


def hgrn(nc, st):
    names = {}

    def S(name):
        if name not in names:
            names[name] = st.sem("hg_" + name)
        return names[name]

    def take(base, at, *shape):
        n = int(np.prod(shape))
        v = base[:, at:at + n]
        if len(shape) == 2:
            v = v.rearrange("p (a b) -> p a b", a=shape[0])
        elif len(shape) == 3:
            v = v.rearrange("p (a b c) -> p a b c", a=shape[0], b=shape[1])
        return v

    logf = take(st.ring, 0, 2 * NH2, TA)
    eb4, enb4 = take(st.ring, 8192, 4, T), take(st.ring, 9216, 4, T)
    kk2, scT2 = take(st.ring, 10240, 2, TA), take(st.ring, 11264, 2, 2, P)
    cum, b, te = (take(st.work, 4096 + j * TA, TA) for j in range(3))
    keT = take(st.work, 5632, TT, P)
    states = take(st.work, 6144, 6, P)
    D4 = take(st.work, 6912, 4, NCH)
    lbs = st.carve(28672, 4, 16)
    y = st.y2
    latt = slice(L, TA)
    v2 = lambda x: x.rearrange("p (n c) -> p n c", c=CH)
    base = col("hg_lb_2")
    U = 2 * NH2
    STEPS = NCH - 1

    def chunk(d, n):
        if d == 0:
            return n
        return 7 - n if n < 8 else 23 - n

    with nc.Block() as block:
        @block.scalar
        def _(act):
            W = lambda name, n: act.wait_ge(S(name), n) if n > 0 else None
            a_ = nc.scalar.activation

            def exponentials(u):
                W("sums", u + 1)
                W("inter", 8 * (u - 3))
                W("scores", u - 3)
                W("state", STEPS * (u - 3))
                a_(eb4[:, u % 4, :], b[:, latt], ACT.Exp).then_inc(S("exps"), 1)
                a_(enb4[:, u % 4, :], b[:, latt], ACT.Exp, scale=-1.0).then_inc(S("exps"), 1)
                a_(D4[:, u % 4, :], v2(cum)[:, :, CH - 1], ACT.Exp).then_inc(S("exps"), 1)
                a_(te, te, ACT.Exp).then_inc(S("exps"), 1)

            def keys_out(u):
                W("keT", u + 1)
                W("kv", u)
                nc.scalar.copy(keT, st.psum[4][:].rearrange("p (a b) -> p a b", a=TT)).then_inc(S("keT_out"), 1)

            W("lb_centred", 1)
            a_(lbs[:, 0:2, :], lbs[:, 0:2, :], ACT.Exp).then_inc(S("lb_exp"), 1)
            a_(st.q2, st.q2, ACT.Silu).then_inc(S("q_silu"), 1)
            for u in range(U):
                f = st.f2[u % 2][:, u // 2, :]
                a_(f, f, ACT.Sigmoid).then_inc(S("sigmoid"), 1)
            for u in range(U):
                W("f_ready", u + 1)
                a_(logf[:, u, :], st.f2[u % 2][:, u // 2, :], ACT.Ln).then_inc(S("logf"), 1)
            exponentials(0)
            exponentials(1)
            keys_out(0)
            for w in range(-1, U):
                if w >= 0 and w % 2:
                    h = w // 2
                    W("o_done", h + 1)
                    nc.scalar.copy(y[:, h, :], st.psum[6 + h % 2][:, 0:T]).then_inc(S("o_out"), 1)
                if w + 3 < U:
                    exponentials(w + 3)
                if w + 2 < U:
                    keys_out(w + 2)

        @block.tensor
        def _(pe):
            W = lambda name, n: pe.wait_ge(S(name), n) if n > 0 else None
            mm = nc.tensor.matmul

            def keys_and_scores(u):
                W("kend", u + 1)
                W("keT_out", u)
                for t in range(TT):
                    last = nc.tensor.transpose(st.psum[4][:, t * P:(t + 1) * P], kk2[:, u % 2, t * P:(t + 1) * P], st.c("ident"))
                last.then_inc(S("keT"), 1)
                W("qk", 2 * (u + 1))
                W("scores_out", u)
                for t in range(2):
                    ts = slice(t * P, (t + 1) * P)
                    last = mm(st.psum[5][:, ts], enb4[:, u % 4, ts], eb4[:, u % 4, ts], start=True, stop=True)
                last.then_inc(S("scores"), 1)

            keys_and_scores(0)
            for u in range(U):
                h, d = u // 2, u % 2
                W("keT_out", u + 1)
                W("state", STEPS * u)
                for q in range(CPT):
                    rows = slice(CH * q, CH * q + CH)
                    for t in range(TT):
                        last = mm(st.psum[q][:, t * P:(t + 1) * P], keT[rows, t, :], st.i2[rows, t, h * P:(h + 1) * P],
                                  start=True, stop=True)
                last.then_inc(S("kv"), 1)
                if u + 1 < U:
                    keys_and_scores(u + 1)
                W("scores_out", u + 1)
                if d == 0:
                    W("o_out", h - 1)
                o = st.psum[6 + h % 2]
                for t in range(2):
                    mm(o[:, t * P:(t + 1) * P], st.i2[:, 2 + t, h * P:(h + 1) * P], scT2[:, u % 2, t, :],
                       start=d == 0 and t == 0, stop=False, skip_group_check=True)
                for n in range(8, 16):
                    W("state", STEPS * u + n)
                    cl = chunk(d, n) - 8
                    last = mm(o[:, cl * CH:(cl + 1) * CH], states[:, 2 + n % 4, :], eb4[:, u % 4, cl * CH:(cl + 1) * CH],
                              start=False, stop=d == 1 and n == 15, skip_group_check=True)
                    last.then_inc(S("inter"), 1)
                if d:
                    W("inter", 8 * (u + 1))
                    pe.sem_inc(S("o_done"), 1)

        @block.gpsimd
        def _(pool):
            W = lambda name, n: pool.wait_ge(S(name), n) if n > 0 else None
            g_ = nc.gpsimd
            W("q_silu", 1)
            for u in range(U):
                f = st.f2[u % 2][:, u // 2, :]
                W("logf", u + 1)
                g_.tensor_scalar(f, f, -1.0, 1.0, ALU.mult, ALU.add).then_inc(S("k_ready"), 1)
                W("k_ready", u + 1)
                W("exps", 4 * u + 2)
                g_.tensor_tensor(enb4[:, u % 4, :], enb4[:, u % 4, :], f[:, latt], ALU.mult).then_inc(S("qk"), 1)
                g_.tensor_tensor(eb4[:, u % 4, :], eb4[:, u % 4, :], st.q2[:, u // 2, :], ALU.mult).then_inc(S("qk"), 1)

        @block.vector
        def _(dve):
            W = lambda name, n: dve.wait_ge(S(name), n) if n > 0 else None
            v_ = nc.vector
            vl = st.vl
            vl.eng = dve
            b0, b1 = st.par[:, base:base + 16], st.par[:, base + 16:base + 32]
            vl(v_.tensor_tensor(lbs[:, 2, :], b0, b1, ALU.max))
            vl.mark(v_.tensor_tensor(lbs[:, 0, :], b0, lbs[:, 2, :], ALU.subtract))
            v_.tensor_tensor(lbs[:, 1, :], b1, lbs[:, 2, :], ALU.subtract).then_inc(S("lb_centred"), 1)
            W("lb_exp", 1)
            vl(v_.tensor_tensor(lbs[:, 3, :], lbs[:, 0, :], lbs[:, 1, :], ALU.add))
            vl(v_.reciprocal(lbs[:, 3, :], lbs[:, 3, :]))
            vl(v_.tensor_tensor(lbs[:, 2, :], lbs[:, 0, :], lbs[:, 3, :], ALU.mult))
            vl(v_.tensor_scalar(lbs[:, 3, :], lbs[:, 2, :], -1.0, 1.0, ALU.mult, ALU.add))
            for u in range(U):
                f, lc = st.f2[u % 2][:, u // 2, :], 8 * (u % 2) + u // 2
                W("sigmoid", u + 1)
                v_.tensor_scalar(f, f, lbs[:, 3, lc:lc + 1], lbs[:, 2, lc:lc + 1], ALU.mult, ALU.add).then_inc(S("f_ready"), 1)
            incl = st.c("mask3").rearrange("p (d m t) -> p d m t", d=2, m=3)[:, :, 0, :]

            def sums(u):
                W("logf", u + 1)
                W("kend", u)
                W("exps", 4 * u)
                vl(v_.tensor_tensor_scan(cum, st.c("carry"), logf[:, u, :], 0.0, ALU.mult, ALU.add))
                tot = v2(cum)[:, :, CH - 1:CH].broadcast_to([P, NCH, CH])
                if u % 2 == 0:
                    vl.mark(v_.tensor_copy(b[:, latt], cum[:, latt]))
                    v_.tensor_tensor(v2(te), tot, v2(cum), ALU.subtract).then_inc(S("sums"), 1)
                else:
                    vl.mark(v_.tensor_tensor(te, cum, logf[:, u, :], ALU.subtract))
                    vl(v_.tensor_tensor(v2(b[:, latt]), tot[:, NCH // 2:, :], v2(cum[:, latt]), ALU.subtract))
                    v_.tensor_tensor(b[:, latt], b[:, latt], logf[:, u, latt], ALU.add).then_inc(S("sums"), 1)

            def end_keys(u):
                W("k_ready", u + 1)
                W("exps", 4 * u + 4)
                W("keT", u - 1)
                v_.tensor_tensor(kk2[:, u % 2, :], st.f2[u % 2][:, u // 2, :], te, ALU.mult).then_inc(S("kend"), 1)

            def scores_out(u):
                W("scores", u + 1)
                W("inter", 8 * (u - 1))
                v_.tensor_tensor(scT2[:, u % 2, :, :], st.psum[5][:, 0:256].rearrange("p (t c) -> p t c", t=2),
                                 incl[:, u % 2:u % 2 + 1, :].broadcast_to([P, 2, P]), ALU.mult).then_inc(S("scores_out"), 1)

            def carry_state(u):
                W("kv", u + 1)
                where = lambda j: states[:, j % 2, :] if j < 8 else states[:, 2 + j % 4, :]
                for n in range(STEPS):
                    g = chunk(u % 2, n)
                    kv = st.psum[g % CPT][:, (g // CPT) * P:(g // CPT + 1) * P]
                    if n == 7:
                        W("inter", 8 * u)
                    elif n >= 11:
                        W("inter", 8 * u + n - 10)
                    if n == 0:
                        v_.tensor_copy(where(1), kv).then_inc(S("state"), 1)
                    else:
                        v_.scalar_tensor_tensor(where(n + 1), where(n), D4[:, u % 4, g:g + 1], kv, ALU.mult, ALU.add
                                                ).then_inc(S("state"), 1)
                    W("state", STEPS * u + n + 1)

            sums(0)
            end_keys(0)
            sums(1)
            for w in range(-1, U):
                if w >= 0:
                    carry_state(w)
                if w + 2 < U:
                    end_keys(w + 2)
                if w + 3 < U:
                    sums(w + 3)
                if w + 1 < U:
                    scores_out(w + 1)


def readout_and_rope(nc, st):
    s_sq, s_ms, s_rt, s_fin, s_rot, s_mid = (st.sem(f"ro_{x}") for x in ("squared", "mean", "root", "normed", "rotated", "parts"))
    tmp = st.carve(4096, 4, 512)
    rs = st.carve(6144, 4, 512)
    y = st.y2
    groups = [(y[:, 2 * j:2 * j + 2, :], "hg_norm_g_2") for j in range(4)]
    groups += [(st.aq[:, 2 * j:2 * j + 2, :], "q_norm_g_2") for j in range(4)]
    groups += [(st.ak[:, j:j + 1, :], "k_norm_g_2") for j in range(2)]
    flat = lambda v, x: v.rearrange("p (a b) -> p a b", a=x.shape[1])
    with nc.Block() as block:
        @block.sync
        def _(sp):
            stream_weights(sp, st, SPANS["out2"][0] + RING)

        @block.scalar
        def _(act):
            for n, (x, _) in enumerate(groups):
                if n >= 4:
                    act.wait_ge(s_fin, n - 3)
                nc.scalar.activation(flat(tmp[:, n % 4, :], x), x, ACT.Square).then_inc(s_sq, 1)
                act.wait_ge(s_ms, n + 1)
                nc.scalar.activation(rs[:, n % 4, :], st.psum[n % 4][:], ACT.Sqrt, scale=1.0 / P, bias=st.eps[:, 0:1]
                                     ).then_inc(s_rt, 1)
            nc.scalar.activation(st.g2, st.g2, ACT.Silu).then_inc(s_rt, 1)

        @block.tensor
        def _(pe):
            for n, (x, _) in enumerate(groups):
                pe.wait_ge(s_sq, n + 1)
                nc.tensor.matmul(st.psum[n % 4][:], st.c("ones"), tmp[:, n % 4, :], start=True, stop=True).then_inc(s_ms, 1)
            for n in range(5):
                pe.wait_ge(s_fin, 4 + n + 1 if n < 4 else 10)
                x = st.aq[:, 2 * n:2 * n + 2, :] if n < 4 else st.ak[:, :, L:TA]
                if n >= 4:
                    pe.wait_ge(s_mid, 1)
                nc.tensor.matmul(st.psum[4 + n % 4][:], st.c("rope_rot"), x, start=True, stop=True).then_inc(s_rot, 1)

        @block.vector
        def _(dve):
            vl = st.vl
            vl.eng = dve
            for n, (x, g) in enumerate(groups):
                dve.wait_ge(s_rt, n + 1)
                r = rs[:, n % 4, :]
                vl(nc.vector.reciprocal(r, r))
                nc.vector.scalar_tensor_tensor(x, x, st.par[:, col(g):col(g) + 1], flat(r, x), ALU.mult, ALU.mult
                                               ).then_inc(s_fin, 1)
            dve.wait_ge(s_rt, len(groups) + 1)
            dve.wait_ge(s_fin, len(groups))
            vl(nc.vector.tensor_tensor(y[:, 0:8, :], y[:, 0:8, :], st.g2, ALU.mult))
            rope = st.c("rope").rearrange("p (f t) -> p f t", f=2)
            cos, sin = (rope[:, f:f + 1, :].broadcast_to([P, 2, T]) for f in range(2))
            for n in range(5):
                x = st.aq[:, 2 * n:2 * n + 2, :] if n < 4 else st.ak[:, :, L:TA]
                t_ = flat(tmp[:, n % 4, :], x)
                dve.wait_ge(s_rot, n + 1)
                ins = nc.vector.tensor_tensor(t_, st.psum[4 + n % 4][:].rearrange("p (a b) -> p a b", a=2), sin, ALU.mult)
                ins.then_inc(s_mid, 1)
                vl(nc.vector.tensor_tensor(x, x, cos, ALU.mult))
                dve.wait_ge(s_mid, n + 1)
                vl(nc.vector.tensor_tensor(x, x, t_, ALU.add))


def attention(nc, st):
    s_sc, s_m, s_e, s_pr, s_pT, s_pTo, s_o, s_oo, s_scf = (st.sem(f"at_{x}") for x in (
        "scores", "max", "exp", "probs", "probsT", "probsT_out", "out_acc", "out_evac", "scores_read"))
    sc = st.carve(4096, 2, 512)
    pT = st.carve(5120, 2, TT, T)
    small = st.carve(7168, 2, 8)
    scale = P ** -0.5
    rounds = [(h, t) for h in range(NH2) for t in range(2)]
    with nc.Block() as block:
        @block.tensor
        def _(pe):
            def scores(n):
                h, t = rounds[n]
                if n >= 2:
                    pe.wait_ge(s_scf, n - 1)
                nc.tensor.matmul(st.psum[n % 2][:], st.aq[:, h, t * P:(t + 1) * P], st.ak[:, h // (NH2 // NKV), :],
                                 start=True, stop=True).then_inc(s_sc, 1)
            scores(0)
            for n, (h, t) in enumerate(rounds):
                if n + 1 < len(rounds):
                    scores(n + 1)
                pe.wait_ge(s_pr, n + 1)
                if n >= 2:
                    pe.wait_ge(s_pTo, n - 1)
                for k in range(TT):
                    last = nc.tensor.transpose(st.psum[2 + n % 2][:, k * P:(k + 1) * P], sc[:, n % 2, k * P:(k + 1) * P], st.c("ident"))
                last.then_inc(s_pT, 1)
                if t == 1:
                    pe.wait_ge(s_pTo, n + 1)
                    if h >= 2:
                        pe.wait_ge(s_oo, h - 1)
                    for k in range(TT):
                        kv = h // (NH2 // NKV)
                        last = nc.tensor.matmul(st.psum[4 + h % 2][:, 0:T], st.av[:, k, kv * P:(kv + 1) * P], pT[:, h % 2, k, :],
                                                start=k == 0, stop=k == TT - 1)
                    last.then_inc(s_o, 1)

        @block.scalar
        def _(act):
            for n, (h, t) in enumerate(rounds):
                act.wait_ge(s_m, n + 1)
                w = small[:, n % 2, :]
                nc.scalar.activation(sc[:, n % 2, :], sc[:, n % 2, :], ACT.Exp, bias=w[:, 1:2], accum_out=w[:, 2:3]).then_inc(s_e, 1)
                nc.scalar.activation(w[:, 3:4], st.sink[:, h:h + 1], ACT.Exp, bias=w[:, 1:2]).then_inc(s_e, 1)
                act.wait_ge(s_pT, n + 1)
                if t == 0 and h >= 2:
                    act.wait_ge(s_o, h - 1)
                nc.scalar.copy(pT[:, h % 2, :, t * P:(t + 1) * P], st.psum[2 + n % 2][:].rearrange("p (k q) -> p k q", k=TT)
                               ).then_inc(s_pTo, 1)

        @block.vector
        def _(dve):
            vl = st.vl
            vl.eng = dve
            win = st.c("window").rearrange("p (t k) -> p t k", t=2)
            for n, (h, t) in enumerate(rounds):
                w = small[:, n % 2, :]
                dve.wait_ge(s_sc, n + 1)
                if n >= 2:
                    dve.wait_ge(s_pT, n - 1)
                x = st.psum[n % 2]
                vl(nc.vector.tensor_scalar(sc[:, n % 2, 0:L], x[:, 0:L], scale, None, ALU.mult))
                nc.vector.scalar_tensor_tensor(sc[:, n % 2, L:TA], x[:, L:TA], scale, win[:, t, :], ALU.mult, ALU.add
                                               ).then_inc(s_scf, 1)
                dve.wait_ge(s_scf, n + 1)
                vl(nc.vector.tensor_reduce(w[:, 0:1], sc[:, n % 2, :], AX.X, ALU.max))
                vl(nc.vector.tensor_tensor(w[:, 0:1], w[:, 0:1], st.sink[:, h:h + 1], ALU.max))
                nc.vector.tensor_scalar(w[:, 1:2], w[:, 0:1], -1.0, None, ALU.mult).then_inc(s_m, 1)
                dve.wait_ge(s_e, 2 * n + 2)
                vl(nc.vector.tensor_tensor(w[:, 2:3], w[:, 2:3], w[:, 3:4], ALU.add))
                vl(nc.vector.reciprocal(w[:, 2:3], w[:, 2:3]))
                nc.vector.tensor_scalar(sc[:, n % 2, :], sc[:, n % 2, :], w[:, 2:3], None, ALU.mult).then_inc(s_pr, 1)
                if t == 1:
                    dve.wait_ge(s_o, h + 1)
                    nc.vector.tensor_copy(st.y2[:, 8 + h, :], st.psum[4 + h % 2][:, 0:T]).then_inc(s_oo, 1)


def store_output(nc, st, out):
    s_T, s_ev, s_out = st.sem("out_transposed"), st.sem("out_evac"), st.sem("out_stored")
    tok = st.carve(0, 2, DM)
    with nc.Block() as block:
        @block.tensor
        def _(pe):
            for m in range(8):
                t, j = m // 4, m % 4
                if m >= 4:
                    pe.wait_ge(s_ev, m - 3)
                for i in range(4):
                    last = nc.tensor.transpose(st.psum[m % 4][:, i * P:(i + 1) * P], st.xT[:, 4 * j + i, t * P:(t + 1) * P], st.c("ident"))
                last.then_inc(s_T, 1)

        @block.vector
        def _(dve):
            for m in range(8):
                dve.wait_ge(s_T, m + 1)
                nc.vector.tensor_copy(tok[:, m // 4, (m % 4) * 512:(m % 4 + 1) * 512], st.psum[m % 4][:]).then_inc(s_ev, 1)

        @block.sync
        def _(sp):
            for t in range(2):
                sp.wait_ge(s_ev, 4 * (t + 1))
                sp.dma_start(out[t * P:(t + 1) * P, :], tok[:, t, :]).then_inc(s_out, 16)
            sp.wait_ge(s_out, 32)


def program(nc, dram, const_where, out):
    st = State()
    st.dram = dram
    st.nc = nc
    with ExitStack() as ctx:
        sb = lambda name, shape: ctx.enter_context(nc.sbuf_tensor(name, shape, F32))
        st.stage_sems = []
        st.sem = lambda name: ctx.enter_context(nc.semaphore(name))
        st.const = sb("const", [P, dram["const"].shape[1]])
        st.par = sb("params", [P, N_BATCH * P])
        st.silu_c = sb("silu_c", [P, 64])
        st.mod = [sb(f"mod{i}", [P, 2, 96]) for i in range(2)]
        st.modraw = [sb(f"modraw{i}", [P, 192]) for i in range(2)]
        st.gain = sb("gain", [P, 2, 3, 16])
        st.eps = sb("eps", [P, 2])
        st.sink = sb("sink", [P, NH2])
        st.xT = sb("x_channels", [P, KT, T])
        st.ring = sb("weight_ring", [P, RING * KT * SLOT_COLS])
        st.work = sb("work", [P, WORK])
        st.psum = [ctx.enter_context(nc.psum_tensor(f"bank{i}", [P, 512], F32)) for i in range(8)]
        st.s_load = [st.sem(f"weights_in{i}") for i in range(RING)]
        st.s_slot_used, st.s_mod_used = st.sem("slot_used"), st.sem("mod_slot_used")
        st.s_silu = st.sem("silu_c_ready")
        st.vl = Link(st.sem("dve_step"))
        st.stream = Stream(st)

        def stage_sem(name):
            st.stage_sems.append(nc.alloc_semaphore(name=name))
            return st.stage_sems[-1]
        st.sem = stage_sem

        def c(name):
            at, shape = const_where[name]
            n = int(np.prod(shape))
            v = st.const[:, at:at + n]
            return v
        st.c = c

        def carve(at, *shape):
            n = int(np.prod(shape))
            v = st.work[:, at:at + n]
            if len(shape) > 1:
                names = "abc"[:len(shape)]
                v = v.rearrange(f"p ({' '.join(names)}) -> p {' '.join(names)}", **{x: y for x, y in zip(names, shape)})
            return v
        st.carve = carve
        st.hT = carve(0, KT, TA)
        st.k, st.v = carve(8192, NP1, TA), carve(12288, NP1, TA)
        st.r = carve(16384, NP1, T)
        st.wd, st.ad, st.gd = carve(18432, 1, TA), carve(18944, 1, TA), carve(19456, 2, T)
        st.conv_u, st.ft, st.ycf = carve(19968, 4, T), carve(20992, 2, 512), carve(22016, 8, T)
        st.yr = carve(6144, 8, T)
        st.h, st.G, st.gate_tmp = carve(0, KT, T), carve(4096, NFF, T), carve(15360, 2, T)
        st.q2, st.g2, st.aq, st.ak = carve(8192, NH2, T), carve(22528, NH2, T), carve(24576, NH2, T), carve(26624, NKV, TA)
        st.f2 = [carve(10240, NH2, TA), carve(14336, NH2, TA)]
        st.i2, st.av, st.y2 = carve(18432, TT, NH2 * P), carve(27648, TT, NKV * P), carve(0, KT, T)
        st.ftz = st.work[:, 0:2048].rearrange("p (j f t) -> p j f t", j=4, f=2)
        st.sq, st.rstd = carve(8192, KT, 256), carve(12288, 2, 256)

        stages = [
            ("eps", lambda: set_eps(nc, st)),
            ("load", lambda: load_inputs(nc, st)),
            ("mod", lambda: first_modulation(nc, st)),
            ("norm1", lambda: normalise(nc, st, "norm1", (
                (st.hT[:, :, 0:L], st.hT[:, :, 0:L], st.gain[:, 0, 1, :], st.mod[0][:, 1, 0:16]),
                (st.xT[:], st.hT[:, :, L:TA], st.gain[:, 0, 0, :], st.mod[0][:, 0, 0:16])))),
            ("in1", lambda: in_projection1(nc, st, 0)),
            ("fourier", lambda: fourier(nc, st)),
            ("rwkv", lambda: rwkv(nc, st)),
            ("rwkv_out", lambda: rwkv_out(nc, st)),
            ("out1", lambda: out_projection(nc, st, "out1", 0, lambda k: st.yr[:, k, :] if k < 8 else st.ycf[:, k - 8, :], OUT1_MOD)),
            ("norm2", lambda: normalise(nc, st, "norm2", ((st.xT[:], st.h, st.gain[:, 0, 2, :], st.mod[0][:, 0, 48:64]),))),
            ("ffn1", lambda: ffn_up(nc, st, "ffn1", FFN1_MOD)),
            ("down1", lambda: ffn_down(nc, st, "down1", 0)),
            ("norm_final", lambda: normalise(nc, st, "norm3", (
                (st.xT[:], st.xT[:], st.par[:, col("norm_final"):col("norm_final") + 16], None),))),
            ("ctx2", lambda: load_context2(nc, st)),
            ("norm4", lambda: normalise(nc, st, "norm4", (
                (st.hT[:, :, 0:L], st.hT[:, :, 0:L], st.gain[:, 1, 1, :], st.mod[1][:, 1, 0:16]),
                (st.xT[:], st.hT[:, :, L:TA], st.gain[:, 1, 0, :], st.mod[1][:, 0, 0:16])))),
            ("in2", lambda: in_projection2(nc, st)),
            ("hgrn", lambda: hgrn(nc, st)),
            ("readout", lambda: readout_and_rope(nc, st)),
            ("attention", lambda: attention(nc, st)),
            ("out2", lambda: out_projection(nc, st, "out2", 1, lambda k: st.y2[:, k, :], None)),
            ("norm5", lambda: normalise(nc, st, "norm5", ((st.xT[:], st.h, st.gain[:, 1, 2, :], st.mod[1][:, 0, 48:64]),))),
            ("ffn2", lambda: ffn_up(nc, st, "ffn2", None)),
            ("down2", lambda: ffn_down(nc, st, "down2", 1)),
            ("store", lambda: store_output(nc, st, out)),
        ]
        for name, run in stages:
            run()
            if name in ("in1", "rwkv", "down1", "hgrn"):
                nc.clear_and_free_semaphores(st.stage_sems)
                st.stage_sems = []
                nc.all_engine_barrier()


def set_eps(nc, st):
    s = st.sem("eps_set")
    with nc.Block() as block:
        @block.vector
        def _(dve):
            nc.vector.memset(st.eps[:, 0:1], RMS_EPS).then_inc(s, 1)
            nc.vector.memset(st.eps[:, 1:2], GN_EPS).then_inc(s, 1)



INPUTS = ("x", "c", "ctx", "c_ctx", "w_mod", "b_mod", "norm_mix", "w_in", "rw_shift", "dec_w0", "dec_up", "iclr_a0",
          "iclr_up", "k_k", "k_a", "r_k", "ln_w", "ln_b", "g_up", "conv_w", "w_out", "norm_ffn", "w_gate", "w_up",
          "w_down", "norm_final", "c_2", "ctx_2", "c_ctx_2", "w_mod_2", "b_mod_2", "norm_mix_g_2", "norm_ffn_g_2",
          "w_in_2", "hg_lb_2", "hg_norm_g_2", "q_norm_g_2", "k_norm_g_2", "attn_sink_2", "w_out_2", "w_gate_up_2",
          "w_down_2")
FLAT = ("c", "c_ctx", "b_mod", "norm_mix", "norm_ffn", "norm_final", "k_k", "k_a", "dec_w0", "iclr_a0", "c_2",
        "c_ctx_2", "b_mod_2", "norm_mix_g_2", "norm_ffn_g_2", "conv_w", "r_k", "hg_norm_g_2", "q_norm_g_2",
        "k_norm_g_2", "hg_lb_2", "attn_sink_2", "ln_w", "ln_b")


def kernel(**inputs):
    import concourse.bacc as bacc
    from concourse.bass_utils import run_bass_kernel_spmd

    nc = bacc.Bacc("TRN2", target_bir_lowering=False, num_devices=1)
    arrays, dram = {}, {}
    const, where = constants()
    for name in INPUTS:
        a = np.ascontiguousarray(inputs[name])
        if name in FLAT:
            a = a.reshape(-1)
        elif a.shape[0] == 1:
            a = a[0]
        arrays["in_" + name] = a
    arrays["in_const"] = const
    for key, a in arrays.items():
        dram[key[3:]] = nc.dram_tensor(key, a.shape, mybir.dt.from_np(a.dtype), kind="ExternalInput").ap()
    out = nc.dram_tensor("out", (1, T, DM), F32, kind="ExternalOutput").ap()
    program(nc, dram, where, out[0, :, :])
    got = run_bass_kernel_spmd(nc, [arrays], core_ids=[0])
    return got.results[0]["out"]
```
